# Optimizing a Trainium2 kernel written in Bass

```python
import jax
import jax.numpy as jnp
from jax import lax
import numpy as np
import math

D_MODEL = 1024
BATCH = 1
SEQ = 256
DEPTH = 1

GRID_W = 64
CTX_LEN = 256
D_MIX = D_MODEL
D_POOL = D_MIX // 2
POOL_WINDOWS = (2, 4, 8, 16)
POOL_GW = D_POOL // len(POOL_WINDOWS)
D_ATTN = D_MIX - D_POOL
NA_HEADS = 8
NA_HEAD_DIM = D_ATTN // NA_HEADS
NA_KH_MAX = 8
NA_KW = 16
D_IN = D_POOL + 3 * D_ATTN
PEER_HEADS = 8
PEER_NKEYS = 128
PEER_N_EXPERTS = PEER_NKEYS * PEER_NKEYS
PEER_TOPK = 16
PEER_DKEY = 256
PEER_TOKEN_BLOCK = 128
N_MOD = 6
EPS = 1e-6


def rmsnorm(x, g):
    xf = x.astype(jnp.float32)
    y = xf * lax.rsqrt(jnp.mean(xf * xf, axis=-1, keepdims=True) + EPS)
    return (y * g.astype(jnp.float32)).astype(x.dtype)

def modulate(h, shift, scale):
    return h * (1 + scale) + shift

def multiscale_pool(p, w_grp, scale):
    B, L, _ = p.shape
    pf = p.astype(jnp.float32)
    cs = jnp.concatenate([jnp.zeros((B, 1, D_POOL), jnp.float32), jnp.cumsum(pf, axis=1)], axis=1)
    t = jnp.arange(L)
    outs = []
    for g, w in enumerate(POOL_WINDOWS):
        sl = slice(g * POOL_GW, (g + 1) * POOL_GW)
        lo = jnp.clip(t - w // 2, 0, L)
        hi = jnp.clip(t + w // 2, 0, L)
        csg = cs[..., sl]
        cnt = (hi - lo).astype(jnp.float32)[None, :, None]
        outs.append((jnp.take(csg, hi, axis=1) - jnp.take(csg, lo, axis=1)) / cnt - pf[..., sl])
    pooled = jnp.stack(outs, axis=2).astype(p.dtype)
    y = jnp.einsum('blgc,gcd->blgd', pooled, w_grp).reshape(B, L, D_POOL)
    return y * scale

def neighbourhood_attention(q, k, v, k_ctx, v_ctx, rpb):
    B, S, H, Dh = q.shape
    rows = S // GRID_W
    kh = min(NA_KH_MAX, rows)
    n_loc = kh * NA_KW
    qg = q.reshape(B, rows, GRID_W, H, Dh)
    kg = k.reshape(B, rows, GRID_W, H, Dh)
    vg = v.reshape(B, rows, GRID_W, H, Dh)
    col = jnp.arange(GRID_W)
    c0 = jnp.clip(col - NA_KW // 2, 0, GRID_W - NA_KW)
    col_idx = c0[:, None] + jnp.arange(NA_KW)[None, :]
    col_off = col_idx - col[:, None] + (NA_KW - 1)
    scale = Dh ** -0.5

    def row_block(r):
        r0 = jnp.clip(r - kh // 2, 0, rows - kh)
        k_rows = lax.dynamic_slice_in_dim(kg, r0, kh, axis=1)
        v_rows = lax.dynamic_slice_in_dim(vg, r0, kh, axis=1)
        k_win = k_rows[:, :, col_idx]
        v_win = v_rows[:, :, col_idx]
        q_r = lax.dynamic_index_in_dim(qg, r, axis=1, keepdims=False)
        row_off = r0 + jnp.arange(kh) - r + (NA_KH_MAX - 1)
        bias = rpb[:, row_off[None, :, None], col_off[:, None, :]].astype(jnp.float32)
        s_loc = jnp.einsum('bwhd,biwjhd->bhwij', q_r, k_win).astype(jnp.float32) * scale + bias
        s_ctx = jnp.einsum('bwhd,bchd->bhwc', q_r, k_ctx).astype(jnp.float32) * scale
        s_all = jnp.concatenate([s_loc.reshape(B, H, GRID_W, n_loc), s_ctx], axis=-1)
        prob = jax.nn.softmax(s_all, axis=-1)
        p_loc = prob[..., :n_loc].reshape(B, H, GRID_W, kh, NA_KW).astype(v.dtype)
        p_ctx = prob[..., n_loc:].astype(v.dtype)
        return (jnp.einsum('bhwij,biwjhd->bwhd', p_loc, v_win)
                + jnp.einsum('bhwc,bchd->bwhd', p_ctx, v_ctx))

    out = lax.map(row_block, jnp.arange(rows))
    return jnp.moveaxis(out, 0, 1).reshape(B, S, H * Dh)

def context_attention(q, k, v):
    B, C, H, Dh = q.shape
    s = jnp.einsum('bqhd,bkhd->bhqk', q, k).astype(jnp.float32) * (Dh ** -0.5)
    prob = jax.nn.softmax(s, axis=-1).astype(v.dtype)
    return jnp.einsum('bhqk,bkhd->bqhd', prob, v).reshape(B, C, H * Dh)

def peer(h, w_q, sub_keys, u, v):
    B, L, D = h.shape
    tok = h.reshape((B * L) // PEER_TOKEN_BLOCK, PEER_TOKEN_BLOCK, D)
    k = PEER_TOPK

    def block(xb):
        tb = xb.shape[0]
        q = (xb @ w_q).reshape(tb, PEER_HEADS, 2, PEER_DKEY // 2)
        s = jnp.einsum('thpd,hpnd->thpn', q, sub_keys).astype(jnp.float32)
        sv, si = lax.top_k(s, k)
        cand = (sv[:, :, 0, :, None] + sv[:, :, 1, None, :]).reshape(tb, PEER_HEADS, k * k)
        cand_idx = (si[:, :, 0, :, None] * PEER_NKEYS + si[:, :, 1, None, :]).reshape(tb, PEER_HEADS, k * k)
        top_v, top_i = lax.top_k(cand, k)
        experts = jnp.take_along_axis(cand_idx, top_i, axis=-1)
        g = jax.nn.softmax(top_v, axis=-1)
        u_e = u[experts]
        v_e = v[experts]
        a = jax.nn.gelu(jnp.einsum('td,thkd->thk', xb, u_e).astype(jnp.float32), approximate=False)
        return jnp.einsum('thk,thkd->td', (g * a).astype(xb.dtype), v_e)

    return lax.map(block, tok).reshape(B, L, D)

def split_heads(t):
    B, L, _ = t.shape
    return t.reshape(B, L, NA_HEADS, NA_HEAD_DIM)

def first_inputs(seed: int = 0) -> dict:
    key = jax.random.key(seed)
    ks = jax.random.split(key, 18)
    f32 = jnp.float32
    D = D_MODEL

    def nrm(k, shape, s):
        return jax.random.normal(k, shape, f32) * s

    return {
        'x': nrm(ks[0], (BATCH, SEQ, D), 1.0),
        'c': nrm(ks[1], (BATCH, D), 1.0),
        'ctx': nrm(ks[2], (BATCH, CTX_LEN, D), 1.0),
        'c_ctx': nrm(ks[3], (D,), 1.0),
        'ada_w': nrm(ks[4], (DEPTH, D, N_MOD * D), 0.5 * D ** -0.5),
        'ada_b': nrm(ks[5], (DEPTH, N_MOD * D), 0.01),
        'norm1_g': 1.0 + nrm(ks[6], (DEPTH, D), 0.05),
        'w_in': nrm(ks[7], (DEPTH, D, D_IN), D ** -0.5),
        'pool_w': nrm(ks[8], (DEPTH, len(POOL_WINDOWS), POOL_GW, POOL_GW), POOL_GW ** -0.5),
        'pool_scale': 1.0 + nrm(ks[9], (DEPTH, D_POOL), 0.1),
        'na_rpb': nrm(ks[10], (DEPTH, NA_HEADS, 2 * NA_KH_MAX - 1, 2 * NA_KW - 1), 0.2),
        'w_out': nrm(ks[11], (DEPTH, D_MIX, D), D_MIX ** -0.5),
        'norm2_g': 1.0 + nrm(ks[12], (DEPTH, D), 0.05),
        'peer_wq': nrm(ks[13], (DEPTH, D, PEER_HEADS * PEER_DKEY), D ** -0.5),
        'peer_keys': nrm(ks[14], (DEPTH, PEER_HEADS, 2, PEER_NKEYS, PEER_DKEY // 2), (PEER_DKEY // 2) ** -0.5),
        'peer_u': nrm(ks[15], (DEPTH, PEER_N_EXPERTS, D), D ** -0.5),
        'peer_v': nrm(ks[16], (DEPTH, PEER_N_EXPERTS, D), 0.5),
        'final_g': 1.0 + nrm(ks[17], (D,), 0.05),
    }

def first_block(x, c, ctx, c_ctx, ada_w, ada_b, norm1_g, w_in, pool_w, pool_scale, na_rpb, w_out,
              norm2_g, peer_wq, peer_keys, peer_u, peer_v, final_g):
    kv_cols = slice(D_POOL + D_ATTN, D_IN)
    for layer in range(DEPTH):
        last = layer == DEPTH - 1
        mod_x = (jax.nn.silu(c) @ ada_w[layer] + ada_b[layer])[:, None, :]
        mod_c = jax.nn.silu(c_ctx) @ ada_w[layer] + ada_b[layer]
        sh1, sc1, g1, sh2, sc2, g2 = jnp.split(mod_x, N_MOD, axis=-1)
        csh1, csc1, cg1, csh2, csc2, cg2 = jnp.split(mod_c, N_MOD, axis=-1)

        hx = modulate(rmsnorm(x, norm1_g[layer]), sh1, sc1)
        hc = modulate(rmsnorm(ctx, norm1_g[layer]), csh1, csc1)
        zx = hx @ w_in[layer]
        px = zx[..., :D_POOL]
        qx = split_heads(zx[..., D_POOL:D_POOL + D_ATTN])
        kx = split_heads(zx[..., D_POOL + D_ATTN:D_POOL + 2 * D_ATTN])
        vx = split_heads(zx[..., D_POOL + 2 * D_ATTN:])
        zc_kv = hc @ w_in[layer][:, kv_cols]
        kc = split_heads(zc_kv[..., :D_ATTN])
        vc = split_heads(zc_kv[..., D_ATTN:])

        pool_x = multiscale_pool(px, pool_w[layer], pool_scale[layer])
        attn_x = neighbourhood_attention(qx, kx, vx, kc, vc, na_rpb[layer])
        x = x + g1 * (jnp.concatenate([pool_x, attn_x], axis=-1) @ w_out[layer])

        if not last:
            zc_pq = hc @ w_in[layer][:, :D_POOL + D_ATTN]
            pool_c = multiscale_pool(zc_pq[..., :D_POOL], pool_w[layer], pool_scale[layer])
            attn_c = context_attention(split_heads(zc_pq[..., D_POOL:]), kc, vc)
            ctx = ctx + cg1 * (jnp.concatenate([pool_c, attn_c], axis=-1) @ w_out[layer])

        h2 = modulate(rmsnorm(x, norm2_g[layer]), sh2, sc2)
        x = x + g2 * peer(h2, peer_wq[layer], peer_keys[layer], peer_u[layer], peer_v[layer])
        if not last:
            h2c = modulate(rmsnorm(ctx, norm2_g[layer]), csh2, csc2)
            ctx = ctx + cg2 * peer(h2c, peer_wq[layer], peer_keys[layer], peer_u[layer], peer_v[layer])

    return rmsnorm(x, final_g)


HG_HEADS = 8
HG_DK = 128
HG_DV = 128
HG_WIDTH = HG_HEADS * HG_DK
HG_VWIDTH = HG_HEADS * HG_DV
HG_CHUNK = 64
NSA_HEADS = 16
NSA_KV = 4
NSA_GROUP = NSA_HEADS // NSA_KV
NSA_DH = 64
NSA_WIDTH = NSA_HEADS * NSA_DH
NSA_KVW = NSA_KV * NSA_DH
CMP_LEN = 32
CMP_STRIDE = 16
CMP_HIDDEN = 256
SEL_BLOCK = 64
SEL_TOPK = 16
WINDOW = 512
Q_BLOCK = 64
ROPE_THETA = 500000.0
ROPE_DIM = NSA_DH // 4
D_FF = 4 * D_MODEL
PLE_DIM = 256
NEG = -1e30

IN_SIZES = [HG_WIDTH, HG_WIDTH, HG_VWIDTH, HG_VWIDTH,
            NSA_WIDTH, 6 * NSA_KVW, 3 * NSA_HEADS,
            D_MODEL, D_MODEL]
N_IN = int(sum(IN_SIZES))
SPLIT_POINTS = [int(v) for v in np.cumsum(IN_SIZES)[:-1]]


def rms_norm(x, w):
    xf = x.astype(jnp.float32)
    y = xf * lax.rsqrt(jnp.mean(xf * xf, axis=-1, keepdims=True) + EPS)
    return y.astype(x.dtype) * w

def masked_softmax(s, mask):
    s = jnp.where(mask, s.astype(jnp.float32), NEG)
    pr = jax.nn.softmax(s, axis=-1)
    return jnp.where(mask, pr, 0.0)

def rope_tables(T):
    half = ROPE_DIM // 2
    inv = jnp.asarray(ROPE_THETA ** (-np.arange(half) * 2.0 / ROPE_DIM), jnp.float32)
    ang = jnp.arange(T, dtype=jnp.float32)[:, None] * inv[None, :]
    return jnp.cos(ang), jnp.sin(ang)

def apply_partial_rope(x, cos, sin):
    half = ROPE_DIM // 2
    extra = x.ndim - 3
    shp = (cos.shape[0],) + (1,) * extra + (half,)
    c = cos.reshape(shp).astype(x.dtype)
    s = sin.reshape(shp).astype(x.dtype)
    x1 = x[..., :half]
    x2 = x[..., half:ROPE_DIM]
    rest = x[..., ROPE_DIM:]
    return jnp.concatenate([x1 * c - x2 * s, x2 * c + x1 * s, rest], axis=-1)

def hgrn2_mixer(q, f_pre, i_in, g, lb, gnorm_w):
    B, T, _ = q.shape
    n = T // HG_CHUNK
    f32 = jnp.float32
    qf = jax.nn.silu(q.astype(f32)) * (HG_DK ** -0.5)
    forget = lb + (1.0 - lb) * jax.nn.sigmoid(f_pre.astype(f32))
    k = 1.0 - forget
    logf = jnp.log(forget)

    def heads(t, d):
        return t.reshape(B, n, HG_CHUNK, HG_HEADS, d).transpose(1, 0, 3, 2, 4)

    qc, kc, lc = heads(qf, HG_DK), heads(k, HG_DK), heads(logf, HG_DK)
    vc = heads(i_in.astype(f32), HG_DV)
    causal = jnp.tril(jnp.ones((HG_CHUNK, HG_CHUNK), dtype=bool))

    def step(S, inp):
        qj, kj, vj, lj = inp
        b = jnp.cumsum(lj, axis=2)
        o_inter = jnp.einsum('bhtk,bhkv->bhtv', qj * jnp.exp(b), S)
        rel = b[:, :, :, None, :] - b[:, :, None, :, :]
        decay = jnp.exp(jnp.where(causal[:, :, None], rel, -jnp.inf))
        A = jnp.einsum('bhtk,bhsk,bhtsk->bhts', qj, kj, decay)
        o = o_inter + jnp.einsum('bhts,bhsv->bhtv', A, vj)
        b_last = b[:, :, -1:, :]
        S = jnp.exp(b_last[:, :, 0, :, None]) * S + jnp.einsum(
            'bhsk,bhsv->bhkv', kj * jnp.exp(b_last - b), vj)
        return S, o

    S0 = jnp.zeros((B, HG_HEADS, HG_DK, HG_DV), f32)
    _, o = lax.scan(step, S0, (qc, kc, vc, lc))
    o = o.transpose(1, 0, 3, 2, 4).reshape(B, T, HG_HEADS, HG_DV)
    gh = g.astype(f32).reshape(B, T, HG_HEADS, HG_DV)
    o = rms_norm(o, gnorm_w.astype(f32)) * jax.nn.silu(gh)
    return o.reshape(B, T, HG_VWIDTH).astype(q.dtype)

def nsa_mixer(q, kc, vc, ks, vs, kw, vw, gates, pe_k, pe_v, wk1, wk2, wv1, wv2):
    B, T, _ = q.shape
    G, R, Dh = NSA_KV, NSA_GROUP, NSA_DH
    scale = Dh ** -0.5
    cos, sin = rope_tables(T)
    q = q.reshape(B, T, G, R, Dh) * scale
    q_rot = apply_partial_rope(q, cos, sin)
    kvh = lambda t: t.reshape(B, T, G, Dh)
    ks = apply_partial_rope(kvh(ks), cos, sin)
    kw = apply_partial_rope(kvh(kw), cos, sin)

    n_cmp = (T - CMP_LEN) // CMP_STRIDE + 1
    blk_idx = np.arange(n_cmp)[:, None] * CMP_STRIDE + np.arange(CMP_LEN)[None, :]
    cmp_end = blk_idx[:, -1]

    def compress(t, pe, w1, w2):
        blocks = kvh(t)[:, blk_idx] + pe[:, None, :]
        flat = blocks.transpose(0, 1, 3, 2, 4).reshape(B, n_cmp, G, CMP_LEN * Dh)
        out = jax.nn.gelu(flat @ w1) @ w2
        return out.transpose(0, 2, 1, 3)

    k_cmp = compress(kc, pe_k, wk1, wk2)
    v_cmp = compress(vc, pe_v, wv1, wv2)

    n_sel = T // SEL_BLOCK
    top = min(SEL_TOPK, n_sel)
    sel_start = np.arange(n_sel) * SEL_BLOCK
    overlap = jnp.asarray(((blk_idx[:, :1] < sel_start[None, :] + SEL_BLOCK)
                           & (cmp_end[:, None] >= sel_start[None, :])).astype(np.float32))
    ks_blocks = ks.transpose(0, 2, 1, 3).reshape(B, G, n_sel, SEL_BLOCK * Dh)
    vs_blocks = kvh(vs).transpose(0, 2, 1, 3).reshape(B, G, n_sel, SEL_BLOCK * Dh)
    sel_ids = jnp.arange(n_sel)

    pad = ((0, 0), (0, 0), (WINDOW, 0), (0, 0))
    kw_pad = jnp.pad(kw.transpose(0, 2, 1, 3), pad)
    vw_pad = jnp.pad(kvh(vw).transpose(0, 2, 1, 3), pad)

    q_all = q.transpose(0, 2, 3, 1, 4)
    qr_all = q_rot.transpose(0, 2, 3, 1, 4)

    def block(c):
        s0 = c * Q_BLOCK
        t_pos = s0 + jnp.arange(Q_BLOCK)
        qb = lax.dynamic_slice_in_dim(q_all, s0, Q_BLOCK, axis=3)
        qr = lax.dynamic_slice_in_dim(qr_all, s0, Q_BLOCK, axis=3)
        s = jnp.einsum('bgrqd,bgnd->bgrqn', qb, k_cmp)
        p_cmp = masked_softmax(s, cmp_end[None, :] <= t_pos[:, None])
        o_cmp = jnp.einsum('bgrqn,bgnd->bgrqd', p_cmp, v_cmp)
        imp = jnp.einsum('bgrqn,ns->bgqs', p_cmp, overlap)
        cur = t_pos // SEL_BLOCK
        forced = ((sel_ids[None, :] == 0) | (sel_ids[None, :] == cur[:, None])
                  | (sel_ids[None, :] == cur[:, None] - 1))
        causal_blk = sel_ids[None, :] * SEL_BLOCK <= t_pos[:, None]
        imp = jnp.where(forced, jnp.inf, imp)
        imp = jnp.where(causal_blk, imp, -jnp.inf)
        _, idx = lax.top_k(imp, top)
        flat_idx = idx.reshape(B, G, Q_BLOCK * top, 1)
        kg = jnp.take_along_axis(ks_blocks, flat_idx, axis=2).reshape(
            B, G, Q_BLOCK, top * SEL_BLOCK, Dh)
        vg = jnp.take_along_axis(vs_blocks, flat_idx, axis=2).reshape(
            B, G, Q_BLOCK, top * SEL_BLOCK, Dh)
        key_pos = (idx[..., None] * SEL_BLOCK + jnp.arange(SEL_BLOCK)).reshape(
            B, G, Q_BLOCK, top * SEL_BLOCK)
        m_sel = (key_pos <= t_pos[None, None, :, None])[:, :, None]
        s = jnp.einsum('bgrqd,bgqkd->bgrqk', qr, kg)
        o_sel = jnp.einsum('bgrqk,bgqkd->bgrqd', masked_softmax(s, m_sel), vg)
        kwb = lax.dynamic_slice_in_dim(kw_pad, s0, WINDOW + Q_BLOCK, axis=2)
        vwb = lax.dynamic_slice_in_dim(vw_pad, s0, WINDOW + Q_BLOCK, axis=2)
        wpos = s0 - WINDOW + jnp.arange(WINDOW + Q_BLOCK)
        diff = t_pos[:, None] - wpos[None, :]
        m_win = (diff >= 0) & (diff < WINDOW) & (wpos[None, :] >= 0)
        s = jnp.einsum('bgrqd,bgkd->bgrqk', qr, kwb)
        o_win = jnp.einsum('bgrqk,bgkd->bgrqd', masked_softmax(s, m_win), vwb)
        return o_cmp, o_sel, o_win

    o_cmp, o_sel, o_win = lax.map(block, jnp.arange(T // Q_BLOCK))
    to_bthd = lambda o: o.transpose(1, 0, 4, 2, 3, 5).reshape(B, T, NSA_HEADS, Dh)
    gt = jax.nn.sigmoid(gates.astype(jnp.float32)).reshape(B, T, 3, NSA_HEADS, 1)
    out = (gt[:, :, 0] * to_bthd(o_cmp) + gt[:, :, 1] * to_bthd(o_sel)
           + gt[:, :, 2] * to_bthd(o_win))
    return out.reshape(B, T, NSA_WIDTH).astype(q.dtype)

def second_inputs(seed: int = 0) -> dict:
    key = jax.random.key(seed)
    k = jax.random.split(key, 24)
    f32 = jnp.float32
    nrm = lambda kk, shape, sc: jax.random.normal(kk, shape, f32) * sc
    gain = lambda kk, n: 1.0 + 0.05 * jax.random.normal(kk, (DEPTH, n), f32)
    return {
        "x": nrm(k[0], (BATCH, SEQ, D_MODEL), 1.0),
        "p": nrm(k[1], (DEPTH, BATCH, SEQ, PLE_DIM), 1.0),
        "w_in": nrm(k[2], (DEPTH, D_MODEL, N_IN), D_MODEL ** -0.5),
        "w_branch_a": nrm(k[3], (DEPTH, HG_VWIDTH, D_MODEL), HG_VWIDTH ** -0.5),
        "w_branch_b": nrm(k[4], (DEPTH, NSA_WIDTH, D_MODEL), NSA_WIDTH ** -0.5),
        "w_out": nrm(k[5], (DEPTH, D_MODEL, D_MODEL), D_MODEL ** -0.5),
        "norm_pre_mix": gain(k[6], D_MODEL),
        "norm_post_mix": gain(k[7], D_MODEL),
        "norm_pre_mlp": gain(k[8], D_MODEL),
        "norm_post_mlp": gain(k[9], D_MODEL),
        "hg_lb_logits": nrm(k[10], (DEPTH + 1, HG_WIDTH), 0.5),
        "hg_gnorm": gain(k[11], HG_DV),
        "cmp_pe_k": nrm(k[12], (DEPTH, CMP_LEN, NSA_DH), 0.1),
        "cmp_pe_v": nrm(k[13], (DEPTH, CMP_LEN, NSA_DH), 0.1),
        "cmp_wk1": nrm(k[14], (DEPTH, CMP_LEN * NSA_DH, CMP_HIDDEN), (CMP_LEN * NSA_DH) ** -0.5),
        "cmp_wk2": nrm(k[15], (DEPTH, CMP_HIDDEN, NSA_DH), CMP_HIDDEN ** -0.5),
        "cmp_wv1": nrm(k[16], (DEPTH, CMP_LEN * NSA_DH, CMP_HIDDEN), (CMP_LEN * NSA_DH) ** -0.5),
        "cmp_wv2": nrm(k[17], (DEPTH, CMP_HIDDEN, NSA_DH), CMP_HIDDEN ** -0.5),
        "w_up": nrm(k[18], (DEPTH, D_MODEL, D_FF), D_MODEL ** -0.5),
        "w_down": nrm(k[19], (DEPTH, D_FF, D_MODEL), D_FF ** -0.5),
        "w_ple": nrm(k[20], (DEPTH, PLE_DIM, D_MODEL), PLE_DIM ** -0.5),
        "w_ple_gate": nrm(k[21], (DEPTH, D_MODEL, D_MODEL), D_MODEL ** -0.5),
        "norm_ple": gain(k[22], D_MODEL),
    }

def second_block(x, p, w_in, w_branch_a, w_branch_b, w_out, norm_pre_mix, norm_post_mix,
              norm_pre_mlp, norm_post_mlp, hg_lb_logits, hg_gnorm, cmp_pe_k, cmp_pe_v,
              cmp_wk1, cmp_wk2, cmp_wv1, cmp_wv2, w_up, w_down, w_ple, w_ple_gate,
              norm_ple):
    lower_bounds = jnp.cumsum(jax.nn.softmax(hg_lb_logits.astype(jnp.float32), axis=0), axis=0)
    h = x
    for i in range(DEPTH):
        u = rms_norm(h, norm_pre_mix[i])
        proj = u @ w_in[i]
        hq, hf, hi, hg, nq, nkv, ngate, ga, gb = jnp.split(proj, SPLIT_POINTS, axis=-1)
        kc, vc, ks, vs, kw, vw = jnp.split(nkv, 6, axis=-1)
        y_a = hgrn2_mixer(hq, hf, hi, hg, lower_bounds[i], hg_gnorm[i])
        y_b = nsa_mixer(nq, kc, vc, ks, vs, kw, vw, ngate, cmp_pe_k[i], cmp_pe_v[i],
                        cmp_wk1[i], cmp_wk2[i], cmp_wv1[i], cmp_wv2[i])
        merged = (jax.nn.sigmoid(ga) * (y_a @ w_branch_a[i])
                  + jax.nn.sigmoid(gb) * (y_b @ w_branch_b[i]))
        h = h + rms_norm(merged @ w_out[i], norm_post_mix[i])
        v = rms_norm(h, norm_pre_mlp[i])
        ff = jnp.square(jax.nn.relu(v @ w_up[i])) @ w_down[i]
        h = h + rms_norm(ff, norm_post_mlp[i])
        e = (p[i] @ w_ple[i]) * jax.nn.sigmoid(h @ w_ple_gate[i])
        h = h + rms_norm(e, norm_ple[i])
    return h


def setup_inputs(seed=0):
    out = dict(first_inputs(seed))
    for name, value in second_inputs(seed + 1).items():
        if name != "x":
            out[name + "_2"] = value
    return out


def reference(
    x, c, ctx, c_ctx, ada_w, ada_b, norm1_g, w_in, pool_w, pool_scale, na_rpb, w_out, norm2_g,
    peer_wq, peer_keys, peer_u, peer_v, final_g, p_2, w_in_2, w_branch_a_2, w_branch_b_2,
    w_out_2, norm_pre_mix_2, norm_post_mix_2, norm_pre_mlp_2, norm_post_mlp_2, hg_lb_logits_2,
    hg_gnorm_2, cmp_pe_k_2, cmp_pe_v_2, cmp_wk1_2, cmp_wk2_2, cmp_wv1_2, cmp_wv2_2, w_up_2,
    w_down_2, w_ple_2, w_ple_gate_2, norm_ple_2,
):
    x = first_block(
        x, c, ctx, c_ctx, ada_w, ada_b, norm1_g, w_in, pool_w, pool_scale, na_rpb, w_out,
        norm2_g, peer_wq, peer_keys, peer_u, peer_v, final_g,
    )
    return second_block(
        x, p_2, w_in_2, w_branch_a_2, w_branch_b_2, w_out_2, norm_pre_mix_2, norm_post_mix_2,
        norm_pre_mlp_2, norm_post_mlp_2, hg_lb_logits_2, hg_gnorm_2, cmp_pe_k_2, cmp_pe_v_2,
        cmp_wk1_2, cmp_wk2_2, cmp_wv1_2, cmp_wv2_2, w_up_2, w_down_2, w_ple_2, w_ple_gate_2,
        norm_ple_2,
    )


_drawn_inputs = setup_inputs


def setup_inputs(seed=0):
    import zlib

    import numpy as np

    out = dict(_drawn_inputs(seed))
    spreads = {}
    factors = {'ada_b': 3.403, 'norm1_g': 3.552, 'na_rpb': 8.0, 'cmp_pe_k_2': 8.0, 'norm2_g': 3.219}
    for name, (base, spread) in spreads.items():
        noise = np.random.default_rng([zlib.crc32(name.encode()), seed]).standard_normal(out[name].shape)
        drawn = base * np.exp(spread * noise) if base else spread * noise
        out[name] = jnp.asarray(drawn.astype(out[name].dtype))
    for name, factor in factors.items():
        out[name] = (out[name] * factor).astype(out[name].dtype)
    return out
```

```python
from contextlib import ExitStack
import math

import numpy as np
import concourse.bass as bass
from concourse import mybir

P = 128
T = 256
TT = T // P
D = 1024
C = D // P
RING = 4
UNIT = 2048
GRID = 64
KW = 16
NA_H = 8
DH = 64
HP = 16
TOPK = 16
PEER_H = 8
NKEYS = 128
CMP = (T - 32) // 16 + 1
HG_H = 8
NSA_H = 16
NSA_G = 4
EPS = 1e-6
NEG = -1e30
LEVELS = 7

F32 = mybir.dt.float32
U32 = mybir.dt.uint32
I32 = mybir.dt.int32
ALU = mybir.AluOpType
ACT = mybir.ActivationFunctionType
AX = mybir.AxisListType

UNITS = {}
_n = 0
for _name, _count in (("ada0", 4), ("ada1", 4), ("w_in", 8), ("band", 1), ("ada2", 4), ("w_out", 4),
                      ("ada3", 4), ("ada4", 4), ("wq", 8), ("keys", 1), ("peer", 128), ("ada5", 4),
                      ("hq_hf", 8), ("hi_hg", 8), ("nsa_t", 8), ("vs_vw", 2), ("ga_gb", 8),
                      ("wk1", 2), ("wv1", 2), ("branch_a", 4), ("branch_b", 4), ("w_out2", 4),
                      ("mlp", 32), ("ple", 1), ("ple_gate", 4)):
    UNITS[_name] = _n
    _n += _count
N_UNITS = _n

COLS = {}
_n = 0
for _name, _count in (("ada_b", 48), ("norm1_g", 8), ("norm2_g", 8), ("c", 8), ("c_ctx", 8),
                      ("pool_scale", 4), ("pre_mix", 8), ("pre_mlp", 8), ("lb_logits", 16)):
    COLS[_name] = (_n, _count)
    _n += _count
N_COLS = _n
ROWS = {"final_g": 0, "post_mix": 1, "post_mlp": 2, "ple": 3}

CONST2 = {}
_n = 0
for _name, _count in (("causal", P), ("cmp_add", 2 * CMP), ("cmp_keep", 2 * CMP), ("rope_cos", T),
                      ("rope_sin", T), ("rope_swap", P), ("level_mask", LEVELS * P), ("scan_keep", T)):
    CONST2[_name] = (_n, _count)
    _n += _count
N_CONST2 = _n


def constants():
    first = np.zeros((P, 2 * P + GRID), np.float32)
    first[:, :P] = np.eye(P)
    first[:, P:2 * P] = np.arange(P)
    col = np.arange(GRID)
    c0 = np.clip(col - KW // 2, 0, GRID - KW)
    inside = (col[None, :] >= c0[:, None]) & (col[None, :] < c0[:, None] + KW)
    first[:, 2 * P:] = np.tile(np.where(inside, 0.0, NEG), (2, 1))

    second = np.zeros((P, N_CONST2), np.float32)

    def put(name, a):
        at, n = CONST2[name]
        second[:, at:at + n] = a.reshape(P, n)

    q = np.arange(P)
    put("causal", np.where(q[None, :] <= q[:, None], 0.0, NEG))
    end = np.arange(CMP) * 16 + 31
    seen = end[None, None, :] <= (q[:, None, None] + P * np.arange(TT)[None, :, None])
    put("cmp_add", np.where(seen, 0.0, NEG))
    put("cmp_keep", seen.astype(np.float32))
    inv = (500000.0 ** (-np.arange(8) * 2.0 / 16)).astype(np.float32)
    ang = np.arange(T, dtype=np.float32)[:, None] * inv[None, :]
    cos, sin = np.cos(ang), np.sin(ang)
    rc, rs, swap = np.ones((P, T)), np.zeros((P, T)), np.zeros((P, P))
    for base in (0, 64):
        for d in range(8):
            rc[base + d], rc[base + 8 + d] = cos[:, d], cos[:, d]
            rs[base + d], rs[base + 8 + d] = -sin[:, d], sin[:, d]
            swap[base + 8 + d, base + d] = swap[base + d, base + 8 + d] = 1.0
    put("rope_cos", rc)
    put("rope_sin", rs)
    put("rope_swap", swap)
    masks = np.zeros((P, LEVELS, P), np.float32)
    for level in range(LEVELS):
        half = 1 << level
        same = (q[:, None] // (2 * half)) == (q[None, :] // (2 * half))
        masks[:, level] = same & (q[:, None] % (2 * half) < half) & (q[None, :] % (2 * half) >= half)
    put("level_mask", masks)
    put("scan_keep", np.tile((np.arange(T) % 64 != 0).astype(np.float32), (P, 1)))

    band = np.zeros((4, T, T), np.float32)
    t = np.arange(T)
    for g, w in enumerate((2, 4, 8, 16)):
        lo, hi = np.clip(t - w // 2, 0, T), np.clip(t + w // 2, 0, T)
        in_win = (t[:, None] >= lo[None, :]) & (t[:, None] < hi[None, :])
        band[g] = np.where(in_win, 1.0 / (hi - lo)[None, :], 0.0) - np.eye(T)
    band = band.reshape(4, TT, P, T).transpose(2, 1, 0, 3).reshape(P, UNIT)
    return first, second, np.ascontiguousarray(band.astype(np.float32))


def build(nc, weights, x, ctx_in, cols_in, rows_in, gnorm_in, const1, const2, rpb, pool_w, gate_w,
          pe_t, w2_in, p_t, out):
    with ExitStack() as stack:
        def sb(name, shape, dt=F32):
            return stack.enter_context(nc.sbuf_tensor(name, shape, dt))

        def sem(name):
            return stack.enter_context(nc.semaphore(name))

        ring = [sb(f"ring{s}", [P, UNIT]) for s in range(RING)]
        res = sb("res", [P, TT, D])
        act_t = sb("act_t", [P, C, T])
        cols = sb("cols", [P, N_COLS])
        c1 = sb("c1", [P, 2 * P + GRID])
        mod = sb("mod", [P, 6, C, 2])
        scale_t = sb("scale_t", [P, 3, C])
        silu_c = sb("silu_c", [P, C, 2])
        stat = sb("stat", [P, 9, 4, TT])
        hk_t = sb("hk_t", [P, 3, T])
        hidden = sb("hidden", [P, 4, 512])
        ident = c1[:, 0:P]
        iota = c1[:, P:2 * P]
        win_mask = c1[:, 2 * P:]

        ARENA = 32850
        arena = sb("arena", [P, ARENA])

        class Area:
            def __init__(self, at):
                self.at = at

            def take(self, *shape):
                n = math.prod(shape)
                ap = arena[:, self.at:self.at + n]
                self.at += n
                assert self.at <= ARENA, self.at
                if len(shape) == 2:
                    return ap.rearrange("p (a b) -> p a b", a=shape[0])
                if len(shape) == 3:
                    return ap.rearrange("p (a b c) -> p a b c", a=shape[0], b=shape[1])
                return ap

        a1 = Area(0)
        hat = a1.take(TT, D)
        ctx_nat = a1.take(TT, D)
        ctx_t = a1.take(C, T)
        px = a1.take(2, TT, 256)
        qx_t = a1.take(4, T)
        kx_t = a1.take(4, T)
        kc_t = a1.take(4, T)
        vx = a1.take(2, TT, 256)
        vc = a1.take(2, TT, 256)
        pooled_t = a1.take(4, T)
        mix_t = a1.take(C, T)
        bias = a1.take(TT, NA_H, T)
        na_p = a1.take(3, 512)
        na_pt = a1.take(4, 512)
        na_stat = a1.take(3, 3)
        gate_row = a1.take(D)
        poolw = a1.take(4, P)

        a2 = Area(2048)
        pq_t = a2.take(HP, T)
        score = a2.take(TT, HP * NKEYS)
        rest = a2.take(HP * NKEYS)
        top = a2.take(TT, HP * TOPK)
        top_i = a2.take(HP * TOPK)
        top_if = a2.take(TT, HP * TOPK)
        cand = a2.take(UNIT)
        cand_rest = a2.take(UNIT)
        best = a2.take(TT, P)
        best_i = a2.take(P)
        part_a = a2.take(P)
        part_af = a2.take(P)
        pick = a2.take(UNIT)
        chosen = a2.take(3, P)
        soft = a2.take(4, PEER_H)
        a3 = Area(0)
        dense = a3.take(NKEYS, T)
        onehot = hidden.rearrange("p a b -> p (a b)")
        junk = onehot.rearrange("p (t d) -> p t d", t=TT)
        gate_row2 = act_t.rearrange("p c t -> p (c t)")[:, 0:D]

        a4 = Area(0)
        c2 = a4.take(N_CONST2)
        gnorm = a4.take(P)
        row = a4.take(D)
        hqf = a4.take(16, T)
        hig = a4.take(8, 512)
        nsa_t = a4.take(16, T)
        vsw = a4.take(2, 512)
        gab = a4.take(8, 512)
        gates = a4.take(TT, 48)
        pt = a4.take(2, T)
        gw = a4.take(C, 48)
        yb_t = act_t
        reuse = a4.at
        a5 = Area(reuse)
        logf = a5.take(HG_H, T)
        cum = a5.take(HG_H, T)
        level_x = [a5.take(HG_H, T), a5.take(HG_H, T)]
        ad_t = a5.take(TT, HG_H, P)
        ax_t = a5.take(HG_H, P)
        a5_end = a5.at
        o_nat = logf.rearrange("p h t -> p (h t)").rearrange("p (a b) -> p a b", a=TT)
        o_sq = cum.rearrange("p h t -> p (h t)").rearrange("p (a b) -> p a b", a=TT)
        hat3 = logf.rearrange("p h t -> p (h t)").rearrange("p (a b) -> p a b", a=TT)
        lbt = sb("lbt", [P, 6, C])
        ostat = sb("ostat", [P, 4, 16])
        ya_t = hqf[:, 0:8, :]
        a6 = Area(reuse)
        q_rot = hqf[:, 8:16, :]
        rope_tmp = a6.take(512)
        k_rot = a6.take(4, T)
        k_both = a6.take(2 * NSA_G, T)
        cmp_in = a6.take(2, 16 * 60)
        cmp_hid = a6.take(4, 60)
        kcmp_t = a6.take(NSA_G, 2, CMP)
        vb = a6.take(NSA_G * 2 * P)
        cmp_s = a6.take(TT, NSA_H * CMP)
        cmp_p = a6.take(TT, NSA_H * 32)
        cmp_pt = a6.take(TT, 512)
        cmp_stat = a6.take(TT, 4 * NSA_H)
        pe_cols = a6.take(2, 16)
        w2 = a6.take(2, 2 * P)
        hig_flat = hig.rearrange("p a b -> p (a b)")
        at_p = hig_flat[:, 0:1536].rearrange("p (a b) -> p a b", a=3)
        at_pt = hig_flat[:, 1536:3584].rearrange("p (a b) -> p a b", a=4)
        at_stat = hig_flat[:, 3584:3632].rearrange("p (a b) -> p a b", a=3)
        a8 = Area(reuse)
        merged = a8.take(TT, D)
        side = a8.take(TT, D)
        hat2 = a8.take(TT, D)

        psum = [stack.enter_context(nc.psum_tensor(f"bank{b}", [P, 512], F32)) for b in range(8)]

        loaded = [sem(f"unit_loaded{s}") for s in range(RING)]
        passed = [sem(f"unit_passed{s}") for s in range(RING)]
        filled = [sem(f"bank_filled{b}") for b in range(4)]
        emptied = [sem(f"bank_emptied{b}") for b in range(4)]
        sum_filled = [sem(f"sum_filled{b}") for b in range(4)]
        sum_emptied = [sem(f"sum_emptied{b}") for b in range(4)]
        small_loaded = sem("small_loaded")
        x_loaded = sem("x_loaded")
        ctx_loaded = sem("ctx_loaded")
        bias_loaded = sem("bias_loaded")
        bias_masked = sem("bias_masked")
        poolw_loaded = sem("poolw_loaded")
        const2_loaded = sem("const2_loaded")
        nsa_small_loaded = sem("nsa_small_loaded")
        row_loaded = sem("row_loaded")
        row_used = sem("row_used")
        silu_ready = sem("silu_ready")
        scale_ready = sem("scale_ready")
        squares = sem("squares")
        variance = sem("variance")
        root = sem("root")
        hat_ready = sem("hat_ready")
        res_ready = sem("res_ready")
        dve_chain = sem("dve_chain")
        act_chain = sem("act_chain")
        onehot_ready = [sem(f"onehot_ready{h}") for h in range(2)]
        tokens_filled = [sem(f"tokens_filled{h}") for h in range(2)]
        tokens_placed = [sem(f"tokens_placed{h}") for h in range(2)]
        hid_filled = [sem(f"hid_filled{h}") for h in range(2)]
        hid_raw = [sem(f"hid_raw{h}") for h in range(2)]
        hid_ready = [sem(f"hid_ready{h}") for h in range(2)]
        hid_used = [sem(f"hid_used{h}") for h in range(2)]
        na_neg_ready = sem("na_neg_ready")
        na_exp = sem("na_exp")
        na_norm = sem("na_norm")
        chosen_ready = sem("chosen_ready")
        soft_ready = sem("soft_ready")
        soft_exp = sem("soft_exp")
        lb_ready = sem("lb_ready")
        hg_pre = sem("hg_pre")
        hg_log = sem("hg_log")
        level_arg = sem("level_arg")
        level_exp = sem("level_exp")
        level_ready = sem("level_ready")
        ovar = sem("ovar")
        oroot = sem("oroot")
        ya_ready = sem("ya_ready")
        rot_ready = sem("rot_ready")
        cmp_copied = sem("cmp_copied")
        cmp_in_ready = sem("cmp_in_ready")
        cmp_arg = sem("cmp_arg")
        cmp_exp = sem("cmp_exp")
        cmp_ready = sem("cmp_ready")
        vb_zero = sem("vb_zero")
        at_neg = sem("at_neg")
        at_exp = sem("at_exp")
        at_norm = sem("at_norm")
        sig_ready = sem("sig_ready")
        merged_ready = sem("merged_ready")
        stored = sem("stored")

        JOB = {}
        SUM = {}
        count = {"job": 0, "sum": 0}

        def jobs(name, n):
            JOB[name] = count["job"]
            count["job"] += n

        def sums(name, n):
            SUM[name] = count["sum"]
            count["sum"] += n

        jobs("ada0", 1), jobs("ada1", 1), jobs("x_t", 4), jobs("ctx_t", 4), jobs("w_in", 12)
        jobs("pool", 2), jobs("pool_y", 2), jobs("ada2", 1), jobs("gate1", 2)
        NA_LAG_T, NA_LAG_V = 2, 3

        def attention_jobs(name, n):
            for k in range(n + NA_LAG_V):
                if k < n:
                    jobs((name, "s", k), 1)
                if 0 <= k - NA_LAG_T < n:
                    jobs((name, "t", k - NA_LAG_T), 1)

        N_NA = NA_H * TT
        attention_jobs("na", N_NA)
        sums("na", N_NA // 2)
        sums("w_out", 4)
        jobs("ada3", 1), jobs("ada4", 1), jobs("h2_t", 4), jobs("wq", 8), jobs("key", 8), jobs("hk", 2)
        sums("peer", 4)
        jobs("ada5", 1), jobs("gate2", 2), jobs("u_t", 4)
        jobs("hq_hf", 8), jobs("hi_hg", 8), jobs("nsa_t", 8), jobs("vs_vw", 2), jobs("gates", 1), jobs("ga_gb", 8)
        jobs("level", 8 * 4 + 2), jobs("o", 4), jobs("ya_t", 4)
        jobs("rope", 6), jobs("cmp_hid", 4), jobs("cmp_out", 2), jobs("cmp_s", 2), jobs("cmp_t", 2)
        N_AT = NSA_H * TT
        attention_jobs("at", N_AT)
        sums("at", NSA_H // 2 * TT)
        sums("branch_a", 4), sums("branch_b", 4)
        jobs("m_t", 4)
        sums("w_out2", 4)
        jobs("v_t", 4)
        sums("mlp", 4)
        jobs("h_t", 4)
        sums("ple", 4), sums("ple_gate", 4)

        def bank(j):
            return psum[j % 4]

        def is_filled(eng, j):
            eng.wait_ge(filled[j % 4], j // 4 + 1)

        def is_emptied(eng, j):
            eng.wait_ge(emptied[j % 4], j // 4 + 1)

        def sum_bank(j):
            return psum[4 + j % 4]

        def sum_is_filled(eng, j):
            eng.wait_ge(sum_filled[j % 4], j // 4 + 1)

        def sum_is_emptied(eng, j):
            eng.wait_ge(sum_emptied[j % 4], j // 4 + 1)

        def col(name, i=0):
            at = COLS[name][0] + i
            return cols[:, at:at + 1]

        def colset(name):
            at, n = COLS[name]
            return cols[:, at:at + n]

        def const(name):
            at, n = CONST2[name]
            return c2[:, at:at + n]

        AT_ITEMS = [(h // 2, t, h) for c in range(NSA_H // 2) for t in range(TT) for h in (2 * c, 2 * c + 1)]

        block = stack.enter_context(nc.Block())

        @block.sync
        def _(sp):
            sp.dma_start(cols[:], cols_in).then_inc(small_loaded, 16)
            sp.dma_start(c1[:], const1).then_inc(small_loaded, 16)
            sp.dma_start(res[:], x.rearrange("(t p) d -> p t d", p=P)).then_inc(x_loaded, 16)
            sp.dma_start(ctx_nat, ctx_in.rearrange("(t p) d -> p t d", p=P)).then_inc(ctx_loaded, 16)
            for s in range(RING):
                sp.dma_start(ring[s][:], weights[s]).then_inc(loaded[s], 16)
            with sp.Fori(1, N_UNITS // RING) as i:
                for s in range(RING):
                    sp.wait_ge(passed[s], i)
                    sp.dma_start(ring[s][:], weights[bass.ds(i * RING + s, 1)].rearrange("a p n -> (a p) n"))\
                      .then_inc(loaded[s], 16)
            for s in range(N_UNITS % RING):
                sp.wait_ge(passed[s], N_UNITS // RING)
                sp.dma_start(ring[s][:], weights[N_UNITS // RING * RING + s]).then_inc(loaded[s], 16)
            sp.wait_ge(res_ready, 6)
            sp.dma_start(out.rearrange("(t p) d -> p t d", p=P), res[:]).then_inc(stored, 16)
            sp.wait_ge(stored, 16)

        @block.gpsimd
        def _(pool):
            for turn in (*tokens_filled, *tokens_placed, *hid_ready, *hid_used):
                pool.sem_inc(turn, 1)
            pool.dma_start(poolw, pool_w).then_inc(poolw_loaded, 16)
            for r in range(4):
                lo = (r % 2) * GRID
                pool.dma_start(bias[lo:lo + GRID, r // 2], rpb[:, :, 3 - r:7 - r, :]
                               .rearrange("w h i c -> w h (i c)")).then_inc(bias_loaded, 16)
            pool.wait_ge(bias_loaded, 64)
            pool.wait_ge(small_loaded, 32)
            flat = bias.rearrange("p t h (i c) -> p (t h i) c", c=GRID)
            nc.gpsimd.tensor_tensor(flat, flat, win_mask.unsqueeze(1).broadcast_to([P, 64, GRID]), ALU.add)\
                .then_inc(bias_masked, 1)
            pool.wait_ge(res_ready, 2)
            pool.dma_start(row, rows_in[0:1, :].broadcast_to([P, D])).then_inc(row_loaded, 16)
            pool.dma_start(c2, const2).then_inc(const2_loaded, 16)
            pool.dma_start(gnorm, gnorm_in.broadcast_to([P, P])).then_inc(const2_loaded, 16)
            pool.dma_start(gw, gate_w).then_inc(const2_loaded, 16)
            pool.dma_start(pt, p_t).then_inc(const2_loaded, 16)
            for n in range(1, 4):
                pool.wait_ge(row_used, n)
                pool.dma_start(row, rows_in[n:n + 1, :].broadcast_to([P, D])).then_inc(row_loaded, 16)
                if n == 1:
                    pool.wait_ge(ya_ready, 1)
                    pool.dma_start(pe_cols, pe_t).then_inc(nsa_small_loaded, 16)
                    pool.dma_start(w2.rearrange("p a b -> p (a b)"), w2_in).then_inc(nsa_small_loaded, 16)
                    nc.gpsimd.memset(vb, 0.0).then_inc(vb_zero, 1)
                    nc.gpsimd.memset(kcmp_t, 0.0).then_inc(vb_zero, 1)
                    nc.gpsimd.memset(cmp_p, 0.0).then_inc(vb_zero, 1)

        @block.tensor
        def _(pe):
            mm = nc.tensor.matmul

            def unit(u):
                pe.wait_ge(loaded[u % RING], 16 * (u // RING + 1))
                return ring[u % RING]

            def pass_previous(ins, u):
                if u:
                    ins.then_inc(passed[(u - 1) % RING], 1)

            def open_job(j):
                if j >= 4:
                    is_emptied(pe, j - 4)
                return bank(j)

            def open_sum(j):
                if j >= 4:
                    sum_is_emptied(pe, j - 4)
                return sum_bank(j)

            def adaln(v):
                b = open_job(JOB[f"ada{v}"])
                for k in range(4):
                    w = unit(UNITS[f"ada{v}"] + k).rearrange("p (c n) -> p c n", c=C)
                    for m in range(2):
                        at = (2 * k + m) * 2
                        for c in range(C):
                            last = mm(b[:, at:at + 2], w[:, c, m * P:m * P + P], silu_c[:, c, :],
                                      start=(c == 0), stop=(c == C - 1))
                            if m == 0 and c == 0:
                                pass_previous(last, UNITS[f"ada{v}"] + k)
                last.then_inc(filled[JOB[f"ada{v}"] % 4], 1)

            def transposed_job(u, j, src, first=True):
                w = unit(u).rearrange("p (c n) -> p c n", c=C)
                b = open_job(j)
                for m in range(2):
                    for c in range(C):
                        last = mm(b[:, m * T:m * T + T], w[:, c, m * P:m * P + P], src[:, c, :],
                                  start=(c == 0), stop=(c == C - 1))
                        if first and m == 0 and c == 0:
                            pass_previous(last, u)
                last.then_inc(filled[j % 4], 1)

            def natural_job(u, j, src, first=True):
                w = unit(u).rearrange("p (c n) -> p c n", c=C)
                b = open_job(j)
                for t in range(TT):
                    for c in range(C):
                        last = mm(b[:, t * 256:t * 256 + 256], src[:, c, t * P:t * P + P], w[:, c, :],
                                  start=(c == 0), stop=(c == C - 1))
                        if first and t == 0 and c == 0:
                            pass_previous(last, u)
                last.then_inc(filled[j % 4], 1)

            def row_units(name, n, src):
                for k in range(4):
                    open_sum(SUM[name] + k)
                for k in range(n):
                    w = unit(UNITS[name] + k)
                    for r in range(2):
                        for t in range(TT):
                            for half in range(2):
                                s = SUM[name] + 2 * t + half
                                last = mm(sum_bank(s)[:, :], src[:, 2 * k + r, t * P:t * P + P],
                                          w[:, r * D + half * 512:r * D + half * 512 + 512],
                                          start=(k == 0 and r == 0), stop=(k == n - 1 and r == 1))
                                if r == 0 and t == 0 and half == 0:
                                    pass_previous(last, UNITS[name] + k)
                                if k == n - 1 and r == 1:
                                    last.then_inc(sum_filled[s % 4], 1)

            def transposes(name, src):
                for k in range(4):
                    b = open_job(JOB[name] + k)
                    for m in range(2):
                        for t in range(TT):
                            at = m * T + t * P
                            last = nc.tensor.transpose(b[:, at:at + P], src[:, t, (2 * k + m) * P:(2 * k + m) * P + P],
                                                       ident)
                    last.then_inc(filled[(JOB[name] + k) % 4], 1)

            def gate_rows(name, v):
                for k in range(2):
                    b = open_job(JOB[name] + k)
                    for m in range(4):
                        last = mm(b[:, m * P:m * P + P], mod[:, v, 4 * k + m, 0:1].broadcast_to([P, P]), ident,
                                  start=True, stop=True)
                    last.then_inc(filled[(JOB[name] + k) % 4], 1)

            def mlp_like(first_unit, n, src, base, s0):
                def up(k, u, done):
                    slot, rnd = u
                    pe.wait_ge(loaded[slot], 16 * (rnd + 1))
                    pe.wait_ge(hid_raw[k], done)
                    w = ring[slot].rearrange("p (c n) -> p c n", c=C)
                    for m in range(2):
                        for c in range(C):
                            last = mm(psum[k][:, m * T:m * T + T], w[:, c, m * P:m * P + P], src[:, c, :],
                                      start=(c == 0), stop=(c == C - 1))
                            if m == 0 and c == 0:
                                last.then_inc(passed[(slot - 1) % RING], 1)
                    last.then_inc(hid_filled[k], 1)

                def down(k, u, done, first, final):
                    slot, rnd = u
                    pe.wait_ge(loaded[slot], 16 * (rnd + 1))
                    pe.wait_ge(hid_ready[k], done + 2)
                    for r in range(2):
                        for t in range(TT):
                            for half in range(2):
                                s = s0 + 2 * t + half
                                last = mm(sum_bank(s)[:, :], hidden[:, 2 + k, r * T + t * P:r * T + t * P + P],
                                          ring[slot][:, r * D + half * 512:r * D + half * 512 + 512],
                                          start=(first and r == 0), stop=(final and r == 1))
                                if r == 0 and t == 0 and half == 0:
                                    last.then_inc(passed[(slot - 1) % RING], 1)
                                if final and r == 1:
                                    last.then_inc(sum_filled[s % 4], 1)
                    if not final:
                        last.then_inc(hid_used[k], 1)

                def at(k, i=0):
                    u = first_unit + k
                    return u % RING, u // RING + i

                for k in range(4):
                    open_sum(s0 + k)
                up(0, at(0), base)
                up(1, at(1), base)
                down(0, at(2), base, True, False)
                with pe.Fori(0, n // 2 - 1) as i:
                    up(0, at(3, i), i + (base + 1))
                    down(1, at(4, i), i + base, False, False)
                    up(1, at(5, i), i + (base + 1))
                    down(0, at(6, i), i + (base + 1), False, False)
                down(1, at(2 * n - 1), base + n // 2 - 1, False, True)

            def attention(name, n, scores, transpose, values):
                for k in range(n + NA_LAG_V):
                    if k < n:
                        scores(k)
                    if 0 <= k - NA_LAG_T < n:
                        transpose(k - NA_LAG_T)
                    if 0 <= k - NA_LAG_V < n:
                        values(k - NA_LAG_V)

            pe.wait_ge(silu_ready, 2)
            adaln(0)
            adaln(1)
            pe.wait_ge(small_loaded, 32)
            pe.wait_ge(hat_ready, 1)
            transposes("x_t", hat)
            pe.wait_ge(hat_ready, 2)
            transposes("ctx_t", ctx_nat)
            for k in range(4):
                is_emptied(pe, JOB["x_t"] + k)
                is_emptied(pe, JOB["ctx_t"] + k)
            u0, j0 = UNITS["w_in"], JOB["w_in"]
            natural_job(u0, j0, act_t)
            natural_job(u0 + 1, j0 + 1, act_t)
            transposed_job(u0 + 2, j0 + 2, act_t)
            transposed_job(u0 + 3, j0 + 3, act_t)
            for k in range(2):
                transposed_job(u0 + 4 + k, j0 + 4 + 2 * k, act_t)
                transposed_job(u0 + 4 + k, j0 + 5 + 2 * k, ctx_t, first=False)
            for k in range(2):
                natural_job(u0 + 6 + k, j0 + 8 + 2 * k, act_t)
                natural_job(u0 + 6 + k, j0 + 9 + 2 * k, ctx_t, first=False)
            is_emptied(pe, j0), is_emptied(pe, j0 + 1)
            band = unit(UNITS["band"]).rearrange("p (s g t) -> p s g t", s=TT, g=4)
            for k in range(2):
                b = open_job(JOB["pool"] + k)
                for m in range(2):
                    g = 2 * k + m
                    for s in range(TT):
                        last = mm(b[:, m * T:m * T + T], px[:, k, s, m * P:m * P + P], band[:, s, g, :],
                                  start=(s == 0), stop=(s == TT - 1))
                        if k == 0 and m == 0 and s == 0:
                            pass_previous(last, UNITS["band"])
                last.then_inc(filled[(JOB["pool"] + k) % 4], 1)
            pe.wait_ge(poolw_loaded, 16)
            for k in range(2):
                is_emptied(pe, JOB["pool"] + k)
                b = open_job(JOB["pool_y"] + k)
                for m in range(2):
                    last = mm(b[:, m * T:m * T + T], poolw[:, 2 * k + m, :], pooled_t[:, 2 * k + m, :],
                              start=True, stop=True)
                last.then_inc(filled[(JOB["pool_y"] + k) % 4], 1)
            adaln(2)
            is_emptied(pe, JOB["ada2"])
            gate_rows("gate1", 2)

            for k in range(12):
                is_emptied(pe, j0 + k)

            def na_scores(k):
                h, t = (k // 4) * 2 + k % 2, (k // 2) % 2
                lo, j = (h % 2) * DH, JOB["na", "s", k]
                b = open_job(j)
                q = qx_t[lo:lo + DH, h // 2, t * P:t * P + P]
                mm(b[:, 0:T], q, kx_t[lo:lo + DH, h // 2, :], start=True, stop=True)
                mm(b[:, T:2 * T], q, kc_t[lo:lo + DH, h // 2, :], start=True, stop=True).then_inc(filled[j % 4], 1)

            def na_transpose(k):
                j = JOB["na", "t", k]
                b = open_job(j)
                pe.wait_ge(na_norm, k + 1)
                for m in range(4):
                    last = nc.tensor.transpose(b[:, m * P:m * P + P], na_p[:, k % 3, m * P:m * P + P], ident)
                last.then_inc(filled[j % 4], 1)

            def na_values(k):
                h = (k // 4) * 2 + k % 2
                lo, s = (h % 2) * DH, SUM["na"] + k // 2
                if k % 2 == 0:
                    open_sum(s)
                is_emptied(pe, JOB["na", "t", k])
                cs = (h % 4) * DH
                for m in range(4):
                    v = vx if m < 2 else vc
                    last = mm(sum_bank(s)[lo:lo + DH, 0:P], v[:, h // 4, m % 2, cs:cs + DH],
                              na_pt[:, k % 4, m * P:m * P + P], start=(m == 0), stop=(m == 3))
                if k % 2:
                    last.then_inc(sum_filled[s % 4], 1)

            attention("na", N_NA, na_scores, na_transpose, na_values)
            for k in range(N_NA // 2):
                sum_is_emptied(pe, SUM["na"] + k)
            for k in range(2):
                is_emptied(pe, JOB["pool_y"] + k)
            row_units("w_out", 4, mix_t)
            adaln(3)
            adaln(4)
            pe.wait_ge(hat_ready, 3)
            transposes("h2_t", hat)
            for k in range(4):
                is_emptied(pe, JOB["h2_t"] + k)
            for k in range(8):
                transposed_job(UNITS["wq"] + k, JOB["wq"] + k, act_t)
            keys = unit(UNITS["keys"])
            for k in range(8):
                t, part = k // 4, k % 4
                if t == 0:
                    is_emptied(pe, JOB["wq"] + 2 * part)
                    is_emptied(pe, JOB["wq"] + 2 * part + 1)
                b = open_job(JOB["key"] + k)
                for m in range(4):
                    hp = 4 * part + m
                    last = mm(b[:, m * P:m * P + P], pq_t[:, hp, t * P:t * P + P], keys[:, hp * P:hp * P + P],
                              start=True, stop=True)
                    if k == 0 and m == 0:
                        pass_previous(last, UNITS["keys"])
                last.then_inc(filled[(JOB["key"] + k) % 4], 1)
            for t in range(TT):
                b = open_job(JOB["hk"] + t)
                pe.wait_ge(chosen_ready, t + 1)
                for m in range(3):
                    last = nc.tensor.transpose(b[:, m * P:m * P + P], chosen[:, m, :], ident)
                last.then_inc(filled[(JOB["hk"] + t) % 4], 1)
            for k in range(4):
                is_emptied(pe, JOB["hk"] + 1 - k)
            with pe.Fori(0, T // 8) as i:
                for half in range(2):
                    pe.wait_ge(onehot_ready[half], i + 1)
                    pe.wait_ge(tokens_placed[half], i + 1)
                    for m in range(4):
                        n = 4 * half + m
                        last = mm(psum[2 + half][:, m * P:m * P + P], onehot[:, n * P:n * P + P],
                                  onehot[:, D + n * P:D + n * P + P], start=True, stop=True)
                    last.then_inc(tokens_filled[half], 1)
            mlp_like(UNITS["peer"], 64, act_t, 0, SUM["peer"])
            adaln(5)
            is_emptied(pe, JOB["ada5"])
            gate_rows("gate2", 5)

            pe.wait_ge(hat_ready, 5)
            transposes("u_t", hat3)
            for k in range(4):
                is_emptied(pe, JOB["u_t"] + k)
            for k in range(8):
                transposed_job(UNITS["hq_hf"] + k, JOB["hq_hf"] + k, act_t)
            for k in range(8):
                natural_job(UNITS["hi_hg"] + k, JOB["hi_hg"] + k, act_t)
            for k in range(8):
                transposed_job(UNITS["nsa_t"] + k, JOB["nsa_t"] + k, act_t)
            for k in range(2):
                natural_job(UNITS["vs_vw"] + k, JOB["vs_vw"] + k, act_t)
            pe.wait_ge(const2_loaded, 64)
            b = open_job(JOB["gates"])
            for t in range(TT):
                for c in range(C):
                    last = mm(b[:, t * 48:t * 48 + 48], act_t[:, c, t * P:t * P + P], gw[:, c, :],
                              start=(c == 0), stop=(c == C - 1))
            last.then_inc(filled[JOB["gates"] % 4], 1)
            for k in range(8):
                natural_job(UNITS["ga_gb"] + k, JOB["ga_gb"] + k, act_t)

            hq, hk = hqf[:, 0:8, :], hqf[:, 8:16, :]
            j = JOB["level"]
            for level in range(9):
                if level != 7:
                    pe.wait_ge(level_ready, level + 1 if level < 7 else 8)
                xl = level_x[level % 2] if level < 7 else level_x[1]
                for t in range(TT if level < 8 else 1):
                    for g in range(2):
                        b = open_job(j)
                        for m in range(4):
                            h = 4 * g + m
                            if level == 7:
                                lhs, rhs = hk[:, h, t * P:t * P + P], hq[:, h, t * P:t * P + P]
                            elif level == 8:
                                lhs, rhs = xl[:, h, 0:P], xl[:, h, P:T]
                            else:
                                lhs = rhs = xl[:, h, t * P:t * P + P]
                            last = mm(b[:, m * P:m * P + P], lhs, rhs, start=True, stop=True)
                        last.then_inc(filled[j % 4], 1)
                        j += 1
            for k in range(34):
                is_emptied(pe, JOB["level"] + k)
            for k in range(8):
                is_emptied(pe, JOB["hi_hg"] + k)
            for k in range(4):
                t, g = k // 2, k % 2
                b = open_job(JOB["o"] + k)
                for m in range(4):
                    h = 4 * g + m
                    o = b[:, m * P:m * P + P]
                    v = [hig[:, h // 2, s * 256 + (h % 2) * P:s * 256 + (h % 2) * P + P] for s in range(TT)]
                    if t:
                        mm(o, ax_t[:, h, :], v[0], start=True, stop=False)
                    last = mm(o, ad_t[:, t, h, :], v[t], start=(t == 0), stop=True)
                last.then_inc(filled[(JOB["o"] + k) % 4], 1)
            pe.wait_ge(ya_ready, 1)
            transposes("ya_t", o_nat)

            for k in range(8):
                is_emptied(pe, JOB["nsa_t"] + k)
            for k in range(6):
                b = open_job(JOB["rope"] + k)
                at = 2 * k if k < 4 else 12 + 2 * (k - 4)
                mm(b[:, :], const("rope_swap"), nsa_t[:, at:at + 2, :], start=True, stop=True)\
                    .then_inc(filled[(JOB["rope"] + k) % 4], 1)
            for kv in range(2):
                name = ("wk1", "wv1")[kv]
                j = JOB["cmp_hid"] + 2 * kv
                open_job(j), open_job(j + 1)
                pe.wait_ge(cmp_in_ready, kv + 1)
                for k in range(2):
                    w = unit(UNITS[name] + k).rearrange("p (l n) -> p l n", l=8)
                    for m in range(2):
                        for l in range(8):
                            last = mm(bank(j + m)[:, 0:60], w[:, l, m * P:m * P + P],
                                      cmp_in[:, kv, (8 * k + l) * 60:(8 * k + l) * 60 + 60],
                                      start=(k == 0 and l == 0), stop=(k == 1 and l == 7))
                            if m == 0 and l == 0:
                                pass_previous(last, UNITS[name] + k)
                        if k == 1:
                            last.then_inc(filled[(j + m) % 4], 1)
            pe.wait_ge(nsa_small_loaded, 32)
            for k in range(4):
                is_emptied(pe, JOB["cmp_hid"] + k)
            b = open_job(JOB["cmp_out"])
            for m in range(2):
                last = mm(b[:, 0:60], w2[:, 0, m * P:m * P + P], cmp_hid[:, m, :], start=(m == 0), stop=(m == 1))
            last.then_inc(filled[JOB["cmp_out"] % 4], 1)
            b = open_job(JOB["cmp_out"] + 1)
            for g in range(NSA_G):
                for m in range(2):
                    last = mm(b[0:CMP, g * DH:g * DH + DH], cmp_hid[:, 2 + m, g * CMP:g * CMP + CMP],
                              w2[:, 1, m * DH:m * DH + DH], start=(m == 0), stop=(m == 1))
            last.then_inc(filled[(JOB["cmp_out"] + 1) % 4], 1)
            is_emptied(pe, JOB["cmp_out"])
            for t in range(TT):
                b = open_job(JOB["cmp_s"] + t)
                for c in range(NSA_H // 2):
                    last = mm(b[:, 2 * c * CMP:(2 * c + 2) * CMP], nsa_t[:, c, t * P:t * P + P],
                              kcmp_t[:, c // 2, :, :], start=True, stop=True)
                last.then_inc(filled[(JOB["cmp_s"] + t) % 4], 1)
            for t in range(TT):
                b = open_job(JOB["cmp_t"] + t)
                pe.wait_ge(cmp_ready, t + 1)
                for g in range(NSA_G):
                    last = nc.tensor.transpose(b[:, g * P:g * P + P], cmp_p[:, t, g * P:g * P + P], ident)
                last.then_inc(filled[(JOB["cmp_t"] + t) % 4], 1)
            for t in range(TT):
                is_emptied(pe, JOB["cmp_t"] + t)
            is_emptied(pe, JOB["cmp_out"] + 1)
            pe.wait_ge(rot_ready, 1)
            for k in range(2):
                is_emptied(pe, JOB["vs_vw"] + k)
            vb4 = vb.rearrange("p (g i n) -> p g i n", g=NSA_G, i=2)

            def at_scores(k):
                c, t, h = AT_ITEMS[k]
                j = JOB["at", "s", k]
                b = open_job(j)
                width = P * (t + 1)
                lo, g = (h % 2) * DH, h // 4
                for branch in range(2):
                    last = mm(b[:, branch * width:(branch + 1) * width], q_rot[lo:lo + DH, c, t * P:t * P + P],
                              k_both[lo:lo + DH, branch * NSA_G + g, 0:width], start=True, stop=True)
                last.then_inc(filled[j % 4], 1)

            def at_transpose(k):
                j = JOB["at", "t", k]
                b = open_job(j)
                pe.wait_ge(at_norm, k + 1)
                for m in range(2 * (AT_ITEMS[k][1] + 1)):
                    last = nc.tensor.transpose(b[:, m * P:m * P + P], at_p[:, k % 3, m * P:m * P + P], ident)
                last.then_inc(filled[j % 4], 1)

            def at_values(k):
                c, t, h = AT_ITEMS[k]
                s = SUM["at"] + 2 * c + t
                if h % 2 == 0:
                    b = open_sum(s)
                    mm(b[:, 0:P], vb4[:, c // 2, c % 2, :], cmp_pt[:, t, (c // 2) * P:(c // 2) * P + P],
                       start=True, stop=False, skip_group_check=True)
                is_emptied(pe, JOB["at", "t", k])
                lo, g = (h % 2) * DH, h // 4
                for branch in range(2):
                    for tile in range(t + 1):
                        m = branch * (t + 1) + tile
                        v = vsw[:, branch, tile * 256 + g * DH:tile * 256 + g * DH + DH]
                        last = mm(sum_bank(s)[lo:lo + DH, 0:P], v, at_pt[:, k % 4, m * P:m * P + P],
                                  start=False, stop=(branch == 1 and tile == t), skip_group_check=True)
                if h % 2:
                    last.then_inc(sum_filled[s % 4], 1)

            attention("at", N_AT, at_scores, at_transpose, at_values)
            for k in range(4):
                is_emptied(pe, JOB["ya_t"] + k)
            row_units("branch_a", 4, ya_t)
            for k in range(NSA_H // 2 * TT):
                sum_is_emptied(pe, SUM["at"] + k)
            row_units("branch_b", 4, yb_t)
            pe.wait_ge(merged_ready, 1)
            transposes("m_t", merged)
            for k in range(4):
                is_emptied(pe, JOB["m_t"] + k)
            row_units("w_out2", 4, act_t)
            pe.wait_ge(hat_ready, 7)
            transposes("v_t", hat2)
            for k in range(4):
                is_emptied(pe, JOB["v_t"] + k)
            mlp_like(UNITS["mlp"], 16, act_t, 32, SUM["mlp"])
            pe.wait_ge(res_ready, 5)
            transposes("h_t", res)
            row_units("ple", 1, pt)
            for k in range(4):
                is_emptied(pe, JOB["h_t"] + k)
            row_units("ple_gate", 4, act_t)

        @block.scalar
        def _(act):
            fn = nc.scalar.activation
            chain = [0]

            def link(ins):
                chain[0] += 1
                ins.then_inc(act_chain, 1)
                act.wait_ge(act_chain, chain[0])

            def sum_squares(n, src):
                act.wait_ge(squares, n)
                for t in range(TT):
                    last = fn(junk[:, t, :], src[:, t, :], ACT.Square, accum_out=stat[:, n, 0, t:t + 1])
                last.then_inc(squares, 1)

            def take_root(n):
                act.wait_ge(variance, n + 1)
                fn(stat[:, n, 2, :], stat[:, n, 1, :], ACT.Sqrt).then_inc(root, 1)

            def evacuate(j, dst, scale=1.0, func=ACT.Copy):
                is_filled(act, j)
                fn(dst, bank(j)[:, :], func, scale=scale).then_inc(emptied[j % 4], 1)

            def evacuate_scaled(name, dst, scale, shift):
                for k in (0, 2):
                    j = JOB[name] + k
                    is_filled(act, j)
                    for m in range(2):
                        c = 2 * k + m
                        kw = {"bias": shift(c)} if shift else {}
                        last = fn(dst[:, c, :], bank(j)[:, m * T:m * T + T], ACT.Identity, scale=scale(c), **kw)
                    last.then_inc(emptied[j % 4], 1)

            def tokens_and_hidden(func, n, base):
                def raw(k, done):
                    act.wait_ge(hid_filled[k], done + 1)
                    act.wait_ge(hid_ready[k], done + 1)
                    fn(hidden[:, k, :], psum[k][:, :], func).then_inc(hid_raw[k], 1)

                with act.Fori(0, n // 2) as i:
                    raw(0, i + base)
                    raw(1, i + base)

            act.wait_ge(small_loaded, 32)
            fn(silu_c[:, :, 0], colset("c"), ACT.Silu).then_inc(silu_ready, 1)
            fn(silu_c[:, :, 1], colset("c_ctx"), ACT.Silu).then_inc(silu_ready, 1)
            act.wait_ge(x_loaded, 16)
            sum_squares(0, res)
            take_root(0)
            act.wait_ge(ctx_loaded, 16)
            sum_squares(1, ctx_nat)
            take_root(1)
            act.wait_ge(scale_ready, 1)
            evacuate_scaled("x_t", act_t, lambda c: scale_t[:, 0, c:c + 1], lambda c: mod[:, 0, c, 0:1])
            evacuate_scaled("ctx_t", ctx_t, lambda c: scale_t[:, 1, c:c + 1], lambda c: mod[:, 0, c, 1:2])
            j0 = JOB["w_in"]
            flat2 = lambda ap: ap.rearrange("p a b -> p (a b)")
            evacuate(j0, flat2(px[:, 0]))
            evacuate(j0 + 1, flat2(px[:, 1]))
            evacuate(j0 + 2, flat2(qx_t[:, 0:2, :]), scale=DH ** -0.5)
            evacuate(j0 + 3, flat2(qx_t[:, 2:4, :]), scale=DH ** -0.5)
            for k in range(2):
                evacuate(j0 + 4 + 2 * k, flat2(kx_t[:, 2 * k:2 * k + 2, :]))
                evacuate(j0 + 5 + 2 * k, flat2(kc_t[:, 2 * k:2 * k + 2, :]))
            for k in range(2):
                evacuate(j0 + 8 + 2 * k, flat2(vx[:, k]))
                evacuate(j0 + 9 + 2 * k, flat2(vc[:, k]))
            for k in range(2):
                evacuate(JOB["pool"] + k, flat2(pooled_t[:, 2 * k:2 * k + 2, :]))
            for k in range(2):
                j = JOB["pool_y"] + k
                is_filled(act, j)
                for m in range(2):
                    last = fn(mix_t[:, 2 * k + m, :], bank(j)[:, m * T:m * T + T], ACT.Copy,
                              scale=col("pool_scale", 2 * k + m))
                last.then_inc(emptied[j % 4], 1)
            for k in range(2):
                evacuate(JOB["gate1"] + k, gate_row[:, k * 512:k * 512 + 512])

            def na_sum(k):
                s = SUM["na"] + k
                sum_is_filled(act, s)
                fn(mix_t[:, 4 + k // 2, (k % 2) * P:(k % 2) * P + P], sum_bank(s)[:, 0:P], ACT.Copy)\
                    .then_inc(sum_emptied[s % 4], 1)

            for k in range(N_NA + NA_LAG_V + 1):
                if k < N_NA:
                    j = JOB["na", "s", k]
                    act.wait_ge(na_neg_ready, k + 1)
                    if k >= 3:
                        is_filled(act, JOB["na", "t", k - 3])
                    fn(na_p[:, k % 3, :], bank(j)[:, :], ACT.Exp, bias=na_stat[:, k % 3, 0:1],
                       accum_out=na_stat[:, k % 3, 1:2]).then_inc(emptied[j % 4], 1)
                if 0 <= k - NA_LAG_T < N_NA:
                    n = k - NA_LAG_T
                    j = JOB["na", "t", n]
                    is_filled(act, j)
                    if n >= 4:
                        sum_is_filled(act, SUM["na"] + (n - 4) // 2)
                    fn(na_pt[:, n % 4, :], bank(j)[:, :], ACT.Copy).then_inc(emptied[j % 4], 1)
                if 0 <= k - NA_LAG_V - 1 < N_NA and (k - NA_LAG_V - 1) % 2:
                    na_sum((k - NA_LAG_V - 1) // 2)

            act.wait_ge(res_ready, 1)
            sum_squares(2, res)
            take_root(2)
            act.wait_ge(scale_ready, 2)
            evacuate_scaled("h2_t", act_t, lambda c: scale_t[:, 2, c:c + 1], lambda c: mod[:, 3, c, 0:1])
            for k in range(8):
                evacuate(JOB["wq"] + k, flat2(pq_t[:, 2 * k:2 * k + 2, :]))
            for k in range(8):
                evacuate(JOB["key"] + k, score[:, k // 4, (k % 4) * 512:(k % 4) * 512 + 512])
            for t in range(TT):
                act.wait_ge(soft_ready, t + 1)
                fn(chosen[:, 2, :], chosen[:, 2, :], ACT.Exp).then_inc(soft_exp, 1)
                j = JOB["hk"] + t
                is_filled(act, j)
                fn(hk_t[:, :, t * P:t * P + P], bank(j)[:, 0:3 * P].rearrange("p (a b) -> p a b", a=3), ACT.Copy)\
                    .then_inc(emptied[j % 4], 1)
            with act.Fori(0, T // 8) as i:
                for half in range(2):
                    act.wait_ge(tokens_filled[half], i + 2)
                    fn(dense[:, :, bass.ds(i * 8 + 4 * half, 4)].rearrange("p j t -> p t j"),
                       psum[2 + half][:, :].rearrange("p (t j) -> p t j", t=4), ACT.Copy)\
                        .then_inc(tokens_placed[half], 1)
            tokens_and_hidden(ACT.Gelu, 64, 0)
            for k in range(2):
                evacuate(JOB["gate2"] + k, gate_row2[:, k * 512:k * 512 + 512])

            act.wait_ge(res_ready, 2)
            sum_squares(3, res)
            take_root(3)
            act.wait_ge(res_ready, 3)
            sum_squares(4, res)
            take_root(4)
            evacuate_scaled("u_t", act_t, lambda c: col("pre_mix", c), None)
            act.wait_ge(lb_ready, 1)
            fn(lbt[:, 1:3, :], lbt[:, 1:3, :], ACT.Exp).then_inc(lb_ready, 1)
            for k in range(8):
                evacuate(JOB["hq_hf"] + k, flat2(hqf[:, 2 * k:2 * k + 2, :]), func=ACT.Silu if k < 4 else ACT.Sigmoid)
            for k in range(8):
                evacuate(JOB["hi_hg"] + k, hig[:, k, :], func=ACT.Copy if k < 4 else ACT.Silu)
            act.wait_ge(hg_pre, 1)
            fn(flat2(logf), flat2(hqf[:, 8:16, :]), ACT.Ln).then_inc(hg_log, 1)
            for k in range(8):
                evacuate(JOB["nsa_t"] + k, flat2(nsa_t[:, 2 * k:2 * k + 2, :]), scale=DH ** -0.5 if k < 4 else 1.0)
            for k in range(2):
                evacuate(JOB["vs_vw"] + k, vsw[:, k, :])
            j = JOB["gates"]
            is_filled(act, j)
            fn(flat2(gates), bank(j)[:, 0:TT * 48], ACT.Sigmoid).then_inc(emptied[j % 4], 1)
            for k in range(8):
                evacuate(JOB["ga_gb"] + k, gab[:, k, :], func=ACT.Sigmoid)
            for n in range(8):
                act.wait_ge(level_arg, n + 1)
                fn(flat2(level_x[n % 2]), flat2(level_x[n % 2]), ACT.Exp).then_inc(level_exp, 1)
            for k in range(4):
                evacuate(JOB["o"] + k, o_nat[:, k // 2, (k % 2) * 512:(k % 2) * 512 + 512])
            act.wait_ge(ovar, 1)
            fn(ostat[:, 2, :], ostat[:, 1, :], ACT.Sqrt).then_inc(oroot, 1)
            for k in (0, 2):
                evacuate(JOB["ya_t"] + k, flat2(ya_t[:, 2 * k:2 * k + 2, :]))
            for kv in range(2):
                is_emptied(act, JOB["nsa_t"] + 4 + kv)
                for a in range(2):
                    for b in range(2):
                        src = nsa_t[a * DH:a * DH + DH, 8 + 2 * kv:10 + 2 * kv, 16 * b:16 * b + 16 * CMP]
                        dst = cmp_in[b * DH:b * DH + DH, kv].rearrange("p (l c a n) -> p a l c n", l=16, c=2, a=2)
                        last = fn(dst[:, a], src.rearrange("p c (n l) -> p l c n", l=16), ACT.Copy)
                last.then_inc(cmp_copied, 1)
            for k in range(4):
                j = JOB["cmp_hid"] + k
                is_filled(act, j)
                fn(cmp_hid[:, k, :], bank(j)[:, 0:60], ACT.Gelu_apprx_tanh).then_inc(emptied[j % 4], 1)
            j = JOB["cmp_out"]
            is_filled(act, j)
            act.wait_ge(vb_zero, 2)
            for z in range(2):
                half = slice(z * DH, z * DH + DH)
                last = fn(kcmp_t[half, :, z, :], bank(j)[half, 0:60].rearrange("p (g n) -> p g n", g=NSA_G), ACT.Copy)
            last.then_inc(emptied[j % 4], 1)
            is_filled(act, j + 1)
            vb5 = vb.rearrange("p (g i n) -> p g i n", g=NSA_G, i=2)
            for r in range(4):
                last = fn(vb5[32 * r:32 * r + CMP, :, r // 2, (r % 2) * DH:(r % 2) * DH + DH],
                          bank(j + 1)[0:CMP, 0:NSA_G * DH].rearrange("p (g d) -> p g d", g=NSA_G), ACT.Copy)
            last.then_inc(emptied[(j + 1) % 4], 1)
            for t in range(TT):
                act.wait_ge(cmp_arg, t + 1)
                fn(cmp_s[:, t, :], cmp_s[:, t, :], ACT.Exp).then_inc(cmp_exp, 1)
            for t in range(TT):
                evacuate(JOB["cmp_t"] + t, cmp_pt[:, t, :])

            def at_sum(s):
                sum_is_filled(act, SUM["at"] + s)
                fn(yb_t[:, s // 2, (s % 2) * P:(s % 2) * P + P], sum_bank(SUM["at"] + s)[:, 0:P], ACT.Copy)\
                    .then_inc(sum_emptied[(SUM["at"] + s) % 4], 1)

            for k in range(N_AT + NA_LAG_V + 1):
                if k < N_AT:
                    width = P * (AT_ITEMS[k][1] + 1)
                    j = JOB["at", "s", k]
                    act.wait_ge(at_neg, k + 1)
                    if k >= 3:
                        is_filled(act, JOB["at", "t", k - 3])
                    for m in range(2):
                        last = fn(at_p[:, k % 3, m * width:m * width + width], bank(j)[:, m * width:m * width + width],
                                  ACT.Exp, bias=at_stat[:, k % 3, m:m + 1], accum_out=at_stat[:, k % 3, 2 + m:3 + m])
                    last.then_inc(emptied[j % 4], 1)
                if 0 <= k - NA_LAG_T < N_AT:
                    n = k - NA_LAG_T
                    j = JOB["at", "t", n]
                    used = 2 * P * (AT_ITEMS[n][1] + 1)
                    is_filled(act, j)
                    if n >= 4:
                        sum_is_filled(act, SUM["at"] + (n - 4) // 2)
                    fn(at_pt[:, n % 4, 0:used], bank(j)[:, 0:used], ACT.Copy).then_inc(emptied[j % 4], 1)
                n = k - NA_LAG_V - 1
                if 0 <= n < N_AT and n % 2:
                    at_sum(n // 2)
            for k in (0, 2):
                evacuate(JOB["m_t"] + k, flat2(act_t[:, 2 * k:2 * k + 2, :]))

            def take_sums(name, dst, func=ACT.Copy):
                for k in range(4):
                    s = SUM[name] + k
                    sum_is_filled(act, s)
                    fn(dst[:, k // 2, (k % 2) * 512:(k % 2) * 512 + 512], sum_bank(s)[:, :], func)\
                        .then_inc(sum_emptied[s % 4], 1)
                for k in range(4):
                    sum_is_emptied(act, SUM[name] + k)

            take_sums("w_out2", side)
            sum_squares(5, side)
            take_root(5)
            act.wait_ge(res_ready, 4)
            sum_squares(6, res)
            take_root(6)
            evacuate_scaled("v_t", act_t, lambda c: col("pre_mlp", c), None)
            tokens_and_hidden(ACT.Relu, 16, 32)
            take_sums("mlp", side)
            sum_squares(7, side)
            take_root(7)
            for k in (0, 2):
                evacuate(JOB["h_t"] + k, flat2(act_t[:, 2 * k:2 * k + 2, :]))
            take_sums("ple", merged)
            take_sums("ple_gate", side, ACT.Sigmoid)
            act.wait_ge(merged_ready, 2)
            sum_squares(8, merged)
            take_root(8)

        @block.vector
        def _(dve):
            v = nc.vector
            chain = [0]

            def link(ins):
                chain[0] += 1
                ins.then_inc(dve_chain, 1)
                dve.wait_ge(dve_chain, chain[0])

            def flat(ap):
                return ap.rearrange("p a b -> p (a b)")

            def adaln(n):
                j = JOB[f"ada{n}"]
                is_filled(dve, j)
                v.tensor_tensor(mod[:, n], bank(j)[:, 0:16].rearrange("p (c z) -> p c z", z=2),
                                cols[:, COLS["ada_b"][0] + 8 * n:COLS["ada_b"][0] + 8 * n + 8]
                                .unsqueeze(2).broadcast_to([P, C, 2]), ALU.add).then_inc(emptied[j % 4], 1)
                is_emptied(dve, j)

            def norm(n, src, dst):
                dve.wait_ge(squares, n + 1)
                v.tensor_scalar(stat[:, n, 1, :], stat[:, n, 0, :], 1.0 / D, EPS, ALU.mult, ALU.add)\
                    .then_inc(variance, 1)
                dve.wait_ge(root, n + 1)
                link(v.reciprocal(stat[:, n, 3, :], stat[:, n, 2, :]))
                for t in range(TT):
                    last = v.tensor_scalar(dst[:, t, :], src[:, t, :], stat[:, n, 3, t:t + 1], None, ALU.mult)
                last.then_inc(hat_ready, 1)

            def times_row(n, dst):
                dve.wait_ge(row_loaded, 16 * (n + 1))
                v.tensor_tensor(dst, dst, row.unsqueeze(1).broadcast_to([P, TT, D]), ALU.mult).then_inc(row_used, 1)
                dve.wait_ge(row_used, n + 1)

            def evacuate_scaled(name, dst, scale, shift):
                for k in (1, 3):
                    j = JOB[name] + k
                    is_filled(dve, j)
                    for m in range(2):
                        c = 2 * k + m
                        b = bank(j)[:, m * T:m * T + T]
                        if shift:
                            last = v.tensor_scalar(dst[:, c, :], b, scale(c), shift(c), ALU.mult, ALU.add)
                        else:
                            last = v.tensor_scalar(dst[:, c, :], b, scale(c), None, ALU.mult)
                    last.then_inc(emptied[j % 4], 1)

            def evacuate(j, dst):
                is_filled(dve, j)
                v.tensor_copy(dst, bank(j)[:, :]).then_inc(emptied[j % 4], 1)

            def add_gated(name, rows, scratch):
                for k in range(4):
                    s = SUM[name] + k
                    sum_is_filled(dve, s)
                    at = (k % 2) * 512
                    v.tensor_tensor(scratch[:, k // 2, at:at + 512], sum_bank(s)[:, :], rows[:, at:at + 512],
                                    ALU.mult).then_inc(sum_emptied[s % 4], 1)
                for k in range(4):
                    sum_is_emptied(dve, SUM[name] + k)
                v.tensor_tensor(flat(res[:]), flat(res[:]), flat(scratch), ALU.add).then_inc(res_ready, 1)

            def products(n, base, used, factor):
                def one(k, pair, done):
                    dve.wait_ge(hid_raw[k], done + base + 1)
                    dve.wait_ge(hid_used[k], done + (used[k] + 1))
                    v.tensor_tensor(hidden[:, 2 + k, :], hidden[:, k, :], factor(k, pair), ALU.mult)\
                        .then_inc(hid_ready[k], 1)

                with dve.Fori(0, n // 2) as i:
                    one(0, 2 * i, i)
                    one(1, 2 * i + 1, i)

            dve.wait_ge(small_loaded, 32)
            dve.wait_ge(x_loaded, 16)
            norm(0, res, hat)
            dve.wait_ge(ctx_loaded, 16)
            norm(1, ctx_nat, ctx_nat)
            adaln(0)
            adaln(1)
            for z in range(2):
                last = v.scalar_tensor_tensor(scale_t[:, z, :], mod[:, 1, :, z], 1.0, colset("norm1_g"), ALU.add, ALU.mult)
            last.then_inc(scale_ready, 1)
            dve.wait_ge(scale_ready, 1)
            evacuate_scaled("x_t", act_t, lambda c: scale_t[:, 0, c:c + 1], lambda c: mod[:, 0, c, 0:1])
            evacuate_scaled("ctx_t", ctx_t, lambda c: scale_t[:, 1, c:c + 1], lambda c: mod[:, 0, c, 1:2])
            adaln(2)

            dve.wait_ge(bias_masked, 1)

            def na_max(k):
                h, t = (k // 4) * 2 + k % 2, (k // 2) % 2
                j = JOB["na", "s", k]
                is_filled(dve, j)
                link(v.tensor_tensor(bank(j)[:, 0:T], bank(j)[:, 0:T], bias[:, t, h, :], ALU.add))
                if k >= 3:
                    dve.wait_ge(na_norm, k - 2)
                v.tensor_reduce(na_stat[:, k % 3, 0:1], bank(j)[:, :], AX.X, ALU.max, negate=True)\
                    .then_inc(na_neg_ready, 1)

            def na_normalise(k):
                is_emptied(dve, JOB["na", "s", k])
                link(v.reciprocal(na_stat[:, k % 3, 2:3], na_stat[:, k % 3, 1:2]))
                v.tensor_scalar(na_p[:, k % 3, :], na_p[:, k % 3, :], na_stat[:, k % 3, 2:3], None, ALU.mult)\
                    .then_inc(na_norm, 1)

            for k in range(N_NA + 1):
                if k < N_NA:
                    na_max(k)
                if k:
                    na_normalise(k - 1)
            for k in range(2):
                is_emptied(dve, JOB["gate1"] + k)
            add_gated("w_out", gate_row, hat)
            adaln(3)
            adaln(4)
            v.scalar_tensor_tensor(scale_t[:, 2, :], mod[:, 4, :, 0], 1.0, colset("norm2_g"), ALU.add, ALU.mult)\
                .then_inc(scale_ready, 1)
            dve.wait_ge(scale_ready, 2)
            norm(2, res, hat)
            evacuate_scaled("h2_t", act_t, lambda c: scale_t[:, 2, c:c + 1], lambda c: mod[:, 3, c, 0:1])

            u32 = lambda ap: ap.bitcast(U32)

            def top16(values, left, n, width, best_of, index_of):
                one = lambda ap, k, w: ap[:, k * w:k * w + w]
                half = lambda ap, k, z: ap[:, k * TOPK + 8 * z:k * TOPK + 8 * z + 8]
                for k in range(n):
                    last = v.max(half(best_of, k, 0), one(values, k, width))
                link(last)
                for k in range(n):
                    v.max_index(u32(half(index_of, k, 0)), half(best_of, k, 0), one(values, k, width))
                    last = v.match_replace(one(left, k, width), half(best_of, k, 0), one(values, k, width), -3.0e38)
                link(last)
                for k in range(n):
                    last = v.max(half(best_of, k, 1), one(left, k, width))
                link(last)
                for k in range(n):
                    last = v.max_index(u32(half(index_of, k, 1)), half(best_of, k, 1), one(left, k, width))
                link(last)

            for t in range(TT):
                for k in range(4):
                    is_emptied(dve, JOB["key"] + 4 * t + k)
                top16(score[:, t, :], rest, HP, NKEYS, top[:, t, :], top_i)
                link(v.tensor_copy(top_if[:, t, :], u32(top_i)))
                tv = top[:, t, :].rearrange("p (h z k) -> p h z k", z=2, k=TOPK)
                wide = [P, PEER_H, TOPK, TOPK]
                link(v.tensor_tensor(cand.rearrange("p (h a b) -> p h a b", h=PEER_H, a=TOPK),
                                     tv[:, :, 0, :].unsqueeze(3).broadcast_to(wide),
                                     tv[:, :, 1, :].unsqueeze(2).broadcast_to(wide), ALU.add))
                top16(cand, cand_rest, PEER_H, TOPK * TOPK, best[:, t, :], best_i)
                if t:
                    is_filled(dve, JOB["hk"])
                for z in range(2):
                    op, by = (ALU.logical_shift_right, 4) if z == 0 else (ALU.bitwise_and, 15)
                    link(v.tensor_scalar(u32(part_a), u32(best_i), by, None, op))
                    link(v.tensor_copy(part_af, u32(part_a)))
                    pick3 = pick.rearrange("p (q a) -> p q a", a=TOPK)
                    link(v.tensor_tensor(pick3, part_af.unsqueeze(2).broadcast_to([P, P, TOPK]),
                                         iota[:, 0:TOPK].unsqueeze(1).broadcast_to([P, P, TOPK]), ALU.is_equal))
                    ti = top_if[:, t, :].rearrange("p (h z k) -> p h z k", z=2, k=TOPK)
                    pick4 = pick.rearrange("p (h k a) -> p h k a", h=PEER_H, k=TOPK)
                    link(v.tensor_tensor(pick4, pick4, ti[:, :, z, :].unsqueeze(2).broadcast_to(wide), ALU.mult))
                    link(v.tensor_reduce(chosen[:, z, :], pick3, AX.X, ALU.add))
                bt = best[:, t, :].rearrange("p (h k) -> p h k", h=PEER_H)
                ct = chosen[:, 2, :].rearrange("p (h k) -> p h k", h=PEER_H)
                rows8 = [P, PEER_H, TOPK]
                v.tensor_tensor(ct, bt, bt[:, :, 0:1].broadcast_to(rows8), ALU.subtract).then_inc(soft_ready, 1)
                dve.wait_ge(soft_exp, t + 1)
                link(v.tensor_reduce(soft[:, 0, :], ct, AX.X, ALU.add))
                link(v.reciprocal(soft[:, 1, :], soft[:, 0, :]))
                v.tensor_tensor(ct, ct, soft[:, 1, :].unsqueeze(2).broadcast_to(rows8), ALU.mult)\
                    .then_inc(chosen_ready, 1)
            for t in range(TT):
                is_emptied(dve, JOB["hk"] + t)
            with dve.Fori(0, T // 8) as i:
                for half in range(2):
                    dve.wait_ge(tokens_filled[half], i + 1)
                    for m in range(4):
                        n = 4 * half + m
                        at = bass.ds(i * 8 + n, 1)
                        v.tensor_scalar(onehot[:, n * P:n * P + P], iota, hk_t[:, 0, at], None, ALU.is_equal)
                        last = v.tensor_scalar(onehot[:, D + n * P:D + n * P + P], iota, hk_t[:, 1, at], hk_t[:, 2, at],
                                               ALU.is_equal, ALU.mult)
                    last.then_inc(onehot_ready[half], 1)
            for half in range(2):
                dve.wait_ge(tokens_placed[half], T // 8 + 1)
            products(64, 0, (0, 0), lambda k, pair: dense[:, bass.ds(pair * 2, 2), :])
            adaln(5)
            for k in range(2):
                is_emptied(dve, JOB["gate2"] + k)
            add_gated("peer", gate_row2, hat3)
            dve.wait_ge(res_ready, 2)
            norm(3, res, hat3)
            dve.wait_ge(hat_ready, 4)
            times_row(0, hat3)
            v.tensor_copy(flat(res[:]), flat(hat3)).then_inc(res_ready, 1)
            dve.wait_ge(res_ready, 3)

            norm(4, res, hat3)
            evacuate_scaled("u_t", act_t, lambda c: col("pre_mix", c), None)
            lg = colset("lb_logits")
            link(v.tensor_tensor(lbt[:, 0, :], lg[:, 0:8], lg[:, 8:16], ALU.max))
            v.tensor_tensor(lbt[:, 1, :], lg[:, 0:8], lbt[:, 0, :], ALU.subtract)
            v.tensor_tensor(lbt[:, 2, :], lg[:, 8:16], lbt[:, 0, :], ALU.subtract).then_inc(lb_ready, 1)
            dve.wait_ge(lb_ready, 2)
            link(v.tensor_tensor(lbt[:, 3, :], lbt[:, 1, :], lbt[:, 2, :], ALU.add))
            link(v.reciprocal(lbt[:, 0, :], lbt[:, 3, :]))
            link(v.tensor_tensor(lbt[:, 4, :], lbt[:, 1, :], lbt[:, 0, :], ALU.mult))
            link(v.tensor_scalar(lbt[:, 5, :], lbt[:, 4, :], -1.0, 1.0, ALU.mult, ALU.add))
            hq, hk = hqf[:, 0:8, :], hqf[:, 8:16, :]
            for k in range(8):
                is_emptied(dve, JOB["hq_hf"] + k)
            link(v.tensor_scalar(flat(hq), flat(hq), P ** -0.5, None, ALU.mult))
            for h in range(HG_H):
                last = v.tensor_scalar(hk[:, h, :], hk[:, h, :], lbt[:, 5, h:h + 1], lbt[:, 4, h:h + 1],
                                       ALU.mult, ALU.add)
            last.then_inc(hg_pre, 1)
            dve.wait_ge(hg_pre, 1)
            dve.wait_ge(hg_log, 1)
            link(v.tensor_scalar(flat(hk), flat(hk), -1.0, 1.0, ALU.mult, ALU.add))
            dve.wait_ge(const2_loaded, 64)
            for h in range(HG_H):
                last = v.tensor_tensor_scan(cum[:, h, :], const("scan_keep"), logf[:, h, :], 0.0, ALU.mult, ALU.add)
            link(last)
            link(v.memset(ad_t, 0.0))
            masks = const("level_mask").rearrange("p (l t) -> p l t", l=LEVELS).bitcast(I32)
            cum_flat = flat(cum)

            def level_exponent(n):
                x = flat(level_x[n % 2])
                if n >= 2:
                    is_filled(dve, JOB["level"] + 4 * (n - 2) + 3)
                if n < 7:
                    half = 1 << n
                    cv = cum_flat.rearrange("p (b z w) -> p b z w", z=2, w=half)
                    xv = x.rearrange("p (b z w) -> p b z w", z=2, w=half)
                    shape = [P, T * HG_H // (2 * half), half]
                    edge = cv[:, :, 0, half - 1:half].broadcast_to(shape)
                    v.tensor_tensor(xv[:, :, 0, :], edge, cv[:, :, 0, :], ALU.subtract)
                    if n < 6:
                        v.tensor_tensor(xv[:, :, 1, :], cv[:, :, 1, :], edge, ALU.subtract).then_inc(level_arg, 1)
                    else:
                        v.tensor_copy(xv[:, :, 1, :], cv[:, :, 1, :]).then_inc(level_arg, 1)
                    return
                cv = cum_flat.rearrange("p (h q w) -> p h q w", h=HG_H, q=4)
                xv = x.rearrange("p (h q w) -> p h q w", h=HG_H, q=4)
                shape = [P, HG_H, 64]
                total = [cv[:, :, q, 63:64].broadcast_to(shape) for q in range(4)]
                link(v.tensor_tensor(xv[:, :, 0, :], total[0], cv[:, :, 0, :], ALU.subtract))
                v.tensor_tensor(xv[:, :, 0, :], xv[:, :, 0, :], total[1], ALU.add)
                v.tensor_tensor(xv[:, :, 1, :], total[1], cv[:, :, 1, :], ALU.subtract)
                v.tensor_copy(xv[:, :, 2, :], cv[:, :, 2, :])
                v.tensor_tensor(xv[:, :, 3, :], cv[:, :, 3, :], total[2], ALU.add).then_inc(level_arg, 1)

            def level_scale(n):
                half = 1 << n
                dve.wait_ge(level_exp, n + 1)
                if n == 7:
                    xv = level_x[1].rearrange("p h (z w) -> p h z w", z=2)
                    kv_, qv = (a.rearrange("p h (z w) -> p h z w", z=2) for a in (hk, hq))
                else:
                    xv = flat(level_x[n % 2]).rearrange("p (b z w) -> p b z w", z=2, w=half)
                    kv_, qv = (flat(a).rearrange("p (b z w) -> p b z w", z=2, w=half) for a in (hk, hq))
                v.tensor_tensor(xv[:, :, 0, :], xv[:, :, 0, :], kv_[:, :, 0, :], ALU.mult)
                v.tensor_tensor(xv[:, :, 1, :], xv[:, :, 1, :], qv[:, :, 1, :], ALU.mult).then_inc(level_ready, 1)

            def level_take(n):
                for k in range(4):
                    j = JOB["level"] + 4 * n + k
                    t, g = k // 2, k % 2
                    mask = masks[:, n, :] if n < 7 else ident.bitcast(I32)
                    is_filled(dve, j)
                    v.copy_predicated(ad_t[:, t, 4 * g:4 * g + 4, :], mask.unsqueeze(1).broadcast_to([P, 4, P]),
                                      bank(j)[:, :].rearrange("p (h t) -> p h t", h=4)).then_inc(emptied[j % 4], 1)

            for n in range(8):
                level_exponent(n)
                if n:
                    level_take(n - 1)
                level_scale(n)
            level_take(7)
            for g in range(2):
                j = JOB["level"] + 32 + g
                evacuate(j, flat(ax_t[:, 4 * g:4 * g + 4, :]))
            for k in range(4):
                is_emptied(dve, JOB["o"] + k)
            o3 = lambda ap: flat(ap).rearrange("p (a b) -> p a b", b=P)
            link(v.tensor_tensor(flat(o_sq), flat(o_nat), flat(o_nat), ALU.mult))
            link(v.tensor_reduce(ostat[:, 0, :], o3(o_sq), AX.X, ALU.add))
            v.tensor_scalar(ostat[:, 1, :], ostat[:, 0, :], 1.0 / P, EPS, ALU.mult, ALU.add).then_inc(ovar, 1)
            dve.wait_ge(oroot, 1)
            link(v.reciprocal(ostat[:, 3, :], ostat[:, 2, :]))
            link(v.tensor_tensor(o3(o_nat), o3(o_nat), ostat[:, 3, :].unsqueeze(2).broadcast_to([P, 16, P]), ALU.mult))
            link(v.tensor_tensor(o3(o_nat), o3(o_nat), gnorm.unsqueeze(1).broadcast_to([P, 16, P]), ALU.mult))
            for t in range(TT):
                ov = o_nat[:, t, :].rearrange("p (u n) -> p u n", n=256)
                last = v.tensor_tensor(ov, ov, hig[:, 4:8, t * 256:t * 256 + 256], ALU.mult)
            last.then_inc(ya_ready, 1)
            for k in (1, 3):
                evacuate(JOB["ya_t"] + k, flat(ya_t[:, 2 * k:2 * k + 2, :]))

            two = [P, 2, T]
            cos, sin = (const(n).unsqueeze(1).broadcast_to(two) for n in ("rope_cos", "rope_sin"))
            for k in range(6):
                j = JOB["rope"] + k
                at = 2 * k if k < 4 else 12 + 2 * (k - 4)
                dst = q_rot[:, at:at + 2, :] if k < 4 else k_rot[:, at - 12:at - 10, :]
                tmp = rope_tmp.rearrange("p (a b) -> p a b", a=2)
                is_filled(dve, j)
                v.tensor_tensor(tmp, bank(j)[:, :].rearrange("p (a b) -> p a b", a=2), sin, ALU.mult)\
                    .then_inc(emptied[j % 4], 1)
                link(v.tensor_tensor(dst, nsa_t[:, at:at + 2, :], cos, ALU.mult))
                link(v.tensor_tensor(dst, dst, tmp, ALU.add))
            kb = k_both.rearrange("p (q a) t -> p q a t", a=2)
            for half in range(2):
                for a in range(2):
                    last = v.tensor_copy(kb[half * DH:half * DH + DH, :, a, :], k_rot[a * DH:a * DH + DH, :, :])
            last.then_inc(rot_ready, 1)
            dve.wait_ge(nsa_small_loaded, 32)
            for kv in range(2):
                dve.wait_ge(cmp_copied, kv + 1)
                ci = cmp_in[:, kv, :].rearrange("p (l n) -> p l n", l=16)
                v.tensor_tensor(ci, ci, pe_cols[:, kv, :].unsqueeze(2).broadcast_to([P, 16, 60]), ALU.add)\
                    .then_inc(cmp_in_ready, 1)
            dve.wait_ge(vb_zero, 3)
            is_emptied(dve, JOB["gates"])
            for t in range(TT):
                j = JOB["cmp_s"] + t
                wide = [P, NSA_H, CMP]
                s = cmp_s[:, t, :].rearrange("p (h n) -> p h n", h=NSA_H)
                add = const("cmp_add")[:, t * CMP:t * CMP + CMP].unsqueeze(1).broadcast_to(wide)
                keep = const("cmp_keep")[:, t * CMP:t * CMP + CMP].unsqueeze(1).broadcast_to(wide)
                st = [cmp_stat[:, t, k * NSA_H:k * NSA_H + NSA_H] for k in range(4)]
                is_filled(dve, j)
                v.tensor_tensor(s, bank(j)[:, 0:NSA_H * CMP].rearrange("p (h n) -> p h n", h=NSA_H), add, ALU.add)\
                    .then_inc(emptied[j % 4], 1)
                is_emptied(dve, j)
                link(v.tensor_reduce(st[0], s, AX.X, ALU.max, negate=True))
                v.tensor_tensor(s, s, st[0].unsqueeze(2).broadcast_to(wide), ALU.add).then_inc(cmp_arg, 1)
                dve.wait_ge(cmp_exp, t + 1)
                link(v.tensor_reduce(st[1], s, AX.X, ALU.add))
                link(v.reciprocal(st[2], st[1]))
                link(v.tensor_tensor(st[3], st[2], gates[:, t, 0:NSA_H], ALU.mult))
                link(v.tensor_tensor(s, s, keep, ALU.mult))
                v.tensor_tensor(cmp_p[:, t, :].rearrange("p (h n) -> p h n", h=NSA_H)[:, :, 0:CMP], s,
                                st[3].unsqueeze(2).broadcast_to(wide), ALU.mult).then_inc(cmp_ready, 1)

            def at_max(k):
                c, t, h = AT_ITEMS[k]
                width = P * (t + 1)
                j = JOB["at", "s", k]
                is_filled(dve, j)
                b = bank(j)[:, 0:2 * width].rearrange("p (s w) -> p s w", s=2)
                diag = b[:, :, width - P:width]
                link(v.tensor_tensor(diag, diag, const("causal").unsqueeze(1).broadcast_to([P, 2, P]), ALU.add))
                v.tensor_reduce(at_stat[:, k % 3, 0:2], b, AX.X, ALU.max, negate=True).then_inc(at_neg, 1)

            def at_normalise(k):
                c, t, h = AT_ITEMS[k]
                width = P * (t + 1)
                is_emptied(dve, JOB["at", "s", k])
                st = at_stat[:, k % 3, :]
                link(v.reciprocal(st[:, 4:6], st[:, 2:4]))
                link(v.tensor_tensor(st[:, 6:8], st[:, 4:6], gates[:, t, NSA_H + h::NSA_H], ALU.mult))
                for m in range(2):
                    pv = at_p[:, k % 3, m * width:m * width + width]
                    last = v.tensor_scalar(pv, pv, st[:, 6 + m:7 + m], None, ALU.mult)
                last.then_inc(at_norm, 1)

            for k in range(N_AT + 1):
                if k < N_AT:
                    at_max(k)
                if k:
                    at_normalise(k - 1)
            for n, name in enumerate(("branch_a", "branch_b")):
                dst = (merged, side)[n]
                for k in range(4):
                    s = SUM[name] + k
                    t, half = k // 2, k % 2
                    sum_is_filled(dve, s)
                    v.tensor_tensor(dst[:, t, half * 512:half * 512 + 512].rearrange("p (u n) -> p u n", u=2),
                                    sum_bank(s)[:, :].rearrange("p (u n) -> p u n", u=2),
                                    gab[:, 4 * n + 2 * half:4 * n + 2 * half + 2, t * 256:t * 256 + 256], ALU.mult)\
                        .then_inc(sum_emptied[s % 4], 1)
            for k in range(4):
                sum_is_emptied(dve, SUM["branch_b"] + k)
            v.tensor_tensor(flat(merged), flat(merged), flat(side), ALU.add).then_inc(merged_ready, 1)
            for k in (1, 3):
                evacuate(JOB["m_t"] + k, flat(act_t[:, 2 * k:2 * k + 2, :]))

            def add_normed(n, src, r):
                norm(n, src, hat2)
                dve.wait_ge(hat_ready, n + 1)
                times_row(r, hat2)
                v.tensor_tensor(flat(res[:]), flat(res[:]), flat(hat2), ALU.add).then_inc(res_ready, 1)
                dve.wait_ge(res_ready, 3 + r)

            add_normed(5, side, 1)
            norm(6, res, hat2)
            evacuate_scaled("v_t", act_t, lambda c: col("pre_mlp", c), None)
            products(16, 32, (32, 31), lambda k, pair: hidden[:, k, :])
            add_normed(7, side, 2)
            for k in (1, 3):
                evacuate(JOB["h_t"] + k, flat(act_t[:, 2 * k:2 * k + 2, :]))
            for k in range(4):
                sum_is_emptied(dve, SUM["ple"] + k)
                sum_is_emptied(dve, SUM["ple_gate"] + k)
            v.tensor_tensor(flat(merged), flat(merged), flat(side), ALU.mult).then_inc(merged_ready, 1)
            dve.wait_ge(merged_ready, 2)
            add_normed(8, merged, 3)


def column_units(w):
    return [w[:, n:n + 256].reshape(C, P, 256).transpose(1, 0, 2).reshape(P, UNIT) for n in range(0, w.shape[1], 256)]


def row_units_of(w):
    return [w[n:n + 256].reshape(2, P, D).transpose(1, 0, 2).reshape(P, UNIT) for n in range(0, w.shape[0], 256)]


def staggered(ups, downs):
    order = [ups[0], ups[1], downs[0]]
    for k in range(2, len(ups)):
        order += [ups[k], downs[k - 1]]
    return order + [downs[-1]]


def as_column(v):
    return v.reshape(-1, P).T


def kernel(**inputs):
    import numpy as _np
    import concourse.bacc as _bacc
    from concourse import mybir as _mybir
    from concourse.bass_utils import run_bass_kernel_spmd as _run

    a = {k: _np.asarray(v) for k, v in inputs.items()}
    first, second, band = constants()
    ada, w2 = a["ada_w"][0], a["w_in_2"][0]
    at = {"hq": 0, "hf": 1024, "hi": 2048, "hg": 3072, "nq": 4096, "kc": 5120, "vc": 5376, "ks": 5632,
          "vs": 5888, "kw": 6144, "vw": 6400, "gate": 6656, "ga": 6704, "gb": 7728}
    part = lambda name, n: w2[:, at[name]:at[name] + n]
    experts_u = a["peer_u"][0].reshape(P, NKEYS // 2, 2, D).transpose(1, 3, 2, 0)
    experts_v = a["peer_v"][0].reshape(P, NKEYS // 2, 2 * D).transpose(1, 0, 2)

    def compress_units(w):
        w = w.reshape(2, 16, DH, 256).transpose(0, 2, 1, 3).reshape(P, 16 * 256)
        return [w[:, :UNIT], w[:, UNIT:]]

    stages = {
        **{f"ada{v}": column_units(ada[:, v * D:v * D + D]) for v in range(6)},
        "w_in": column_units(a["w_in"][0]), "band": [band], "w_out": row_units_of(a["w_out"][0]),
        "wq": column_units(a["peer_wq"][0]),
        "keys": [a["peer_keys"][0].reshape(HP, NKEYS, P).transpose(2, 0, 1).reshape(P, UNIT)],
        "peer": staggered([column_units(u.reshape(D, 256))[0] for u in experts_u], list(experts_v)),
        "hq_hf": column_units(part("hq", 2048)), "hi_hg": column_units(part("hi", 2048)),
        "nsa_t": column_units(part("nq", 1024)) + [column_units(part(n, 256))[0] for n in ("kc", "vc", "ks", "kw")],
        "vs_vw": [column_units(part(n, 256))[0] for n in ("vs", "vw")],
        "ga_gb": column_units(part("ga", 2048)),
        "wk1": compress_units(a["cmp_wk1_2"][0]), "wv1": compress_units(a["cmp_wv1_2"][0]),
        "branch_a": row_units_of(a["w_branch_a_2"][0]), "branch_b": row_units_of(a["w_branch_b_2"][0]),
        "w_out2": row_units_of(a["w_out_2"][0]),
        "mlp": staggered(column_units(a["w_up_2"][0]), row_units_of(a["w_down_2"][0])),
        "ple": row_units_of(a["w_ple_2"][0]), "ple_gate": row_units_of(a["w_ple_gate_2"][0]),
    }
    weights = _np.empty((N_UNITS, P, UNIT), _np.float32)
    for name, first_unit in UNITS.items():
        for k, u in enumerate(stages[name]):
            weights[first_unit + k] = u
    small = {"ada_b": a["ada_b"], "norm1_g": a["norm1_g"], "norm2_g": a["norm2_g"], "c": a["c"], "c_ctx": a["c_ctx"],
             "pool_scale": a["pool_scale"], "pre_mix": a["norm_pre_mix_2"], "pre_mlp": a["norm_pre_mlp_2"],
             "lb_logits": a["hg_lb_logits_2"]}
    pe = _np.stack([a[n][0].reshape(2, 16, DH).transpose(0, 2, 1).reshape(P, 16) for n in ("cmp_pe_k_2", "cmp_pe_v_2")], 1)
    w2_in = _np.zeros((P, 2, 2, P), _np.float32)
    wk2 = a["cmp_wk2_2"][0].reshape(2, P, DH).transpose(1, 0, 2)
    w2_in[:, 0, :, :DH] = w2_in[:, 0, :, DH:] = wk2
    w2_in[:, 1].reshape(P, 2 * P)[:, :P] = a["cmp_wv2_2"][0].reshape(2, P, DH).transpose(1, 0, 2).reshape(P, P)
    padded = _np.zeros((NA_H, 7, 2 * GRID - 1), _np.float32)
    padded[:, :, GRID - KW:GRID + KW - 1] = a["na_rpb"][0][:, 4:11]
    shifted = _np.stack([padded[:, :, GRID - 1 - w:2 * GRID - 1 - w] for w in range(GRID)])
    data = {
        "weights": weights, "x": a["x"][0], "ctx_in": a["ctx"][0],
        "cols_in": _np.concatenate([as_column(small[n]) for n in COLS], 1),
        "rows_in": _np.stack([a["final_g"], a["norm_post_mix_2"][0], a["norm_post_mlp_2"][0], a["norm_ple_2"].reshape(-1)]),
        "gnorm_in": a["hg_gnorm_2"], "const1": first, "const2": second, "rpb": shifted,
        "pool_w": a["pool_w"][0].transpose(1, 0, 2), "gate_w": part("gate", 48).reshape(C, P, 48).transpose(1, 0, 2),
        "pe_t": pe, "w2_in": w2_in.reshape(P, 4 * P),
        "p_t": a["p_2"][0, 0].T.reshape(2, P, T).transpose(1, 0, 2),
    }
    nc = _bacc.Bacc("TRN2", target_bir_lowering=False, num_devices=1)
    arrays, args = {}, {}
    for name, v in data.items():
        v = _np.ascontiguousarray(v)
        arrays[f"in_{name}"] = v
        args[name] = nc.dram_tensor(f"in_{name}", v.shape, _mybir.dt.from_np(v.dtype), kind="ExternalInput").ap()
    args["out"] = nc.dram_tensor("out_0", (T, D), F32, kind="ExternalOutput").ap()
    build(nc, **args)
    r = _run(nc, [arrays], core_ids=[0])
    return r.results[0]["out_0"].reshape(1, T, D)
```

```python
from contextlib import ExitStack
import math

import numpy as np
import concourse.bass as bass
from concourse import mybir

P = 128
T = 256
TT = T // P
D = 1024
C = D // P
RING = 4
UNIT = 2048
GRID = 64
KW = 16
NA_H = 8
DH = 64
HP = 16
TOPK = 16
PEER_H = 8
NKEYS = 128
EARLY = 14
CMP = (T - 32) // 16 + 1
HG_H = 8
NSA_H = 16
NSA_G = 4
EPS = 1e-6
NEG = -1e30
LEVELS = 7

F32 = mybir.dt.float32
U32 = mybir.dt.uint32
I32 = mybir.dt.int32
ALU = mybir.AluOpType
ACT = mybir.ActivationFunctionType
AX = mybir.AxisListType

UNITS = {}
_n = 0
for _name, _count in (("ada0", 4), ("ada1", 4), ("w_in", 24), ("band", 1), ("w_out", 4),
                      ("wq", 8), ("u_first", EARLY), ("v_first0", EARLY), ("v_first1", EARLY),
                      ("peer", 2 * (NKEYS // 2 - EARLY)),
                      ("hq_hf", 8), ("hi_hg", 8), ("nsa_t", 8), ("vs_vw", 2), ("ga", 4), ("branch_a", 4),
                      ("wk1", 2), ("wv1", 2), ("gb", 4), ("branch_b", 4), ("w_out2", 4),
                      ("ple", 1), ("mlp", 32), ("ple_gate", 4)):
    UNITS[_name] = _n
    _n += _count
N_UNITS = _n


def w_in_unit(k):
    return UNITS["w_in"] + 3 * k


def ada_unit(v, k):
    if v < 2:
        return UNITS[f"ada{v}"] + k
    n = 4 * (v - 2) + k
    return UNITS["w_in"] + 3 * (n // 2) + 1 + n % 2


COLS = {}
_n = 0
for _name, _count in (("ada_b", 48), ("norm1_g", 8), ("norm2_g", 8), ("c", 8), ("c_ctx", 8),
                      ("pool_scale", 4), ("pre_mix", 8), ("pre_mlp", 8), ("lb_logits", 16)):
    COLS[_name] = (_n, _count)
    _n += _count
N_COLS = _n
ROWS = {"final_g": 0, "post_mix": 1, "post_mlp": 2, "ple": 3}

CONST2 = {}
_n = 0
for _name, _count in (("causal", P), ("cmp_add", 2 * CMP), ("cmp_keep", 2 * CMP), ("rope_cos", T),
                      ("rope_sin", T), ("rope_swap", P), ("level_mask", LEVELS * P), ("scan_keep", T)):
    CONST2[_name] = (_n, _count)
    _n += _count
N_CONST2 = _n


def constants():
    first = np.zeros((P, 2 * P + GRID), np.float32)
    first[:, :P] = np.eye(P)
    first[:, P:2 * P] = np.arange(P)
    col = np.arange(GRID)
    c0 = np.clip(col - KW // 2, 0, GRID - KW)
    inside = (col[None, :] >= c0[:, None]) & (col[None, :] < c0[:, None] + KW)
    first[:, 2 * P:] = np.tile(np.where(inside, 0.0, NEG), (2, 1))

    second = np.zeros((P, N_CONST2), np.float32)

    def put(name, a):
        at, n = CONST2[name]
        second[:, at:at + n] = a.reshape(P, n)

    q = np.arange(P)
    put("causal", np.where(q[None, :] <= q[:, None], 0.0, NEG))
    end = np.arange(CMP) * 16 + 31
    seen = end[None, None, :] <= (q[:, None, None] + P * np.arange(TT)[None, :, None])
    put("cmp_add", np.where(seen, 0.0, NEG))
    put("cmp_keep", seen.astype(np.float32))
    inv = (500000.0 ** (-np.arange(8) * 2.0 / 16)).astype(np.float32)
    ang = np.arange(T, dtype=np.float32)[:, None] * inv[None, :]
    cos, sin = np.cos(ang), np.sin(ang)
    rc, rs, swap = np.ones((P, T)), np.zeros((P, T)), np.zeros((P, P))
    for base in (0, 64):
        for d in range(8):
            rc[base + d], rc[base + 8 + d] = cos[:, d], cos[:, d]
            rs[base + d], rs[base + 8 + d] = -sin[:, d], sin[:, d]
            swap[base + 8 + d, base + d] = swap[base + d, base + 8 + d] = 1.0
    put("rope_cos", rc)
    put("rope_sin", rs)
    put("rope_swap", swap)
    masks = np.zeros((P, LEVELS, P), np.float32)
    for level in range(LEVELS):
        half = 1 << level
        same = (q[:, None] // (2 * half)) == (q[None, :] // (2 * half))
        masks[:, level] = same & (q[:, None] % (2 * half) < half) & (q[None, :] % (2 * half) >= half)
    put("level_mask", masks)
    put("scan_keep", np.tile((np.arange(T) % 64 != 0).astype(np.float32), (P, 1)))

    band = np.zeros((4, T, T), np.float32)
    t = np.arange(T)
    for g, w in enumerate((2, 4, 8, 16)):
        lo, hi = np.clip(t - w // 2, 0, T), np.clip(t + w // 2, 0, T)
        in_win = (t[:, None] >= lo[None, :]) & (t[:, None] < hi[None, :])
        band[g] = np.where(in_win, 1.0 / (hi - lo)[None, :], 0.0) - np.eye(T)
    band = band.reshape(4, TT, P, T).transpose(2, 1, 0, 3).reshape(P, UNIT)
    return first, second, np.ascontiguousarray(band.astype(np.float32))


def build(nc, weights, x, ctx_in, cols_in, rows_in, gnorm_in, const1, const2, rpb, pool_w, keys_in, gate_w,
          pe_t, w2_in, p_t, out):
    with ExitStack() as stack:
        def sb(name, shape, dt=F32):
            return stack.enter_context(nc.sbuf_tensor(name, shape, dt))

        def sem(name):
            return stack.enter_context(nc.semaphore(name))

        ring = [sb(f"ring{s}", [P, UNIT]) for s in range(RING)]
        res = sb("res", [P, TT, D])
        act_t = sb("act_t", [P, C, T])
        cols = sb("cols", [P, N_COLS])
        c1 = sb("c1", [P, 2 * P + GRID])
        mod = sb("mod", [P, 6, C, 2])
        scale_t = sb("scale_t", [P, 3, C])
        eps = sb("eps", [P, 2])
        silu_c = sb("silu_c", [P, C, 2])
        stat = sb("stat", [P, 9, 3, TT])
        hk_t = sb("hk_t", [P, 3, T])
        early_gates = sb("early_gates", [P, 4, 2, 2 * EARLY])
        hidden = sb("hidden", [P, 4, 512])
        ident = c1[:, 0:P]
        iota = c1[:, P:2 * P]
        win_mask = c1[:, 2 * P:]

        ARENA = 32850
        arena = sb("arena", [P, ARENA])

        class Area:
            def __init__(self, at):
                self.at = at

            def take(self, *shape):
                n = math.prod(shape)
                ap = arena[:, self.at:self.at + n]
                self.at += n
                assert self.at <= ARENA, self.at
                if len(shape) == 2:
                    return ap.rearrange("p (a b) -> p a b", a=shape[0])
                if len(shape) == 3:
                    return ap.rearrange("p (a b c) -> p a b c", a=shape[0], b=shape[1])
                return ap

        a1 = Area(0)
        hat = a1.take(TT, D)
        ctx_nat = a1.take(TT, D)
        ctx_t = a1.take(C, T)
        px = a1.take(2, TT, 256)
        qx_t = a1.take(4, T)
        kx_t = a1.take(4, T)
        kc_t = a1.take(4, T)
        vx = a1.take(2, TT, 256)
        vc = a1.take(2, TT, 256)
        pooled_t = a1.take(4, T)
        mix_t = a1.take(C, T)
        bias = a1.take(TT, NA_H, T)
        na_p = a1.take(3, 512)
        na_pt = a1.take(4, 512)
        na_stat = a1.take(3, 3)
        gate_row = a1.take(D)
        poolw = a1.take(4, P)
        weighted = a1.take(4, 256)
        ones = a1.take(1)

        a2 = Area(2048)
        pq_t = a2.take(HP, T)
        score = a2.take(TT, HP * NKEYS)
        rest = a2.take(HP * NKEYS)
        top = a2.take(TT, HP * TOPK)
        top_i = a2.take(TT, HP * TOPK)
        top_if = a2.take(TT, HP * TOPK)
        cand = a2.take(UNIT)
        cand_rest = a2.take(UNIT)
        best = a2.take(TT, P)
        best_i = a2.take(P)
        part_a = a2.take(P)
        part_af = a2.take(P)
        pick = a2.take(UNIT)
        chosen = a2.take(3, P)
        soft = a2.take(4, PEER_H)
        a2_end = a2.at
        a3 = Area(0)
        dense = a3.take(NKEYS, T)
        LATE = NKEYS - 2 * EARLY
        assert EARLY % 2 == 0 and EARLY < T // 16
        early = dense[:, NKEYS - 2 * EARLY:, :]
        keys = arena[:, NKEYS * T - HP * NKEYS:NKEYS * T]
        assert a2_end <= (NKEYS - 2 * EARLY) * T
        onehot = hidden.rearrange("p a b -> p (a b)")
        junk = onehot.rearrange("p (t d) -> p t d", t=TT)
        gate_row2 = act_t.rearrange("p c t -> p (c t)")[:, 0:D]

        a4 = Area(0)
        c2 = a4.take(N_CONST2)
        gnorm = a4.take(P)
        row = a4.take(D)
        hqf = a4.take(16, T)
        hig = a4.take(8, 512)
        nsa_t = a4.take(16, T)
        vsw = a4.take(2, 512)
        gab = a4.take(8, 512)
        gates = a4.take(TT, 48)
        pt = a4.take(2, T)
        gw = a4.take(C, 48)
        reuse = a4.at
        a5 = Area(reuse)
        logf = a5.take(HG_H, T)
        cum = a5.take(HG_H, T)
        level_x = [a5.take(HG_H, T), a5.take(HG_H, T)]
        ad_t = a5.take(TT, HG_H, P)
        ax_t = a5.take(HG_H, P)
        o_nat = logf.rearrange("p h t -> p (h t)").rearrange("p (a b) -> p a b", a=TT)
        o_sq = cum.rearrange("p h t -> p (h t)").rearrange("p (a b) -> p a b", a=TT)
        hat3 = logf.rearrange("p h t -> p (h t)").rearrange("p (a b) -> p a b", a=TT)
        lbt = sb("lbt", [P, 6, C])
        ostat = sb("ostat", [P, 4, 16])
        ya_t = hqf[:, 0:8, :]
        yb_t = ya_t
        a6 = Area(reuse)
        q_rot = hqf[:, 8:16, :]
        rope_tmp = a6.take(512)
        k_rot = a6.take(4, T)
        k_both = a6.take(2 * NSA_G, T)
        cmp_in = a6.take(2, 16 * 60)
        cmp_hid = a6.take(4, 60)
        kcmp_t = a6.take(NSA_G, 2, CMP)
        vb = a6.take(NSA_G * 2 * P)
        cmp_s = a6.take(TT, NSA_H * CMP)
        cmp_p = a6.take(TT, NSA_H * 32)
        cmp_pt = a6.take(TT, 512)
        cmp_stat = a6.take(TT, 4 * NSA_H)
        pe_cols = a6.take(2, 16)
        w2 = a6.take(2, 2 * P)
        hig_flat = hig.rearrange("p a b -> p (a b)")
        at_p = hig_flat[:, 0:1536].rearrange("p (a b) -> p a b", a=3)
        at_pt = hig_flat[:, 1536:3584].rearrange("p (a b) -> p a b", a=4)
        at_stat = hig_flat[:, 3584:3632].rearrange("p (a b) -> p a b", a=3)
        a8 = Area(reuse)
        merged = a8.take(TT, D)
        side = a8.take(TT, D)
        hat2 = a8.take(TT, D)

        psum = [stack.enter_context(nc.psum_tensor(f"bank{b}", [P, 512], F32)) for b in range(8)]

        loaded = [sem(f"unit_loaded{s}") for s in range(RING)]
        passed = [sem(f"unit_passed{s}") for s in range(RING)]
        filled = [sem(f"bank_filled{b}") for b in range(4)]
        emptied = [sem(f"bank_emptied{b}") for b in range(4)]
        sum_filled = [sem(f"sum_filled{b}") for b in range(4)]
        sum_emptied = [sem(f"sum_emptied{b}") for b in range(4)]
        cols_loaded = sem("cols_loaded")
        c1_loaded = sem("c1_loaded")
        x_loaded = sem("x_loaded")
        ctx_loaded = sem("ctx_loaded")
        bias_loaded = sem("bias_loaded")
        bias_masked = sem("bias_masked")
        poolw_loaded = sem("poolw_loaded")
        keys_loaded = sem("keys_loaded")
        const2_loaded = sem("const2_loaded")
        nsa_small_loaded = sem("nsa_small_loaded")
        row_loaded = sem("row_loaded")
        silu_ready = sem("silu_ready")
        weighted_ready = sem("weighted_ready")
        weighted_used = sem("weighted_used")
        ones_ready = sem("ones_ready")
        scale_ready = sem("scale_ready")
        squares = sem("squares")
        root = sem("root")
        eps_ready = sem("eps_ready")
        hat_ready = sem("hat_ready")
        res_ready = sem("res_ready")
        dve_chain = sem("dve_chain")
        onehot_ready = [sem(f"onehot_ready{h}") for h in range(4)]
        early_ready = [sem(f"early_ready{h}") for h in range(4)]
        tokens_filled = [sem(f"tokens_filled{h}") for h in range(4)]
        tokens_placed = [sem(f"tokens_placed{h}") for h in range(4)]
        hid_filled = [sem(f"hid_filled{h}") for h in range(2)]
        hid_raw = [sem(f"hid_raw{h}") for h in range(2)]
        hid_ready = [sem(f"hid_ready{h}") for h in range(2)]
        hid_used = [sem(f"hid_used{h}") for h in range(2)]
        na_neg_ready = sem("na_neg_ready")
        na_norm = sem("na_norm")
        chosen_ready = sem("chosen_ready")
        soft_ready = sem("soft_ready")
        soft_exp = sem("soft_exp")
        lb_ready = sem("lb_ready")
        hg_pre = sem("hg_pre")
        hg_log = sem("hg_log")
        level_arg = sem("level_arg")
        level_exp = sem("level_exp")
        level_ready = sem("level_ready")
        ovar = sem("ovar")
        oroot = sem("oroot")
        ya_ready = sem("ya_ready")
        rot_ready = sem("rot_ready")
        cmp_copied = sem("cmp_copied")
        cmp_in_ready = sem("cmp_in_ready")
        cmp_arg = sem("cmp_arg")
        cmp_exp = sem("cmp_exp")
        cmp_ready = sem("cmp_ready")
        vb_zero = sem("vb_zero")
        at_neg = sem("at_neg")
        at_norm = sem("at_norm")
        merged_ready = sem("merged_ready")
        stored = sem("stored")

        JOB = {}
        SUM = {}
        count = {"job": 0, "sum": 0}

        def jobs(name, n):
            JOB[name] = count["job"]
            count["job"] += n

        def sums(name, n):
            SUM[name] = count["sum"]
            count["sum"] += n

        jobs("ada01", 1), jobs("x_t", 4), jobs("ctx_t", 4), jobs("w_in", 12)
        for v in range(2, 6):
            sums(f"ada{v}", 1)
        jobs("pool", 2), jobs("pool_y", 2), jobs("gate1", 2)
        NA_LAG_T, NA_LAG_V = 2, 3

        def attention_jobs(name, n, between=()):
            for k in range(n + NA_LAG_V):
                if k < n:
                    jobs((name, "s", k), 1)
                if 0 <= k - NA_LAG_T < n:
                    jobs((name, "t", k - NA_LAG_T), 1)
                if k in between:
                    jobs((name, "between", k), 1)

        N_NA = NA_H * TT
        attention_jobs("na", N_NA)
        sums("na", N_NA // 2)
        sums("w_out", 4)
        jobs("h2_t", 4)
        WQ_KEY = []
        for k in range(8):
            WQ_KEY.append(("wq", k))
            if k in (2, 4, 6, 7):
                part = sum(step[0] == "key" for step in WQ_KEY) // TT
                WQ_KEY += [("key", part, t) for t in range(TT)]
        for step in WQ_KEY:
            jobs(step, 1)
        for t in range(TT):
            jobs(("u_first", t), EARLY // 2), jobs(("hk", t), 1)
        sums("peer", 4)
        jobs("gate2", 2), jobs("u_t", 4)
        jobs("hq_hf", 8), jobs("hi_hg", 8)
        for n in range(8):
            jobs(("nsa_t", n), 1)
            jobs(("level", n), 4)
        jobs(("level", 8), 2)
        jobs("vs_vw", 2), jobs("gates", 1)
        jobs("o", 4), jobs("ga", 4), jobs("ya_t", 4), jobs("rope", 6)
        sums("branch_a", 4)
        jobs("cmp_hid", 4), jobs("cmp_out", 2), jobs("cmp_s", 2), jobs("cmp_t", 2)
        N_AT = NSA_H * TT
        GB_AT = (2, 12, 22, 31)
        attention_jobs("at", N_AT, GB_AT)
        sums("at", NSA_H // 2 * TT)
        sums("branch_b", 4)
        jobs("m_t", 4)
        sums("w_out2", 4)
        jobs("v_t", 4)
        sums("ple", 4), sums("mlp", 4)
        jobs("h_t", 4)
        sums("ple_gate", 4)

        def bank(j):
            return psum[j % 4]

        def is_filled(eng, j):
            eng.wait_ge(filled[j % 4], j // 4 + 1)

        def is_emptied(eng, j):
            eng.wait_ge(emptied[j % 4], j // 4 + 1)

        def sum_bank(j):
            return psum[4 + j % 4]

        def sum_is_filled(eng, j):
            eng.wait_ge(sum_filled[j % 4], j // 4 + 1)

        def sum_is_emptied(eng, j):
            eng.wait_ge(sum_emptied[j % 4], j // 4 + 1)

        def col(name, i=0):
            at = COLS[name][0] + i
            return cols[:, at:at + 1]

        def colset(name):
            at, n = COLS[name]
            return cols[:, at:at + n]

        def const(name):
            at, n = CONST2[name]
            return c2[:, at:at + n]

        ADA_ORDER = (1, 0, 3, 2, 5, 4, 6, 7)
        WEIGHED = (0, 2, 4)
        FIRST_WEIGHED = 2 * len(WEIGHED)
        AT_ITEMS = [(h // 2, t, h) for c in range(NSA_H // 2) for t in range(TT) for h in (2 * c, 2 * c + 1)]

        block = stack.enter_context(nc.Block())

        @block.sync
        def _(sp):
            sp.dma_start(cols[:], cols_in).then_inc(cols_loaded, 16)
            for s in range(2):
                sp.dma_start(ring[s][:], weights[s]).then_inc(loaded[s], 16)
            sp.dma_start(res[:], x.rearrange("(t p) d -> p t d", p=P)).then_inc(x_loaded, 16)
            for s in range(2, RING):
                sp.dma_start(ring[s][:], weights[s]).then_inc(loaded[s], 16)
            sp.dma_start(c1[:], const1).then_inc(c1_loaded, 16)
            sp.dma_start(ctx_nat, ctx_in.rearrange("(t p) d -> p t d", p=P)).then_inc(ctx_loaded, 16)
            with sp.Fori(1, N_UNITS // RING) as i:
                for s in range(RING):
                    sp.wait_ge(passed[s], i)
                    sp.dma_start(ring[s][:], weights[bass.ds(i * RING + s, 1)].rearrange("a p n -> (a p) n"))\
                      .then_inc(loaded[s], 16)
            for s in range(N_UNITS % RING):
                sp.wait_ge(passed[s], N_UNITS // RING)
                sp.dma_start(ring[s][:], weights[N_UNITS // RING * RING + s]).then_inc(loaded[s], 16)
            for t in range(TT):
                sp.wait_ge(res_ready, 2 * 5 + t + 1)
                sp.dma_start(out[t * P:t * P + P, :], res[:, t, :]).then_inc(stored, 16)
            sp.wait_ge(stored, 32)

        @block.gpsimd
        def _(pool):
            for turn in (*tokens_filled, *tokens_placed, *hid_ready, *hid_used):
                pool.sem_inc(turn, 1)
            nc.gpsimd.memset(eps[:, 0:1], EPS).then_inc(eps_ready, 1)
            nc.gpsimd.memset(ones, 1.0).then_inc(ones_ready, 1)
            pool.wait_ge(scale_ready, 1)
            pool.dma_start(poolw, pool_w).then_inc(poolw_loaded, 16)
            pool.dma_start(keys, keys_in).then_inc(keys_loaded, 16)
            for r in range(4):
                lo = (r % 2) * GRID
                pool.dma_start(bias[lo:lo + GRID, r // 2], rpb[:, :, 3 - r:7 - r, :]
                               .rearrange("w h i c -> w h (i c)")).then_inc(bias_loaded, 16)
            pool.wait_ge(bias_loaded, 64)
            pool.wait_ge(c1_loaded, 16)
            flat = bias.rearrange("p t h (i c) -> p (t h i) c", c=GRID)
            nc.gpsimd.tensor_tensor(flat, flat, win_mask.unsqueeze(1).broadcast_to([P, 64, GRID]), ALU.add)\
                .then_inc(bias_masked, 1)
            pool.wait_ge(res_ready, 4)
            pool.dma_start(row, rows_in[0:1, :].broadcast_to([P, D])).then_inc(row_loaded, 16)
            pool.dma_start(c2, const2).then_inc(const2_loaded, 16)
            pool.dma_start(gnorm, gnorm_in.broadcast_to([P, P])).then_inc(const2_loaded, 16)
            pool.dma_start(gw, gate_w).then_inc(const2_loaded, 16)
            pool.dma_start(pt, p_t).then_inc(const2_loaded, 16)
            for n in range(1, 4):
                pool.wait_ge(res_ready, 2 * (n + 2))
                pool.dma_start(row, rows_in[n:n + 1, :].broadcast_to([P, D])).then_inc(row_loaded, 16)
                if n == 1:
                    pool.wait_ge(ya_ready, 1)
                    pool.dma_start(pe_cols, pe_t).then_inc(nsa_small_loaded, 16)
                    pool.dma_start(w2.rearrange("p a b -> p (a b)"), w2_in).then_inc(nsa_small_loaded, 16)
                    nc.gpsimd.memset(vb, 0.0).then_inc(vb_zero, 1)
                    nc.gpsimd.memset(kcmp_t, 0.0).then_inc(vb_zero, 1)
                    nc.gpsimd.memset(cmp_p, 0.0).then_inc(vb_zero, 1)

        @block.tensor
        def _(pe):
            mm = nc.tensor.matmul

            def unit(u):
                pe.wait_ge(loaded[u % RING], 16 * (u // RING + 1))
                return ring[u % RING]

            def pass_previous(ins, u):
                if u:
                    ins.then_inc(passed[(u - 1) % RING], 1)

            def open_job(j):
                if j >= 4:
                    is_emptied(pe, j - 4)
                return bank(j)

            def open_sum(j):
                if j >= 4:
                    sum_is_emptied(pe, j - 4)
                return sum_bank(j)

            def adaln_unit(u, b, passes):
                w = unit(u).rearrange("p (c n) -> p c n", c=C)
                for m in range(2):
                    at = (2 * u + m) * 2
                    for c in range(C):
                        last = mm(b[:, at:at + 2], w[:, c, m * P:m * P + P], silu_c[:, c, :],
                                  start=(c == 0), stop=(c == C - 1))
                        if m == 0 and c == 0 and passes is not None:
                            last.then_inc(passed[passes % RING], 1)
                return last

            def sum_weighted(n, b, at, step, passes):
                pe.wait_ge(weighted_ready, n + 1)
                for m in range(2):
                    last = mm(b[:, at + m * step:at + m * step + 1], weighted[:, n % 4, m * P:m * P + P], ones,
                              start=True, stop=True)
                    if m == 0 and passes is not None:
                        last.then_inc(passed[passes % RING], 1)
                return last

            def transposed_job(u, j, src, first=True):
                w = unit(u).rearrange("p (c n) -> p c n", c=C)
                b = open_job(j)
                for m in range(2):
                    for c in range(C):
                        last = mm(b[:, m * T:m * T + T], w[:, c, m * P:m * P + P], src[:, c, :],
                                  start=(c == 0), stop=(c == C - 1))
                        if first and m == 0 and c == 0:
                            pass_previous(last, u)
                last.then_inc(filled[j % 4], 1)

            def natural_job(u, j, src, first=True):
                w = unit(u).rearrange("p (c n) -> p c n", c=C)
                b = open_job(j)
                for t in range(TT):
                    for c in range(C):
                        last = mm(b[:, t * 256:t * 256 + 256], src[:, c, t * P:t * P + P], w[:, c, :],
                                  start=(c == 0), stop=(c == C - 1))
                        if first and t == 0 and c == 0:
                            pass_previous(last, u)
                last.then_inc(filled[j % 4], 1)

            def row_units(name, units, n, src, final=True):
                for k in range(4):
                    open_sum(SUM[name] + k)
                for k in range(n):
                    w = unit(UNITS[units] + k)
                    for r in range(2):
                        for t in range(TT):
                            for half in range(2):
                                s = SUM[name] + 2 * t + half
                                last = mm(sum_bank(s)[:, :], src[:, 2 * k + r, t * P:t * P + P],
                                          w[:, r * D + half * 512:r * D + half * 512 + 512],
                                          start=(k == 0 and r == 0), stop=(final and k == n - 1 and r == 1))
                                if r == 0 and t == 0 and half == 0:
                                    pass_previous(last, UNITS[units] + k)
                                if final and k == n - 1 and r == 1:
                                    last.then_inc(sum_filled[s % 4], 1)

            def transposes(name, src):
                for k in range(4):
                    b = open_job(JOB[name] + k)
                    for m in range(2):
                        for t in range(TT):
                            at = m * T + t * P
                            last = nc.tensor.transpose(b[:, at:at + P], src[:, t, (2 * k + m) * P:(2 * k + m) * P + P],
                                                       ident)
                    last.then_inc(filled[(JOB[name] + k) % 4], 1)

            def gate_rows(name, v):
                for k in range(2):
                    b = open_job(JOB[name] + k)
                    for m in range(4):
                        last = mm(b[:, m * P:m * P + P], mod[:, v, 4 * k + m, 0:1].broadcast_to([P, P]), ident,
                                  start=True, stop=True)
                    last.then_inc(filled[(JOB[name] + k) % 4], 1)

            def mlp_like(first_unit, n, src, base, s0, begun=False, before_last=lambda: None):
                def up(k, u, done):
                    slot, rnd = u
                    pe.wait_ge(loaded[slot], 16 * (rnd + 1))
                    pe.wait_ge(hid_raw[k], done)
                    w = ring[slot].rearrange("p (c n) -> p c n", c=C)
                    for m in range(2):
                        for c in range(C):
                            last = mm(psum[k][:, m * T:m * T + T], w[:, c, m * P:m * P + P], src[:, c, :],
                                      start=(c == 0), stop=(c == C - 1))
                            if m == 0 and c == 0:
                                last.then_inc(passed[(slot - 1) % RING], 1)
                    last.then_inc(hid_filled[k], 1)

                def down(k, u, done, first, final):
                    slot, rnd = u
                    pe.wait_ge(loaded[slot], 16 * (rnd + 1))
                    pe.wait_ge(hid_ready[k], done + 2)
                    for r in range(2):
                        for t in range(TT):
                            for half in range(2):
                                s = s0 + 2 * t + half
                                last = mm(sum_bank(s)[:, :], hidden[:, 2 + k, r * T + t * P:r * T + t * P + P],
                                          ring[slot][:, r * D + half * 512:r * D + half * 512 + 512],
                                          start=(first and r == 0), stop=(final and r == 1))
                                if r == 0 and t == 0 and half == 0:
                                    last.then_inc(passed[(slot - 1) % RING], 1)
                                if final and r == 1:
                                    last.then_inc(sum_filled[s % 4], 1)
                    if not final:
                        last.then_inc(hid_used[k], 1)

                def at(k, i=0):
                    u = first_unit + k
                    return u % RING, u // RING + i

                if not begun:
                    for k in range(4):
                        open_sum(s0 + k)
                up(0, at(0), base)
                up(1, at(1), base)
                down(0, at(2), base, not begun, False)
                with pe.Fori(0, n // 2 - 1) as i:
                    up(0, at(3, i), i + (base + 1))
                    down(1, at(4, i), i + base, False, False)
                    up(1, at(5, i), i + (base + 1))
                    down(0, at(6, i), i + (base + 1), False, False)
                pe.wait_ge(hid_ready[1], base + n // 2 + 1)
                before_last()
                down(1, at(2 * n - 1), base + n // 2 - 1, False, True)

            def attention(name, n, scores, transpose, values, between=lambda k: None):
                for k in range(n + NA_LAG_V):
                    if k < n:
                        scores(k)
                    if 0 <= k - NA_LAG_T < n:
                        transpose(k - NA_LAG_T)
                    if 0 <= k - NA_LAG_V < n:
                        values(k - NA_LAG_V)
                    between(k)

            pe.wait_ge(silu_ready, 2)
            pe.wait_ge(ones_ready, 1)
            b = open_job(JOB["ada01"])
            before = None
            for u in ADA_ORDER:
                if u in WEIGHED:
                    for z in range(2):
                        sum_weighted(2 * WEIGHED.index(u) + z, b, 4 * u + z, 2, None if z else before)\
                            .then_inc(weighted_used, 1)
                else:
                    last = adaln_unit(u, b, before)
                before = u
            last.then_inc(filled[JOB["ada01"] % 4], 1)
            pe.wait_ge(c1_loaded, 16)
            pe.wait_ge(hat_ready, 1)
            transposes("x_t", hat)
            pe.wait_ge(hat_ready, 2)
            transposes("ctx_t", ctx_nat)
            for k in range(4):
                is_emptied(pe, JOB["x_t"] + k)
                is_emptied(pe, JOB["ctx_t"] + k)
            j0 = JOB["w_in"]
            for k in range(8):
                u = w_in_unit(k)
                if k < 2:
                    natural_job(u, j0 + k, act_t)
                elif k < 4:
                    transposed_job(u, j0 + k, act_t)
                elif k < 6:
                    transposed_job(u, j0 + 4 + 2 * (k - 4), act_t)
                    transposed_job(u, j0 + 5 + 2 * (k - 4), ctx_t, first=False)
                else:
                    natural_job(u, j0 + 8 + 2 * (k - 6), act_t)
                    natural_job(u, j0 + 9 + 2 * (k - 6), ctx_t, first=False)
                n = 2 + k // 2
                b = sum_bank(SUM[f"ada{n}"])
                for z in range(2):
                    part = 2 * (k % 2) + z
                    last = sum_weighted(FIRST_WEIGHED + 2 * k + z, b, 2 * part, 1, ada_unit(n, part) - 1)
                    if k % 2 and z:
                        last.then_inc(sum_filled[SUM[f"ada{n}"] % 4], 1)
                    else:
                        last.then_inc(weighted_used, 1)
            is_emptied(pe, j0), is_emptied(pe, j0 + 1)
            band = unit(UNITS["band"]).rearrange("p (s g t) -> p s g t", s=TT, g=4)
            for k in range(2):
                b = open_job(JOB["pool"] + k)
                for m in range(2):
                    g = 2 * k + m
                    for s in range(TT):
                        last = mm(b[:, m * T:m * T + T], px[:, k, s, m * P:m * P + P], band[:, s, g, :],
                                  start=(s == 0), stop=(s == TT - 1))
                        if k == 0 and m == 0 and s == 0:
                            pass_previous(last, UNITS["band"])
                last.then_inc(filled[(JOB["pool"] + k) % 4], 1)
            pe.wait_ge(poolw_loaded, 16)
            for k in range(2):
                is_emptied(pe, JOB["pool"] + k)
                b = open_job(JOB["pool_y"] + k)
                for m in range(2):
                    last = mm(b[:, m * T:m * T + T], poolw[:, 2 * k + m, :], pooled_t[:, 2 * k + m, :],
                              start=True, stop=True)
                last.then_inc(filled[(JOB["pool_y"] + k) % 4], 1)
            sum_is_emptied(pe, SUM["ada2"])
            gate_rows("gate1", 2)

            for k in range(12):
                is_emptied(pe, j0 + k)

            def na_scores(k):
                h, t = (k // 4) * 2 + k % 2, (k // 2) % 2
                lo, j = (h % 2) * DH, JOB["na", "s", k]
                b = open_job(j)
                q = qx_t[lo:lo + DH, h // 2, t * P:t * P + P]
                mm(b[:, 0:T], q, kx_t[lo:lo + DH, h // 2, :], start=True, stop=True)
                mm(b[:, T:2 * T], q, kc_t[lo:lo + DH, h // 2, :], start=True, stop=True).then_inc(filled[j % 4], 1)

            def na_transpose(k):
                j = JOB["na", "t", k]
                b = open_job(j)
                pe.wait_ge(na_norm, k + 1)
                for m in range(4):
                    last = nc.tensor.transpose(b[:, m * P:m * P + P], na_p[:, k % 3, m * P:m * P + P], ident)
                last.then_inc(filled[j % 4], 1)

            def na_values(k):
                h = (k // 4) * 2 + k % 2
                lo, s = (h % 2) * DH, SUM["na"] + k // 2
                if k % 2 == 0:
                    open_sum(s)
                is_emptied(pe, JOB["na", "t", k])
                cs = (h % 4) * DH
                for m in range(4):
                    v = vx if m < 2 else vc
                    last = mm(sum_bank(s)[lo:lo + DH, 0:P], v[:, h // 4, m % 2, cs:cs + DH],
                              na_pt[:, k % 4, m * P:m * P + P], start=(m == 0), stop=(m == 3))
                if k % 2:
                    last.then_inc(sum_filled[s % 4], 1)

            attention("na", N_NA, na_scores, na_transpose, na_values)
            for k in range(N_NA // 2):
                sum_is_emptied(pe, SUM["na"] + k)
            for k in range(2):
                is_emptied(pe, JOB["pool_y"] + k)
            row_units("w_out", "w_out", 4, mix_t)
            pe.wait_ge(hat_ready, 3)
            transposes("h2_t", hat)
            for k in range(4):
                is_emptied(pe, JOB["h2_t"] + k)
            pe.wait_ge(keys_loaded, 16)
            for step in WQ_KEY:
                j = JOB[step]
                if step[0] == "wq":
                    transposed_job(UNITS["wq"] + step[1], j, act_t)
                    continue
                _, part, t = step
                is_emptied(pe, JOB["wq", 2 * part])
                is_emptied(pe, JOB["wq", 2 * part + 1])
                b = open_job(j)
                for m in range(4):
                    hp = 4 * part + m
                    last = mm(b[:, m * P:m * P + P], pq_t[:, hp, t * P:t * P + P], keys[:, hp * P:hp * P + P],
                              start=True, stop=True)
                last.then_inc(filled[j % 4], 1)
            for t in range(TT):
                for k in range(EARLY // 2):
                    transposed_job(UNITS["u_first"] + EARLY // 2 * t + k, JOB["u_first", t] + k, act_t)
                b = open_job(JOB["hk", t])
                pe.wait_ge(chosen_ready, t + 1)
                for m in range(3):
                    last = nc.tensor.transpose(b[:, m * P:m * P + P], chosen[:, m, :], ident)
                last.then_inc(filled[JOB["hk", t] % 4], 1)
            for k in range(4):
                is_emptied(pe, JOB["hk", 1] - k)
            def place(pair, i):
                pe.wait_ge(onehot_ready[pair], i + 1)
                pe.wait_ge(tokens_placed[pair], i + 1)
                for n in (2 * pair, 2 * pair + 1):
                    last = mm(psum[pair][:, n % 2 * P:n % 2 * P + P], onehot[:, n * P:n * P + P],
                              onehot[:, D + n * P:D + n * P + P], start=True, stop=True)
                last.then_inc(tokens_filled[pair], 1)

            def early_down(k, t, r, half):
                u = UNITS[f"v_first{t}"] + k
                w = unit(u)
                last = mm(sum_bank(SUM["peer"] + 2 * t + half)[:, :], early[:, 2 * k + r, t * P:t * P + P],
                          w[:, r * D + half * 512:r * D + half * 512 + 512], start=(k == 0 and r == 0), stop=False)
                if r == 0 and half == 0:
                    pass_previous(last, u)

            TURNS = T // 8
            with pe.Fori(0, TURNS // 2) as i:
                for pair in range(4):
                    place(pair, i)
            for k in range(4):
                open_sum(SUM["peer"] + k)
            for i in range(TURNS // 2, TURNS):
                for pair in range(4):
                    place(pair, i)
                    k = i - TURNS // 2 - 1
                    if 0 <= k < EARLY:
                        early_down(k, 0, pair // 2, pair % 2)
            for pair in range(4):
                pe.wait_ge(early_ready[pair], 1)
            for k in range(EARLY):
                for r in range(2):
                    for half in range(2):
                        early_down(k, 1, r, half)
            mlp_like(UNITS["peer"], NKEYS // 2 - EARLY, act_t, 0, SUM["peer"], begun=True,
                     before_last=lambda: gate_rows("gate2", 5))

            pe.wait_ge(hat_ready, 4)
            transposes("u_t", hat3)
            for k in range(4):
                is_emptied(pe, JOB["u_t"] + k)
            for k in range(8):
                transposed_job(UNITS["hq_hf"] + k, JOB["hq_hf"] + k, act_t)
            for k in range(8):
                natural_job(UNITS["hi_hg"] + k, JOB["hi_hg"] + k, act_t)
            hq, hk = hqf[:, 0:8, :], hqf[:, 8:16, :]
            for level in range(9):
                if level < 8:
                    transposed_job(UNITS["nsa_t"] + level, JOB["nsa_t", level], act_t)
                if level != 7:
                    pe.wait_ge(level_ready, level + 1 if level < 7 else 8)
                xl = level_x[level % 2] if level < 7 else level_x[1]
                j = JOB["level", level]
                for t in range(TT if level < 8 else 1):
                    for g in range(2):
                        b = open_job(j)
                        for m in range(4):
                            h = 4 * g + m
                            if level == 7:
                                lhs, rhs = hk[:, h, t * P:t * P + P], hq[:, h, t * P:t * P + P]
                            elif level == 8:
                                lhs, rhs = xl[:, h, 0:P], xl[:, h, P:T]
                            else:
                                lhs = rhs = xl[:, h, t * P:t * P + P]
                            last = mm(b[:, m * P:m * P + P], lhs, rhs, start=True, stop=True)
                        last.then_inc(filled[j % 4], 1)
                        j += 1
            for k in range(2):
                natural_job(UNITS["vs_vw"] + k, JOB["vs_vw"] + k, act_t)
            pe.wait_ge(const2_loaded, 64)
            b = open_job(JOB["gates"])
            for t in range(TT):
                for c in range(C):
                    last = mm(b[:, t * 48:t * 48 + 48], act_t[:, c, t * P:t * P + P], gw[:, c, :],
                              start=(c == 0), stop=(c == C - 1))
            last.then_inc(filled[JOB["gates"] % 4], 1)
            for level in range(9):
                for k in range(4 if level < 8 else 2):
                    is_emptied(pe, JOB["level", level] + k)
            for k in range(8):
                is_emptied(pe, JOB["hi_hg"] + k)
            for k in range(4):
                t, g = k // 2, k % 2
                b = open_job(JOB["o"] + k)
                for m in range(4):
                    h = 4 * g + m
                    o = b[:, m * P:m * P + P]
                    v = [hig[:, h // 2, s * 256 + (h % 2) * P:s * 256 + (h % 2) * P + P] for s in range(TT)]
                    if t:
                        mm(o, ax_t[:, h, :], v[0], start=True, stop=False)
                    last = mm(o, ad_t[:, t, h, :], v[t], start=(t == 0), stop=True)
                last.then_inc(filled[(JOB["o"] + k) % 4], 1)
            for k in range(4):
                natural_job(UNITS["ga"] + k, JOB["ga"] + k, act_t)
            pe.wait_ge(ya_ready, 1)
            transposes("ya_t", o_nat)

            for k in range(8):
                is_emptied(pe, JOB["nsa_t", k])
            for k in range(6):
                b = open_job(JOB["rope"] + k)
                at = 2 * k if k < 4 else 12 + 2 * (k - 4)
                mm(b[:, :], const("rope_swap"), nsa_t[:, at:at + 2, :], start=True, stop=True)\
                    .then_inc(filled[(JOB["rope"] + k) % 4], 1)
            for k in range(4):
                is_emptied(pe, JOB["ya_t"] + k)
            row_units("branch_a", "branch_a", 4, ya_t)
            for kv in range(2):
                name = ("wk1", "wv1")[kv]
                j = JOB["cmp_hid"] + 2 * kv
                open_job(j), open_job(j + 1)
                pe.wait_ge(cmp_in_ready, kv + 1)
                for k in range(2):
                    w = unit(UNITS[name] + k).rearrange("p (l n) -> p l n", l=8)
                    for m in range(2):
                        for l in range(8):
                            last = mm(bank(j + m)[:, 0:60], w[:, l, m * P:m * P + P],
                                      cmp_in[:, kv, (8 * k + l) * 60:(8 * k + l) * 60 + 60],
                                      start=(k == 0 and l == 0), stop=(k == 1 and l == 7))
                            if m == 0 and l == 0:
                                pass_previous(last, UNITS[name] + k)
                        if k == 1:
                            last.then_inc(filled[(j + m) % 4], 1)
            pe.wait_ge(nsa_small_loaded, 32)
            for k in range(4):
                is_emptied(pe, JOB["cmp_hid"] + k)
            b = open_job(JOB["cmp_out"])
            for m in range(2):
                last = mm(b[:, 0:60], w2[:, 0, m * P:m * P + P], cmp_hid[:, m, :], start=(m == 0), stop=(m == 1))
            last.then_inc(filled[JOB["cmp_out"] % 4], 1)
            b = open_job(JOB["cmp_out"] + 1)
            for g in range(NSA_G):
                for m in range(2):
                    last = mm(b[0:CMP, g * DH:g * DH + DH], cmp_hid[:, 2 + m, g * CMP:g * CMP + CMP],
                              w2[:, 1, m * DH:m * DH + DH], start=(m == 0), stop=(m == 1))
            last.then_inc(filled[(JOB["cmp_out"] + 1) % 4], 1)
            is_emptied(pe, JOB["cmp_out"])
            for t in range(TT):
                b = open_job(JOB["cmp_s"] + t)
                for c in range(NSA_H // 2):
                    last = mm(b[:, 2 * c * CMP:(2 * c + 2) * CMP], nsa_t[:, c, t * P:t * P + P],
                              kcmp_t[:, c // 2, :, :], start=True, stop=True)
                last.then_inc(filled[(JOB["cmp_s"] + t) % 4], 1)
            for t in range(TT):
                b = open_job(JOB["cmp_t"] + t)
                pe.wait_ge(cmp_ready, t + 1)
                for g in range(NSA_G):
                    last = nc.tensor.transpose(b[:, g * P:g * P + P], cmp_p[:, t, g * P:g * P + P], ident)
                last.then_inc(filled[(JOB["cmp_t"] + t) % 4], 1)
            for t in range(TT):
                is_emptied(pe, JOB["cmp_t"] + t)
            is_emptied(pe, JOB["cmp_out"] + 1)
            pe.wait_ge(rot_ready, 1)
            for k in range(2):
                is_emptied(pe, JOB["vs_vw"] + k)
            vb4 = vb.rearrange("p (g i n) -> p g i n", g=NSA_G, i=2)

            def at_scores(k):
                c, t, h = AT_ITEMS[k]
                j = JOB["at", "s", k]
                b = open_job(j)
                width = P * (t + 1)
                lo, g = (h % 2) * DH, h // 4
                for branch in range(2):
                    last = mm(b[:, branch * width:(branch + 1) * width], q_rot[lo:lo + DH, c, t * P:t * P + P],
                              k_both[lo:lo + DH, branch * NSA_G + g, 0:width], start=True, stop=True)
                last.then_inc(filled[j % 4], 1)

            def at_transpose(k):
                j = JOB["at", "t", k]
                b = open_job(j)
                pe.wait_ge(at_norm, k + 1)
                for m in range(2 * (AT_ITEMS[k][1] + 1)):
                    last = nc.tensor.transpose(b[:, m * P:m * P + P], at_p[:, k % 3, m * P:m * P + P], ident)
                last.then_inc(filled[j % 4], 1)

            def at_values(k):
                c, t, h = AT_ITEMS[k]
                s = SUM["at"] + 2 * c + t
                if h % 2 == 0:
                    b = open_sum(s)
                    mm(b[:, 0:P], vb4[:, c // 2, c % 2, :], cmp_pt[:, t, (c // 2) * P:(c // 2) * P + P],
                       start=True, stop=False, skip_group_check=True)
                is_emptied(pe, JOB["at", "t", k])
                lo, g = (h % 2) * DH, h // 4
                for branch in range(2):
                    for tile in range(t + 1):
                        m = branch * (t + 1) + tile
                        v = vsw[:, branch, tile * 256 + g * DH:tile * 256 + g * DH + DH]
                        last = mm(sum_bank(s)[lo:lo + DH, 0:P], v, at_pt[:, k % 4, m * P:m * P + P],
                                  start=False, stop=(branch == 1 and tile == t), skip_group_check=True)
                if h % 2:
                    last.then_inc(sum_filled[s % 4], 1)

            def gb_unit(k):
                if k in GB_AT:
                    natural_job(UNITS["gb"] + GB_AT.index(k), JOB["at", "between", k], act_t)

            attention("at", N_AT, at_scores, at_transpose, at_values, gb_unit)
            for k in range(NSA_H // 2 * TT):
                sum_is_emptied(pe, SUM["at"] + k)
            row_units("branch_b", "branch_b", 4, yb_t)
            pe.wait_ge(merged_ready, 1)
            transposes("m_t", merged)
            for k in range(4):
                is_emptied(pe, JOB["m_t"] + k)
            row_units("w_out2", "w_out2", 4, act_t)
            row_units("ple", "ple", 1, pt)
            pe.wait_ge(hat_ready, 5)
            transposes("v_t", hat2)
            for k in range(4):
                is_emptied(pe, JOB["v_t"] + k)
            mlp_like(UNITS["mlp"], 16, act_t, (NKEYS // 2 - EARLY) // 2, SUM["mlp"])
            pe.wait_ge(res_ready, 2 * 5)
            transposes("h_t", res)
            for k in range(4):
                is_emptied(pe, JOB["h_t"] + k)
            row_units("ple_gate", "ple_gate", 4, act_t)

        @block.scalar
        def _(act):
            fn = nc.scalar.activation
            def sum_squares(n, src, ready=lambda t: None):
                act.wait_ge(root, 2 * n)
                for t in range(TT):
                    ready(t)
                    fn(junk[:, t, :], src[:, t, :], ACT.Square, accum_out=stat[:, n, 0, t:t + 1]).then_inc(squares, 1)
                    act.wait_ge(squares, 2 * n + t + 1)
                    fn(stat[:, n, 1, t:t + 1], stat[:, n, 0, t:t + 1], ACT.Sqrt, scale=1.0 / D, bias=eps[:, 0:1])\
                        .then_inc(root, 1)

            def load_root():
                fn(eps[:, 1:2], eps[:, 0:1], ACT.Sqrt)

            def residual(event):
                return lambda t: act.wait_ge(res_ready, 2 * event - 1 + t)

            def evacuate(j, dst, scale=1.0, func=ACT.Copy):
                is_filled(act, j)
                fn(dst, bank(j)[:, :], func, scale=scale).then_inc(emptied[j % 4], 1)

            def evacuate_scaled(name, dst, scale, shift):
                for k in (0, 2):
                    j = JOB[name] + k
                    is_filled(act, j)
                    for m in range(2):
                        c = 2 * k + m
                        kw = {"bias": shift(c)} if shift else {}
                        last = fn(dst[:, c, :], bank(j)[:, m * T:m * T + T], ACT.Identity, scale=scale(c), **kw)
                    last.then_inc(emptied[j % 4], 1)

            def tokens_and_hidden(func, n, base):
                def raw(k, done):
                    act.wait_ge(hid_filled[k], done + 1)
                    act.wait_ge(hid_ready[k], done + 1)
                    fn(hidden[:, k, :], psum[k][:, :], func).then_inc(hid_raw[k], 1)

                with act.Fori(0, n // 2) as i:
                    raw(0, i + base)
                    raw(1, i + base)

            act.wait_ge(cols_loaded, 16)
            fn(silu_c[:, :, 0], colset("c"), ACT.Silu).then_inc(silu_ready, 1)
            fn(silu_c[:, :, 1], colset("c_ctx"), ACT.Silu).then_inc(silu_ready, 1)
            act.wait_ge(eps_ready, 1)
            load_root()
            act.wait_ge(x_loaded, 16)
            sum_squares(0, res)
            act.wait_ge(ctx_loaded, 16)
            sum_squares(1, ctx_nat)
            act.wait_ge(scale_ready, 1)
            evacuate_scaled("x_t", act_t, lambda c: scale_t[:, 0, c:c + 1], lambda c: mod[:, 0, c, 0:1])
            evacuate_scaled("ctx_t", ctx_t, lambda c: scale_t[:, 1, c:c + 1], lambda c: mod[:, 0, c, 1:2])
            j0 = JOB["w_in"]
            flat2 = lambda ap: ap.rearrange("p a b -> p (a b)")
            evacuate(j0, flat2(px[:, 0]))
            evacuate(j0 + 1, flat2(px[:, 1]))
            evacuate(j0 + 2, flat2(qx_t[:, 0:2, :]), scale=DH ** -0.5)
            evacuate(j0 + 3, flat2(qx_t[:, 2:4, :]), scale=DH ** -0.5)
            for k in range(2):
                evacuate(j0 + 4 + 2 * k, flat2(kx_t[:, 2 * k:2 * k + 2, :]))
                evacuate(j0 + 5 + 2 * k, flat2(kc_t[:, 2 * k:2 * k + 2, :]))
            for k in range(2):
                evacuate(j0 + 8 + 2 * k, flat2(vx[:, k]))
                evacuate(j0 + 9 + 2 * k, flat2(vc[:, k]))
            for k in range(2):
                evacuate(JOB["pool"] + k, flat2(pooled_t[:, 2 * k:2 * k + 2, :]))
            for k in range(2):
                j = JOB["pool_y"] + k
                is_filled(act, j)
                for m in range(2):
                    last = fn(mix_t[:, 2 * k + m, :], bank(j)[:, m * T:m * T + T], ACT.Copy,
                              scale=col("pool_scale", 2 * k + m))
                last.then_inc(emptied[j % 4], 1)
            for k in range(2):
                evacuate(JOB["gate1"] + k, gate_row[:, k * 512:k * 512 + 512])

            def na_sum(k):
                s = SUM["na"] + k
                sum_is_filled(act, s)
                fn(mix_t[:, 4 + k // 2, (k % 2) * P:(k % 2) * P + P], sum_bank(s)[:, 0:P], ACT.Copy)\
                    .then_inc(sum_emptied[s % 4], 1)

            for k in range(N_NA + NA_LAG_V + 1):
                if k < N_NA:
                    j = JOB["na", "s", k]
                    act.wait_ge(na_neg_ready, k + 1)
                    if k >= 3:
                        is_filled(act, JOB["na", "t", k - 3])
                    fn(na_p[:, k % 3, :], bank(j)[:, :], ACT.Exp, bias=na_stat[:, k % 3, 0:1],
                       accum_out=na_stat[:, k % 3, 1:2]).then_inc(emptied[j % 4], 1)
                if 0 <= k - NA_LAG_T < N_NA:
                    n = k - NA_LAG_T
                    j = JOB["na", "t", n]
                    is_filled(act, j)
                    if n >= 4:
                        sum_is_filled(act, SUM["na"] + (n - 4) // 2)
                    fn(na_pt[:, n % 4, :], bank(j)[:, :], ACT.Copy).then_inc(emptied[j % 4], 1)
                if 0 <= k - NA_LAG_V - 1 < N_NA and (k - NA_LAG_V - 1) % 2:
                    na_sum((k - NA_LAG_V - 1) // 2)

            load_root()
            sum_squares(2, res, residual(1))
            act.wait_ge(scale_ready, 2)
            evacuate_scaled("h2_t", act_t, lambda c: scale_t[:, 2, c:c + 1], lambda c: mod[:, 3, c, 0:1])
            for step in WQ_KEY:
                if step[0] == "wq":
                    evacuate(JOB[step], flat2(pq_t[:, 2 * step[1]:2 * step[1] + 2, :]))
                else:
                    _, part, t = step
                    evacuate(JOB[step], score[:, t, part * 512:part * 512 + 512])
            for t in range(TT):
                for k in range(EARLY // 2):
                    n = EARLY // 2 * t + k
                    evacuate(JOB["u_first", t] + k, flat2(early[:, 2 * n:2 * n + 2, :]), func=ACT.Gelu)
                act.wait_ge(soft_ready, t + 1)
                fn(chosen[:, 2, :], chosen[:, 2, :], ACT.Exp).then_inc(soft_exp, 1)
                j = JOB["hk", t]
                is_filled(act, j)
                fn(hk_t[:, :, t * P:t * P + P], bank(j)[:, 0:3 * P].rearrange("p (a b) -> p a b", a=3), ACT.Copy)\
                    .then_inc(emptied[j % 4], 1)
            with act.Fori(0, T // 8) as i:
                for pair in range(4):
                    act.wait_ge(tokens_filled[pair], i + 2)
                    g = psum[pair][:, 0:2 * P].rearrange("p (t j) -> p t j", t=2)
                    fn(early_gates[:, pair], g[:, :, LATE:], ACT.Copy)
                    fn(dense[:, 0:LATE, bass.ds(i * 8 + 2 * pair, 2)].rearrange("p j t -> p t j"),
                       g[:, :, 0:LATE], ACT.Copy).then_inc(tokens_placed[pair], 1)
            tokens_and_hidden(ACT.Gelu, NKEYS // 2 - EARLY, 0)
            for k in range(2):
                evacuate(JOB["gate2"] + k, gate_row2[:, k * 512:k * 512 + 512])

            load_root()
            sum_squares(3, res, residual(2))
            sum_squares(4, res, residual(3))
            evacuate_scaled("u_t", act_t, lambda c: col("pre_mix", c), None)
            act.wait_ge(lb_ready, 1)
            fn(lbt[:, 1:3, :], lbt[:, 1:3, :], ACT.Exp).then_inc(lb_ready, 1)
            for k in range(8):
                evacuate(JOB["hq_hf"] + k, flat2(hqf[:, 2 * k:2 * k + 2, :]), func=ACT.Silu if k < 4 else ACT.Sigmoid)
            def level_exponential(n):
                act.wait_ge(level_arg, n + 1)
                fn(flat2(level_x[n % 2]), flat2(level_x[n % 2]), ACT.Exp).then_inc(level_exp, 1)

            for k in range(8):
                evacuate(JOB["hi_hg"] + k, hig[:, k, :], func=ACT.Copy if k < 4 else ACT.Silu)
                if k == 1:
                    act.wait_ge(hg_pre, 1)
                    fn(flat2(logf), flat2(hqf[:, 8:16, :]), ACT.Ln).then_inc(hg_log, 1)
                if k == 3:
                    level_exponential(0)
            for n in range(8):
                if n:
                    level_exponential(n)
                evacuate(JOB["nsa_t", n], flat2(nsa_t[:, 2 * n:2 * n + 2, :]), scale=DH ** -0.5 if n < 4 else 1.0)
            for k in range(2):
                evacuate(JOB["vs_vw"] + k, vsw[:, k, :])
            j = JOB["gates"]
            is_filled(act, j)
            fn(flat2(gates), bank(j)[:, 0:TT * 48], ACT.Sigmoid).then_inc(emptied[j % 4], 1)
            for k in range(4):
                evacuate(JOB["o"] + k, o_nat[:, k // 2, (k % 2) * 512:(k % 2) * 512 + 512])
            act.wait_ge(ovar, 1)
            fn(ostat[:, 2, :], ostat[:, 1, :], ACT.Sqrt).then_inc(oroot, 1)
            for k in range(4):
                evacuate(JOB["ga"] + k, gab[:, k, :], func=ACT.Sigmoid)
            for k in (0, 2):
                evacuate(JOB["ya_t"] + k, flat2(ya_t[:, 2 * k:2 * k + 2, :]))
            for kv in range(2):
                is_emptied(act, JOB["nsa_t", 4 + kv])
                for a in range(2):
                    for b in range(2):
                        src = nsa_t[a * DH:a * DH + DH, 8 + 2 * kv:10 + 2 * kv, 16 * b:16 * b + 16 * CMP]
                        dst = cmp_in[b * DH:b * DH + DH, kv].rearrange("p (l c a n) -> p a l c n", l=16, c=2, a=2)
                        last = fn(dst[:, a], src.rearrange("p c (n l) -> p l c n", l=16), ACT.Copy)
                last.then_inc(cmp_copied, 1)
            for k in range(4):
                j = JOB["cmp_hid"] + k
                is_filled(act, j)
                fn(cmp_hid[:, k, :], bank(j)[:, 0:60], ACT.Gelu_apprx_tanh).then_inc(emptied[j % 4], 1)
            j = JOB["cmp_out"]
            is_filled(act, j)
            act.wait_ge(vb_zero, 2)
            for z in range(2):
                half = slice(z * DH, z * DH + DH)
                last = fn(kcmp_t[half, :, z, :], bank(j)[half, 0:60].rearrange("p (g n) -> p g n", g=NSA_G), ACT.Copy)
            last.then_inc(emptied[j % 4], 1)
            is_filled(act, j + 1)
            vb5 = vb.rearrange("p (g i n) -> p g i n", g=NSA_G, i=2)
            for r in range(4):
                last = fn(vb5[32 * r:32 * r + CMP, :, r // 2, (r % 2) * DH:(r % 2) * DH + DH],
                          bank(j + 1)[0:CMP, 0:NSA_G * DH].rearrange("p (g d) -> p g d", g=NSA_G), ACT.Copy)
            last.then_inc(emptied[(j + 1) % 4], 1)
            for t in range(TT):
                act.wait_ge(cmp_arg, t + 1)
                fn(cmp_s[:, t, :], cmp_s[:, t, :], ACT.Exp).then_inc(cmp_exp, 1)
            for t in range(TT):
                evacuate(JOB["cmp_t"] + t, cmp_pt[:, t, :])

            def at_sum(s):
                sum_is_filled(act, SUM["at"] + s)
                fn(yb_t[:, s // 2, (s % 2) * P:(s % 2) * P + P], sum_bank(SUM["at"] + s)[:, 0:P], ACT.Copy)\
                    .then_inc(sum_emptied[(SUM["at"] + s) % 4], 1)

            for k in range(N_AT + NA_LAG_V + 1):
                if k < N_AT:
                    width = P * (AT_ITEMS[k][1] + 1)
                    j = JOB["at", "s", k]
                    act.wait_ge(at_neg, k + 1)
                    if k >= 3:
                        is_filled(act, JOB["at", "t", k - 3])
                    for m in range(2):
                        last = fn(at_p[:, k % 3, m * width:m * width + width], bank(j)[:, m * width:m * width + width],
                                  ACT.Exp, bias=at_stat[:, k % 3, m:m + 1], accum_out=at_stat[:, k % 3, 2 + m:3 + m])
                    last.then_inc(emptied[j % 4], 1)
                if 0 <= k - NA_LAG_T < N_AT:
                    n = k - NA_LAG_T
                    j = JOB["at", "t", n]
                    used = 2 * P * (AT_ITEMS[n][1] + 1)
                    is_filled(act, j)
                    if n >= 4:
                        sum_is_filled(act, SUM["at"] + (n - 4) // 2)
                    fn(at_pt[:, n % 4, 0:used], bank(j)[:, 0:used], ACT.Copy).then_inc(emptied[j % 4], 1)
                n = k - NA_LAG_V - 1
                if 0 <= n < N_AT and n % 2:
                    at_sum(n // 2)
                if k in GB_AT:
                    evacuate(JOB["at", "between", k], gab[:, 4 + GB_AT.index(k), :], func=ACT.Sigmoid)
            for k in (0, 2):
                evacuate(JOB["m_t"] + k, flat2(act_t[:, 2 * k:2 * k + 2, :]))

            def take_sums(name, dst, func=ACT.Copy):
                for k in range(4):
                    s = SUM[name] + k
                    sum_is_filled(act, s)
                    fn(dst[:, k // 2, (k % 2) * 512:(k % 2) * 512 + 512], sum_bank(s)[:, :], func)\
                        .then_inc(sum_emptied[s % 4], 1)

            def taken(name):
                return lambda t: [sum_is_emptied(act, SUM[name] + 2 * t + half) for half in range(2)]

            load_root()
            take_sums("w_out2", side)
            sum_squares(5, side, taken("w_out2"))
            sum_squares(6, res, residual(4))
            evacuate_scaled("v_t", act_t, lambda c: col("pre_mlp", c), None)
            take_sums("ple", merged)
            tokens_and_hidden(ACT.Relu, 16, (NKEYS // 2 - EARLY) // 2)
            load_root()
            take_sums("mlp", side)
            sum_squares(7, side, taken("mlp"))
            for k in (0, 2):
                evacuate(JOB["h_t"] + k, flat2(act_t[:, 2 * k:2 * k + 2, :]))
            take_sums("ple_gate", side, ACT.Sigmoid)
            load_root()
            sum_squares(8, merged, lambda t: act.wait_ge(merged_ready, 2 + t))

        @block.vector
        def _(dve):
            v = nc.vector
            chain = [0]

            def link(ins):
                chain[0] += 1
                ins.then_inc(dve_chain, 1)
                dve.wait_ge(dve_chain, chain[0])

            def flat(ap):
                return ap.rearrange("p a b -> p (a b)")

            def add_bias(n):
                j = JOB["ada01"]
                return v.tensor_tensor(mod[:, n], bank(j)[:, 16 * n:16 * n + 16].rearrange("p (c z) -> p c z", z=2),
                                       cols[:, COLS["ada_b"][0] + 8 * n:COLS["ada_b"][0] + 8 * n + 8]
                                       .unsqueeze(2).broadcast_to([P, C, 2]), ALU.add)

            def weigh(n, u, z):
                dve.wait_ge(loaded[u % RING], 16 * (u // RING + 1))
                w = ring[u % RING].rearrange("p (c n) -> p c n", c=C)
                dst = weighted[:, n % 4, :]
                link(v.tensor_scalar(dst, w[:, 0, :], silu_c[:, 0, z:z + 1], None, ALU.mult))
                for c in range(1, C):
                    last = v.scalar_tensor_tensor(dst, w[:, c, :], silu_c[:, c, z:z + 1], dst, ALU.mult, ALU.add)
                    if c < C - 1:
                        link(last)
                last.then_inc(weighted_ready, 1)

            def weighted_free(m):
                if m >= 0 and m % 4 == 3:
                    sum_is_filled(dve, SUM[f"ada{2 + m // 4}"])
                else:
                    dve.wait_ge(weighted_used, FIRST_WEIGHED + (m + 1 if m < 0 else 3 * (m // 4) + m % 4 + 1))

            def adaln_sum(n):
                s = SUM[f"ada{n}"]
                sum_is_filled(dve, s)
                v.tensor_tensor(mod[:, n, :, 0], sum_bank(s)[:, 0:8],
                                cols[:, COLS["ada_b"][0] + 8 * n:COLS["ada_b"][0] + 8 * n + 8], ALU.add)\
                    .then_inc(sum_emptied[s % 4], 1)
                sum_is_emptied(dve, s)

            def inverse_root(n, t):
                dve.wait_ge(root, 2 * n + t + 1)
                link(v.reciprocal(stat[:, n, 2, t:t + 1], stat[:, n, 1, t:t + 1]))
                return stat[:, n, 2, t:t + 1]

            def norm(n, src, dst):
                for t in range(TT):
                    last = v.tensor_scalar(dst[:, t, :], src[:, t, :], inverse_root(n, t), None, ALU.mult)
                last.then_inc(hat_ready, 1)

            def norm_gained(n, r, t, dst, src):
                inverse = inverse_root(n, t)
                dve.wait_ge(row_loaded, 16 * (r + 1))
                return v.scalar_tensor_tensor(dst[:, t, :], src[:, t, :], inverse, row, ALU.mult, ALU.mult)

            def evacuate_scaled(name, dst, scale, shift):
                for k in (1, 3):
                    j = JOB[name] + k
                    is_filled(dve, j)
                    for m in range(2):
                        c = 2 * k + m
                        b = bank(j)[:, m * T:m * T + T]
                        if shift:
                            last = v.tensor_scalar(dst[:, c, :], b, scale(c), shift(c), ALU.mult, ALU.add)
                        else:
                            last = v.tensor_scalar(dst[:, c, :], b, scale(c), None, ALU.mult)
                    last.then_inc(emptied[j % 4], 1)

            def evacuate(j, dst):
                is_filled(dve, j)
                v.tensor_copy(dst, bank(j)[:, :]).then_inc(emptied[j % 4], 1)

            def add_gated(name, rows, scratch):
                for t in range(TT):
                    for half in range(2):
                        s = SUM[name] + 2 * t + half
                        sum_is_filled(dve, s)
                        at = half * 512
                        v.tensor_tensor(scratch[:, t, at:at + 512], sum_bank(s)[:, :], rows[:, at:at + 512],
                                        ALU.mult).then_inc(sum_emptied[s % 4], 1)
                    for half in range(2):
                        sum_is_emptied(dve, SUM[name] + 2 * t + half)
                    v.tensor_tensor(res[:, t, :], res[:, t, :], scratch[:, t, :], ALU.add).then_inc(res_ready, 1)

            def products(n, base, used, factor):
                def one(k, pair, done):
                    dve.wait_ge(hid_raw[k], done + base + 1)
                    dve.wait_ge(hid_used[k], done + (used[k] + 1))
                    v.tensor_tensor(hidden[:, 2 + k, :], hidden[:, k, :], factor(k, pair), ALU.mult)\
                        .then_inc(hid_ready[k], 1)

                with dve.Fori(0, n // 2) as i:
                    one(0, 2 * i, i)
                    one(1, 2 * i + 1, i)

            dve.wait_ge(cols_loaded, 16)
            dve.wait_ge(silu_ready, 2)
            for k, u in enumerate(WEIGHED):
                for z in range(2):
                    if k == 2:
                        dve.wait_ge(weighted_used, z + 1)
                    weigh(2 * k + z, u, z)
                if k == 1:
                    dve.wait_ge(x_loaded, 16)
                    norm(0, res, hat)
            dve.wait_ge(ctx_loaded, 16)
            norm(1, ctx_nat, ctx_nat)
            j = JOB["ada01"]
            is_filled(dve, j)
            add_bias(0)
            add_bias(1).then_inc(emptied[j % 4], 1)
            is_emptied(dve, j)
            for z in range(2):
                last = v.scalar_tensor_tensor(scale_t[:, z, :], mod[:, 1, :, z], 1.0, colset("norm1_g"), ALU.add, ALU.mult)
            last.then_inc(scale_ready, 1)
            dve.wait_ge(scale_ready, 1)
            evacuate_scaled("x_t", act_t, lambda c: scale_t[:, 0, c:c + 1], lambda c: mod[:, 0, c, 0:1])
            evacuate_scaled("ctx_t", ctx_t, lambda c: scale_t[:, 1, c:c + 1], lambda c: mod[:, 0, c, 1:2])
            for n in range(16):
                weighted_free(n - 4)
                weigh(FIRST_WEIGHED + n, ada_unit(2 + n // 4, n % 4), 0)
                if n >= 5 and n % 4 == 1:
                    adaln_sum(2 + n // 4 - 1)
            adaln_sum(5)
            v.scalar_tensor_tensor(scale_t[:, 2, :], mod[:, 4, :, 0], 1.0, colset("norm2_g"), ALU.add, ALU.mult)\
                .then_inc(scale_ready, 1)

            dve.wait_ge(bias_masked, 1)

            def na_max(k):
                h, t = (k // 4) * 2 + k % 2, (k // 2) % 2
                j = JOB["na", "s", k]
                is_filled(dve, j)
                link(v.tensor_tensor(bank(j)[:, 0:T], bank(j)[:, 0:T], bias[:, t, h, :], ALU.add))
                if k >= 3:
                    dve.wait_ge(na_norm, k - 2)
                v.tensor_reduce(na_stat[:, k % 3, 0:1], bank(j)[:, :], AX.X, ALU.max, negate=True)\
                    .then_inc(na_neg_ready, 1)

            def na_normalise(k):
                is_emptied(dve, JOB["na", "s", k])
                link(v.reciprocal(na_stat[:, k % 3, 2:3], na_stat[:, k % 3, 1:2]))
                v.tensor_scalar(na_p[:, k % 3, :], na_p[:, k % 3, :], na_stat[:, k % 3, 2:3], None, ALU.mult)\
                    .then_inc(na_norm, 1)

            for k in range(N_NA + 1):
                if k < N_NA:
                    na_max(k)
                if k:
                    na_normalise(k - 1)
            for k in range(2):
                is_emptied(dve, JOB["gate1"] + k)
            add_gated("w_out", gate_row, hat)
            dve.wait_ge(scale_ready, 2)
            norm(2, res, hat)
            evacuate_scaled("h2_t", act_t, lambda c: scale_t[:, 2, c:c + 1], lambda c: mod[:, 3, c, 0:1])

            u32 = lambda ap: ap.bitcast(U32)

            def top16(values, left, n, width, best_of, index_of):
                one = lambda ap, k, w: ap[:, k * w:k * w + w]
                half = lambda ap, k, z: ap[:, k * TOPK + 8 * z:k * TOPK + 8 * z + 8]
                for k in range(n):
                    last = v.max(half(best_of, k, 0), one(values, k, width))
                link(last)
                for k in range(n):
                    v.max_index(u32(half(index_of, k, 0)), half(best_of, k, 0), one(values, k, width))
                    last = v.match_replace(one(left, k, width), half(best_of, k, 0), one(values, k, width), -3.0e38)
                link(last)
                for k in range(n):
                    last = v.max(half(best_of, k, 1), one(left, k, width))
                link(last)
                for k in range(n):
                    last = v.max_index(u32(half(index_of, k, 1)), half(best_of, k, 1), one(left, k, width))
                link(last)

            for _, part, t in (step for step in WQ_KEY if step[0] == "key"):
                is_emptied(dve, JOB["key", part, t])
                at = slice(4 * part * TOPK, 4 * part * TOPK + 4 * TOPK)
                top16(score[:, t, part * 512:part * 512 + 512], rest[:, part * 512:part * 512 + 512], 4, NKEYS,
                      top[:, t, at], top_i[:, t, at])
            link(v.tensor_copy(flat(top_if), u32(flat(top_i))))
            for t in range(TT):
                tv = top[:, t, :].rearrange("p (h z k) -> p h z k", z=2, k=TOPK)
                wide = [P, PEER_H, TOPK, TOPK]
                link(v.tensor_tensor(cand.rearrange("p (h a b) -> p h a b", h=PEER_H, a=TOPK),
                                     tv[:, :, 0, :].unsqueeze(3).broadcast_to(wide),
                                     tv[:, :, 1, :].unsqueeze(2).broadcast_to(wide), ALU.add))
                top16(cand, cand_rest, PEER_H, TOPK * TOPK, best[:, t, :], best_i)
                if t:
                    is_filled(dve, JOB["hk", 0])
                for z in range(2):
                    op, by = (ALU.logical_shift_right, 4) if z == 0 else (ALU.bitwise_and, 15)
                    link(v.tensor_scalar(u32(part_a), u32(best_i), by, None, op))
                    link(v.tensor_copy(part_af, u32(part_a)))
                    pick3 = pick.rearrange("p (q a) -> p q a", a=TOPK)
                    link(v.tensor_tensor(pick3, part_af.unsqueeze(2).broadcast_to([P, P, TOPK]),
                                         iota[:, 0:TOPK].unsqueeze(1).broadcast_to([P, P, TOPK]), ALU.is_equal))
                    ti = top_if[:, t, :].rearrange("p (h z k) -> p h z k", z=2, k=TOPK)
                    pick4 = pick.rearrange("p (h k a) -> p h k a", h=PEER_H, k=TOPK)
                    link(v.tensor_tensor(pick4, pick4, ti[:, :, z, :].unsqueeze(2).broadcast_to(wide), ALU.mult))
                    link(v.tensor_reduce(chosen[:, z, :], pick3, AX.X, ALU.add))
                bt = best[:, t, :].rearrange("p (h k) -> p h k", h=PEER_H)
                ct = chosen[:, 2, :].rearrange("p (h k) -> p h k", h=PEER_H)
                rows8 = [P, PEER_H, TOPK]
                v.tensor_tensor(ct, bt, bt[:, :, 0:1].broadcast_to(rows8), ALU.subtract).then_inc(soft_ready, 1)
                dve.wait_ge(soft_exp, t + 1)
                link(v.tensor_reduce(soft[:, 0, :], ct, AX.X, ALU.add))
                link(v.reciprocal(soft[:, 1, :], soft[:, 0, :]))
                v.tensor_tensor(ct, ct, soft[:, 1, :].unsqueeze(2).broadcast_to(rows8), ALU.mult)\
                    .then_inc(chosen_ready, 1)
            for t in range(TT):
                is_emptied(dve, JOB["hk", t])

            def onehots(token, pair):
                at = 2 * pair * P
                v.tensor_tensor(onehot[:, at:at + 2 * P].rearrange("p (t n) -> p t n", t=2),
                                iota.unsqueeze(1).broadcast_to([P, 2, P]),
                                hk_t[:, 0, bass.ds(token + 2 * pair, 2)].unsqueeze(2).broadcast_to([P, 2, P]),
                                ALU.is_equal)
                for n in (2 * pair, 2 * pair + 1):
                    one = bass.ds(token + n, 1)
                    last = v.tensor_scalar(onehot[:, D + n * P:D + n * P + P], iota, hk_t[:, 1, one],
                                           hk_t[:, 2, one], ALU.is_equal, ALU.mult)
                last.then_inc(onehot_ready[pair], 1)

            def times_early(token, pair):
                at = early[:, :, bass.ds(token + 2 * pair, 2)].rearrange("p j t -> p t j")
                return v.tensor_tensor(at, early_gates[:, pair], at, ALU.mult)

            for pair in range(4):
                onehots(0, pair)
            with dve.Fori(1, T // 8) as i:
                for pair in range(4):
                    dve.wait_ge(tokens_filled[pair], i + 1)
                    dve.wait_ge(tokens_placed[pair], i + 1)
                    times_early(i * 8 - 8, pair)
                    onehots(i * 8, pair)
            for pair in range(4):
                dve.wait_ge(tokens_placed[pair], T // 8 + 1)
                times_early(T - 8, pair).then_inc(early_ready[pair], 1)
            products(NKEYS // 2 - EARLY, 0, (0, 0), lambda k, pair: dense[:, bass.ds(pair * 2, 2), :])
            for k in range(2):
                is_emptied(dve, JOB["gate2"] + k)
            add_gated("peer", gate_row2, hat3)
            for t in range(TT):
                norm_gained(3, 0, t, res, res).then_inc(res_ready, 1)

            norm(4, res, hat3)
            evacuate_scaled("u_t", act_t, lambda c: col("pre_mix", c), None)
            lg = colset("lb_logits")
            link(v.tensor_tensor(lbt[:, 0, :], lg[:, 0:8], lg[:, 8:16], ALU.max))
            v.tensor_tensor(lbt[:, 1, :], lg[:, 0:8], lbt[:, 0, :], ALU.subtract)
            v.tensor_tensor(lbt[:, 2, :], lg[:, 8:16], lbt[:, 0, :], ALU.subtract).then_inc(lb_ready, 1)
            dve.wait_ge(lb_ready, 2)
            link(v.tensor_tensor(lbt[:, 3, :], lbt[:, 1, :], lbt[:, 2, :], ALU.add))
            link(v.reciprocal(lbt[:, 0, :], lbt[:, 3, :]))
            link(v.tensor_tensor(lbt[:, 4, :], lbt[:, 1, :], lbt[:, 0, :], ALU.mult))
            link(v.tensor_scalar(lbt[:, 5, :], lbt[:, 4, :], -1.0, 1.0, ALU.mult, ALU.add))
            hq, hk = hqf[:, 0:8, :], hqf[:, 8:16, :]
            for k in range(8):
                is_emptied(dve, JOB["hq_hf"] + k)
            link(v.tensor_scalar(flat(hq), flat(hq), P ** -0.5, None, ALU.mult))
            for h in range(HG_H):
                last = v.tensor_scalar(hk[:, h, :], hk[:, h, :], lbt[:, 5, h:h + 1], lbt[:, 4, h:h + 1],
                                       ALU.mult, ALU.add)
            last.then_inc(hg_pre, 1)
            dve.wait_ge(hg_pre, 1)
            dve.wait_ge(hg_log, 1)
            link(v.tensor_scalar(flat(hk), flat(hk), -1.0, 1.0, ALU.mult, ALU.add))
            dve.wait_ge(const2_loaded, 64)
            for h in range(HG_H):
                last = v.tensor_tensor_scan(cum[:, h, :], const("scan_keep"), logf[:, h, :], 0.0, ALU.mult, ALU.add)
            link(last)
            link(v.memset(ad_t, 0.0))
            masks = const("level_mask").rearrange("p (l t) -> p l t", l=LEVELS).bitcast(I32)
            cum_flat = flat(cum)

            def level_exponent(n):
                x = flat(level_x[n % 2])
                if n >= 2:
                    is_filled(dve, JOB["level", n - 2] + 3)
                if n < 7:
                    half = 1 << n
                    cv = cum_flat.rearrange("p (b z w) -> p b z w", z=2, w=half)
                    xv = x.rearrange("p (b z w) -> p b z w", z=2, w=half)
                    shape = [P, T * HG_H // (2 * half), half]
                    edge = cv[:, :, 0, half - 1:half].broadcast_to(shape)
                    v.tensor_tensor(xv[:, :, 0, :], edge, cv[:, :, 0, :], ALU.subtract)
                    if n < 6:
                        v.tensor_tensor(xv[:, :, 1, :], cv[:, :, 1, :], edge, ALU.subtract).then_inc(level_arg, 1)
                    else:
                        v.tensor_copy(xv[:, :, 1, :], cv[:, :, 1, :]).then_inc(level_arg, 1)
                    return
                cv = cum_flat.rearrange("p (h q w) -> p h q w", h=HG_H, q=4)
                xv = x.rearrange("p (h q w) -> p h q w", h=HG_H, q=4)
                shape = [P, HG_H, 64]
                total = [cv[:, :, q, 63:64].broadcast_to(shape) for q in range(4)]
                link(v.tensor_tensor(xv[:, :, 0, :], total[0], cv[:, :, 0, :], ALU.subtract))
                v.tensor_tensor(xv[:, :, 0, :], xv[:, :, 0, :], total[1], ALU.add)
                v.tensor_tensor(xv[:, :, 1, :], total[1], cv[:, :, 1, :], ALU.subtract)
                v.tensor_copy(xv[:, :, 2, :], cv[:, :, 2, :])
                v.tensor_tensor(xv[:, :, 3, :], cv[:, :, 3, :], total[2], ALU.add).then_inc(level_arg, 1)

            def level_scale(n):
                half = 1 << n
                dve.wait_ge(level_exp, n + 1)
                if n == 7:
                    xv = level_x[1].rearrange("p h (z w) -> p h z w", z=2)
                    kv_, qv = (a.rearrange("p h (z w) -> p h z w", z=2) for a in (hk, hq))
                else:
                    xv = flat(level_x[n % 2]).rearrange("p (b z w) -> p b z w", z=2, w=half)
                    kv_, qv = (flat(a).rearrange("p (b z w) -> p b z w", z=2, w=half) for a in (hk, hq))
                v.tensor_tensor(xv[:, :, 0, :], xv[:, :, 0, :], kv_[:, :, 0, :], ALU.mult)
                v.tensor_tensor(xv[:, :, 1, :], xv[:, :, 1, :], qv[:, :, 1, :], ALU.mult).then_inc(level_ready, 1)

            def level_take(n):
                for k in range(4):
                    j = JOB["level", n] + k
                    t, g = k // 2, k % 2
                    mask = masks[:, n, :] if n < 7 else ident.bitcast(I32)
                    is_filled(dve, j)
                    v.copy_predicated(ad_t[:, t, 4 * g:4 * g + 4, :], mask.unsqueeze(1).broadcast_to([P, 4, P]),
                                      bank(j)[:, :].rearrange("p (h t) -> p h t", h=4)).then_inc(emptied[j % 4], 1)

            for n in range(8):
                level_exponent(n)
                if n:
                    level_take(n - 1)
                level_scale(n)
            level_take(7)
            for g in range(2):
                j = JOB["level", 8] + g
                evacuate(j, flat(ax_t[:, 4 * g:4 * g + 4, :]))
            for k in range(4):
                is_emptied(dve, JOB["o"] + k)
            o3 = lambda ap: flat(ap).rearrange("p (a b) -> p a b", b=P)
            link(v.tensor_tensor(flat(o_sq), flat(o_nat), flat(o_nat), ALU.mult))
            link(v.tensor_reduce(ostat[:, 0, :], o3(o_sq), AX.X, ALU.add))
            v.tensor_scalar(ostat[:, 1, :], ostat[:, 0, :], 1.0 / P, EPS, ALU.mult, ALU.add).then_inc(ovar, 1)
            dve.wait_ge(oroot, 1)
            link(v.reciprocal(ostat[:, 3, :], ostat[:, 2, :]))
            link(v.tensor_tensor(o3(o_nat), o3(o_nat), ostat[:, 3, :].unsqueeze(2).broadcast_to([P, 16, P]), ALU.mult))
            link(v.tensor_tensor(o3(o_nat), o3(o_nat), gnorm.unsqueeze(1).broadcast_to([P, 16, P]), ALU.mult))
            for t in range(TT):
                ov = o_nat[:, t, :].rearrange("p (u n) -> p u n", n=256)
                last = v.tensor_tensor(ov, ov, hig[:, 4:8, t * 256:t * 256 + 256], ALU.mult)
            last.then_inc(ya_ready, 1)
            for k in (1, 3):
                evacuate(JOB["ya_t"] + k, flat(ya_t[:, 2 * k:2 * k + 2, :]))

            two = [P, 2, T]
            cos, sin = (const(n).unsqueeze(1).broadcast_to(two) for n in ("rope_cos", "rope_sin"))
            for k in range(6):
                j = JOB["rope"] + k
                at = 2 * k if k < 4 else 12 + 2 * (k - 4)
                dst = q_rot[:, at:at + 2, :] if k < 4 else k_rot[:, at - 12:at - 10, :]
                tmp = rope_tmp.rearrange("p (a b) -> p a b", a=2)
                is_filled(dve, j)
                v.tensor_tensor(tmp, bank(j)[:, :].rearrange("p (a b) -> p a b", a=2), sin, ALU.mult)\
                    .then_inc(emptied[j % 4], 1)
                link(v.tensor_tensor(dst, nsa_t[:, at:at + 2, :], cos, ALU.mult))
                link(v.tensor_tensor(dst, dst, tmp, ALU.add))
            kb = k_both.rearrange("p (q a) t -> p q a t", a=2)
            for half in range(2):
                for a in range(2):
                    last = v.tensor_copy(kb[half * DH:half * DH + DH, :, a, :], k_rot[a * DH:a * DH + DH, :, :])
            last.then_inc(rot_ready, 1)
            dve.wait_ge(nsa_small_loaded, 32)
            for kv in range(2):
                dve.wait_ge(cmp_copied, kv + 1)
                ci = cmp_in[:, kv, :].rearrange("p (l n) -> p l n", l=16)
                v.tensor_tensor(ci, ci, pe_cols[:, kv, :].unsqueeze(2).broadcast_to([P, 16, 60]), ALU.add)\
                    .then_inc(cmp_in_ready, 1)
            def times_branch(name, n):
                for k in range(4):
                    s = SUM[name] + k
                    t, half = k // 2, k % 2
                    sum_is_filled(dve, s)
                    gate = gab[:, 4 * n + 2 * half:4 * n + 2 * half + 2, t * 256:t * 256 + 256]
                    v.tensor_tensor(gate, sum_bank(s)[:, :].rearrange("p (u n) -> p u n", u=2), gate, ALU.mult)\
                        .then_inc(sum_emptied[s % 4], 1)

            for k in range(4):
                is_emptied(dve, JOB["ga"] + k)
            times_branch("branch_a", 0)
            dve.wait_ge(vb_zero, 3)
            is_emptied(dve, JOB["gates"])
            for t in range(TT):
                j = JOB["cmp_s"] + t
                wide = [P, NSA_H, CMP]
                s = cmp_s[:, t, :].rearrange("p (h n) -> p h n", h=NSA_H)
                add = const("cmp_add")[:, t * CMP:t * CMP + CMP].unsqueeze(1).broadcast_to(wide)
                keep = const("cmp_keep")[:, t * CMP:t * CMP + CMP].unsqueeze(1).broadcast_to(wide)
                st = [cmp_stat[:, t, k * NSA_H:k * NSA_H + NSA_H] for k in range(4)]
                is_filled(dve, j)
                v.tensor_tensor(s, bank(j)[:, 0:NSA_H * CMP].rearrange("p (h n) -> p h n", h=NSA_H), add, ALU.add)\
                    .then_inc(emptied[j % 4], 1)
                is_emptied(dve, j)
                link(v.tensor_reduce(st[0], s, AX.X, ALU.max, negate=True))
                v.tensor_tensor(s, s, st[0].unsqueeze(2).broadcast_to(wide), ALU.add).then_inc(cmp_arg, 1)
                dve.wait_ge(cmp_exp, t + 1)
                link(v.tensor_reduce(st[1], s, AX.X, ALU.add))
                link(v.reciprocal(st[2], st[1]))
                link(v.tensor_tensor(st[3], st[2], gates[:, t, 0:NSA_H], ALU.mult))
                link(v.tensor_tensor(s, s, keep, ALU.mult))
                v.tensor_tensor(cmp_p[:, t, :].rearrange("p (h n) -> p h n", h=NSA_H)[:, :, 0:CMP], s,
                                st[3].unsqueeze(2).broadcast_to(wide), ALU.mult).then_inc(cmp_ready, 1)

            def at_max(k):
                c, t, h = AT_ITEMS[k]
                width = P * (t + 1)
                j = JOB["at", "s", k]
                is_filled(dve, j)
                b = bank(j)[:, 0:2 * width].rearrange("p (s w) -> p s w", s=2)
                diag = b[:, :, width - P:width]
                link(v.tensor_tensor(diag, diag, const("causal").unsqueeze(1).broadcast_to([P, 2, P]), ALU.add))
                v.tensor_reduce(at_stat[:, k % 3, 0:2], b, AX.X, ALU.max, negate=True).then_inc(at_neg, 1)

            def at_normalise(k):
                c, t, h = AT_ITEMS[k]
                width = P * (t + 1)
                is_emptied(dve, JOB["at", "s", k])
                st = at_stat[:, k % 3, :]
                link(v.reciprocal(st[:, 4:6], st[:, 2:4]))
                link(v.tensor_tensor(st[:, 6:8], st[:, 4:6], gates[:, t, NSA_H + h::NSA_H], ALU.mult))
                for m in range(2):
                    pv = at_p[:, k % 3, m * width:m * width + width]
                    last = v.tensor_scalar(pv, pv, st[:, 6 + m:7 + m], None, ALU.mult)
                last.then_inc(at_norm, 1)

            for k in range(N_AT + 1):
                if k < N_AT:
                    at_max(k)
                if k:
                    at_normalise(k - 1)
            for k in GB_AT:
                is_emptied(dve, JOB["at", "between", k])
            times_branch("branch_b", 1)
            for k in range(4):
                sum_is_emptied(dve, SUM["branch_b"] + k)
            for t in range(TT):
                last = v.tensor_tensor(merged[:, t, :].rearrange("p (u n) -> p u n", u=4),
                                       gab[:, 0:4, t * 256:t * 256 + 256], gab[:, 4:8, t * 256:t * 256 + 256], ALU.add)
            last.then_inc(merged_ready, 1)
            for k in (1, 3):
                evacuate(JOB["m_t"] + k, flat(act_t[:, 2 * k:2 * k + 2, :]))

            def add_normed(n, src, r):
                for t in range(TT):
                    link(norm_gained(n, r, t, hat2, src))
                    add = v.tensor_tensor(res[:, t, :], res[:, t, :], hat2[:, t, :], ALU.add)
                    add.then_inc(res_ready, 1)

            add_normed(5, side, 1)
            norm(6, res, hat2)
            evacuate_scaled("v_t", act_t, lambda c: col("pre_mlp", c), None)
            products(16, (NKEYS // 2 - EARLY) // 2, ((NKEYS // 2 - EARLY) // 2, (NKEYS // 2 - EARLY) // 2 - 1), lambda k, pair: hidden[:, k, :])
            add_normed(7, side, 2)
            for k in (1, 3):
                evacuate(JOB["h_t"] + k, flat(act_t[:, 2 * k:2 * k + 2, :]))
            for k in range(4):
                sum_is_emptied(dve, SUM["ple"] + k)
                sum_is_emptied(dve, SUM["ple_gate"] + k)
            for t in range(TT):
                v.tensor_tensor(merged[:, t, :], merged[:, t, :], side[:, t, :], ALU.mult).then_inc(merged_ready, 1)
            add_normed(8, merged, 3)


def column_units(w):
    return [w[:, n:n + 256].reshape(C, P, 256).transpose(1, 0, 2).reshape(P, UNIT) for n in range(0, w.shape[1], 256)]


def row_units_of(w):
    return [w[n:n + 256].reshape(2, P, D).transpose(1, 0, 2).reshape(P, UNIT) for n in range(0, w.shape[0], 256)]


def staggered(ups, downs):
    order = [ups[0], ups[1], downs[0]]
    for k in range(2, len(ups)):
        order += [ups[k], downs[k - 1]]
    return order + [downs[-1]]


def as_column(v):
    return v.reshape(-1, P).T


def kernel(**inputs):
    import numpy as _np
    import concourse.bacc as _bacc
    from concourse import mybir as _mybir
    from concourse.bass_utils import run_bass_kernel_spmd as _run

    a = {k: _np.asarray(v) for k, v in inputs.items()}
    first, second, band = constants()
    ada, w2 = a["ada_w"][0], a["w_in_2"][0]
    at = {"hq": 0, "hf": 1024, "hi": 2048, "hg": 3072, "nq": 4096, "kc": 5120, "vc": 5376, "ks": 5632,
          "vs": 5888, "kw": 6144, "vw": 6400, "gate": 6656, "ga": 6704, "gb": 7728}
    part = lambda name, n: w2[:, at[name]:at[name] + n]
    experts_u = a["peer_u"][0].reshape(P, NKEYS // 2, 2, D).transpose(1, 3, 2, 0)
    experts_v = a["peer_v"][0].reshape(P, NKEYS // 2, 2 * D).transpose(1, 0, 2)

    us = [column_units(u.reshape(D, 256))[0] for u in experts_u]
    late = NKEYS // 2 - EARLY

    def compress_units(w):
        w = w.reshape(2, 16, DH, 256).transpose(0, 2, 1, 3).reshape(P, 16 * 256)
        return [w[:, :UNIT], w[:, UNIT:]]

    ada_units = column_units(ada)
    stages = {
        "ada0": ada_units[0:4], "ada1": ada_units[4:8],
        "w_in": [u for k, w in enumerate(column_units(a["w_in"][0])) for u in (w, *ada_units[8 + 2 * k:10 + 2 * k])],
        "band": [band], "w_out": row_units_of(a["w_out"][0]),
        "wq": column_units(a["peer_wq"][0]),
        "u_first": us[late:], "v_first0": list(experts_v[late:]), "v_first1": list(experts_v[late:]), "peer": staggered(us[:late], list(experts_v[:late])),
        "hq_hf": column_units(part("hq", 2048)), "hi_hg": column_units(part("hi", 2048)),
        "nsa_t": column_units(part("nq", 1024)) + [column_units(part(n, 256))[0] for n in ("kc", "vc", "ks", "kw")],
        "vs_vw": [column_units(part(n, 256))[0] for n in ("vs", "vw")],
        "ga": column_units(part("ga", 1024)), "gb": column_units(part("gb", 1024)),
        "wk1": compress_units(a["cmp_wk1_2"][0]), "wv1": compress_units(a["cmp_wv1_2"][0]),
        "branch_a": row_units_of(a["w_branch_a_2"][0]), "branch_b": row_units_of(a["w_branch_b_2"][0]),
        "w_out2": row_units_of(a["w_out_2"][0]),
        "mlp": staggered(column_units(a["w_up_2"][0]), row_units_of(a["w_down_2"][0])),
        "ple": row_units_of(a["w_ple_2"][0]), "ple_gate": row_units_of(a["w_ple_gate_2"][0]),
    }
    weights = _np.empty((N_UNITS, P, UNIT), _np.float32)
    for name, first_unit in UNITS.items():
        for k, u in enumerate(stages[name]):
            weights[first_unit + k] = u
    small = {"ada_b": a["ada_b"], "norm1_g": a["norm1_g"], "norm2_g": a["norm2_g"], "c": a["c"], "c_ctx": a["c_ctx"],
             "pool_scale": a["pool_scale"], "pre_mix": a["norm_pre_mix_2"], "pre_mlp": a["norm_pre_mlp_2"],
             "lb_logits": a["hg_lb_logits_2"]}
    pe = _np.stack([a[n][0].reshape(2, 16, DH).transpose(0, 2, 1).reshape(P, 16) for n in ("cmp_pe_k_2", "cmp_pe_v_2")], 1)
    w2_in = _np.zeros((P, 2, 2, P), _np.float32)
    wk2 = a["cmp_wk2_2"][0].reshape(2, P, DH).transpose(1, 0, 2)
    w2_in[:, 0, :, :DH] = w2_in[:, 0, :, DH:] = wk2
    w2_in[:, 1].reshape(P, 2 * P)[:, :P] = a["cmp_wv2_2"][0].reshape(2, P, DH).transpose(1, 0, 2).reshape(P, P)
    padded = _np.zeros((NA_H, 7, 2 * GRID - 1), _np.float32)
    padded[:, :, GRID - KW:GRID + KW - 1] = a["na_rpb"][0][:, 4:11]
    shifted = _np.stack([padded[:, :, GRID - 1 - w:2 * GRID - 1 - w] for w in range(GRID)])
    data = {
        "weights": weights, "x": a["x"][0], "ctx_in": a["ctx"][0],
        "cols_in": _np.concatenate([as_column(small[n]) for n in COLS], 1),
        "rows_in": _np.stack([a["final_g"], a["norm_post_mix_2"][0], a["norm_post_mlp_2"][0], a["norm_ple_2"].reshape(-1)]),
        "gnorm_in": a["hg_gnorm_2"], "const1": first, "const2": second, "rpb": shifted,
        "pool_w": a["pool_w"][0].transpose(1, 0, 2), "keys_in": a["peer_keys"][0].reshape(HP, NKEYS, P).transpose(2, 0, 1).reshape(P, HP * NKEYS),
        "gate_w": part("gate", 48).reshape(C, P, 48).transpose(1, 0, 2),
        "pe_t": pe, "w2_in": w2_in.reshape(P, 4 * P),
        "p_t": a["p_2"][0, 0].T.reshape(2, P, T).transpose(1, 0, 2),
    }
    nc = _bacc.Bacc("TRN2", target_bir_lowering=False, num_devices=1)
    arrays, args = {}, {}
    for name, v in data.items():
        v = _np.ascontiguousarray(v)
        arrays[f"in_{name}"] = v
        args[name] = nc.dram_tensor(f"in_{name}", v.shape, _mybir.dt.from_np(v.dtype), kind="ExternalInput").ap()
    args["out"] = nc.dram_tensor("out_0", (T, D), F32, kind="ExternalOutput").ap()
    build(nc, **args)
    r = _run(nc, [arrays], core_ids=[0])
    return r.results[0]["out_0"].reshape(1, T, D)
```
